# Optimizing a Trainium2 kernel written in Bass

```python
import math
import jax, jax.numpy as jnp
from jax import lax
import numpy as np

D_MODEL = 1024
BATCH = 1
SEQ = 128
DEPTH = 2
DEC_BATCH = 1
DEC_SEQ = 512
PAST_LEN = 128

GRID_W = 64
D_MIX = D_MODEL
SSD_WIDTH = D_MIX // 2
SSD_HEAD_DIM = 64
SSD_HEADS = SSD_WIDTH // SSD_HEAD_DIM
SSD_GROUPS = 2
SSD_STATE = 64
SSD_CONV = 5
SSD_CHUNK = 128
SSD_XBC = SSD_WIDTH + 2 * SSD_GROUPS * SSD_STATE
MLA_WIDTH = D_MIX - SSD_WIDTH
MLA_V_DIM = 64
MLA_HEADS = MLA_WIDTH // MLA_V_DIM
MLA_NOPE_DIM = 64
MLA_ROPE_DIM = 32
MLA_Q_RANK = 384
MLA_KV_RANK = 256
ROPE_THETA = 10000.0
Q_BLOCK = 128
D_FF = 2816
N_EXPERTS = 8
TOP_K = 2
D_FF_EXPERT = 1408
N_DENSE_LAYERS = (DEPTH + 1) // 2
N_MOE_LAYERS = DEPTH // 2
N_MOD = 6
EPS = 1e-6
IN_COLS = SSD_WIDTH + SSD_XBC + 2 * SSD_HEADS + MLA_Q_RANK + MLA_KV_RANK + MLA_ROPE_DIM

kernel_name = "hybrid_ssd_mla_prefix_diffusion_step"

def rms_norm(x, g):
    xf = x.astype(jnp.float32)
    y = xf * lax.rsqrt(jnp.mean(xf * xf, axis=-1, keepdims=True) + EPS)
    return (y * g.astype(jnp.float32)).astype(x.dtype)

def centred_depthwise_conv(u, w, b):
    pad = SSD_CONV // 2
    length = u.shape[1]
    up = jnp.pad(u, ((0, 0), (pad, pad), (0, 0)))
    out = b
    for k in range(SSD_CONV):
        out = out + up[:, k:k + length] * w[k]
    return out

def ssd_chunked(x, dt, a, bm, cm, h0):
    b, length, nh, p = x.shape
    n = bm.shape[-1]
    q = SSD_CHUNK
    nc = length // q
    xc = x.reshape(b, nc, q, nh, p)
    bc = bm.reshape(b, nc, q, nh, n)
    cc = cm.reshape(b, nc, q, nh, n)
    dtc = dt.reshape(b, nc, q, nh)
    la = jnp.cumsum((dtc * a).astype(jnp.float32), axis=2)
    lower = jnp.tril(jnp.ones((q, q), dtype=bool))[:, :, None]
    seg = la[:, :, :, None, :] - la[:, :, None, :, :]
    decay = jnp.exp(jnp.where(lower, seg, -jnp.inf)).astype(x.dtype)
    scores = jnp.einsum('bcthn,bcshn->bctsh', cc, bc) * decay * dtc[:, :, None, :, :]
    y_intra = jnp.einsum('bctsh,bcshp->bcthp', scores, xc)
    to_end = jnp.exp(la[:, :, -1:, :] - la).astype(x.dtype)
    chunk_states = jnp.einsum('bcshn,bcsh,bcshp->bchpn', bc, to_end * dtc, xc)
    chunk_decay = jnp.exp(la[:, :, -1, :]).astype(x.dtype)

    def step(h, inp):
        st, dec = inp
        return h * dec[:, :, None, None] + st, h

    h_final, h_start = lax.scan(step, h0, (jnp.moveaxis(chunk_states, 1, 0), jnp.moveaxis(chunk_decay, 1, 0)))
    h_start = jnp.moveaxis(h_start, 0, 1)
    y_inter = jnp.einsum('bcthn,bchpn->bcthp', cc, h_start) * jnp.exp(la).astype(x.dtype)[..., None]
    return (y_intra + y_inter).reshape(b, length, nh, p), h_final

def axial_rope_tables(n_tokens, dtype):
    rows = n_tokens // GRID_W
    row = jnp.repeat(jnp.arange(rows, dtype=jnp.float32), GRID_W)
    col = jnp.tile(jnp.arange(GRID_W, dtype=jnp.float32), rows)
    half = MLA_ROPE_DIM // 2
    inv = ROPE_THETA ** (-jnp.arange(0, half, 2, dtype=jnp.float32) / half)
    ar = row[:, None] * inv[None, :]
    ac = col[:, None] * inv[None, :]
    ang = jnp.concatenate([ar, ar, ac, ac], axis=-1)
    return jnp.cos(ang).astype(dtype), jnp.sin(ang).astype(dtype)

def apply_axial_rope(u, cos, sin):
    r1, r2, c1, c2 = jnp.split(u, 4, axis=-1)
    rot = jnp.concatenate([-r2, r1, -c2, c1], axis=-1)
    return u * cos + rot * sin

def blocked_attention(q, k, v):
    b, lq, nh, dqk = q.shape
    scale = dqk ** -0.5
    qb = jnp.moveaxis(q.reshape(b, lq // Q_BLOCK, Q_BLOCK, nh, dqk), 1, 0)

    def one_block(qblk):
        s = jnp.einsum('bqhd,bkhd->bhqk', qblk, k).astype(jnp.float32) * scale
        pr = jax.nn.softmax(s, axis=-1).astype(v.dtype)
        return jnp.einsum('bhqk,bkhd->bqhd', pr, v)

    out = lax.map(one_block, qb)
    return jnp.moveaxis(out, 0, 1).reshape(b, lq, nh, v.shape[-1])

def token_mixers(h, w_in, conv_w, conv_b, dt_bias, a_log, d_skip, ssd_norm, q_norm, w_uq, kv_norm, w_ukv,
                 mla_norm, w_out, ctx):
    b, length, _ = h.shape
    proj = h @ w_in
    s1 = SSD_WIDTH
    s2 = s1 + SSD_XBC
    s3 = s2 + 2 * SSD_HEADS
    s4 = s3 + MLA_Q_RANK
    s5 = s4 + MLA_KV_RANK
    z, xbc, dt_raw, cq, ckv, k_rope = jnp.split(proj, [s1, s2, s3, s4, s5], axis=-1)

    xbc = jax.nn.silu(centred_depthwise_conv(xbc, conv_w, conv_b))
    xs, bm, cm = jnp.split(xbc, [SSD_WIDTH, SSD_WIDTH + SSD_GROUPS * SSD_STATE], axis=-1)
    xs = xs.reshape(b, length, SSD_HEADS, SSD_HEAD_DIM)
    rep = SSD_HEADS // SSD_GROUPS
    bm = jnp.repeat(bm.reshape(b, length, SSD_GROUPS, SSD_STATE), rep, axis=2)
    cm = jnp.repeat(cm.reshape(b, length, SSD_GROUPS, SSD_STATE), rep, axis=2)
    dt = jax.nn.softplus(dt_raw.reshape(b, length, 2, SSD_HEADS) + dt_bias)
    a = -jnp.exp(a_log.astype(jnp.float32))
    if ctx is None:
        h0 = jnp.zeros((b, 2, SSD_HEADS, SSD_HEAD_DIM, SSD_STATE), h.dtype)
    else:
        h0 = ctx[2]
    y_f, h_f = ssd_chunked(xs, dt[:, :, 0], a[0], bm, cm, h0[:, 0])
    flip = lambda u: jnp.flip(u, axis=1)
    y_b, h_b = ssd_chunked(flip(xs), flip(dt[:, :, 1]), a[1], flip(bm), flip(cm), h0[:, 1])
    y_ssd = y_f + flip(y_b) + d_skip[:, None] * xs
    y_ssd = y_ssd * jax.nn.silu(z.reshape(b, length, SSD_HEADS, SSD_HEAD_DIM))
    y_ssd = rms_norm(y_ssd.reshape(b, length, SSD_WIDTH), ssd_norm)

    q = (rms_norm(cq, q_norm) @ w_uq).reshape(b, length, MLA_HEADS, MLA_NOPE_DIM + MLA_ROPE_DIM)
    q_nope, q_rope = jnp.split(q, [MLA_NOPE_DIM], axis=-1)
    ckv_n = rms_norm(ckv, kv_norm)
    if ctx is None:
        ckv_all, kr_all = ckv_n, k_rope
    else:
        cos, sin = axial_rope_tables(length, h.dtype)
        q_rope = apply_axial_rope(q_rope, cos[:, None, :], sin[:, None, :])
        kr_lat = apply_axial_rope(k_rope, cos, sin)
        ckv_all = jnp.concatenate([ctx[0], ckv_n], axis=1)
        kr_all = jnp.concatenate([ctx[1], kr_lat], axis=1)
    n_keys = ckv_all.shape[1]
    kv = (ckv_all @ w_ukv).reshape(b, n_keys, MLA_HEADS, MLA_NOPE_DIM + MLA_V_DIM)
    k_nope, v = jnp.split(kv, [MLA_NOPE_DIM], axis=-1)
    k_full = jnp.concatenate(
        [k_nope, jnp.broadcast_to(kr_all[:, :, None, :], (b, n_keys, MLA_HEADS, MLA_ROPE_DIM))], axis=-1)
    q_full = jnp.concatenate([q_nope, q_rope], axis=-1)
    o = blocked_attention(q_full, k_full, v).reshape(b, length, MLA_WIDTH)
    o = rms_norm(o, mla_norm)

    y = jnp.concatenate([y_ssd, o], axis=-1) @ w_out
    if ctx is None:
        return y, (ckv_n, k_rope, jnp.stack([h_f, h_b], axis=1))
    return y, None

def swiglu(u, w_gate, w_up, w_down):
    return (jax.nn.silu(u @ w_gate) * (u @ w_up)) @ w_down

def moe_swiglu(u, router, w_gate, w_up, w_down):
    logits = (u @ router).astype(jnp.float32)
    top_v, top_i = lax.top_k(logits, TOP_K)
    top_w = jax.nn.softmax(top_v, axis=-1)
    combine = jnp.sum(jax.nn.one_hot(top_i, N_EXPERTS, dtype=jnp.float32) * top_w[..., None], axis=-2)
    hidden = jax.nn.silu(jnp.einsum('bld,edf->blef', u, w_gate)) * jnp.einsum('bld,edf->blef', u, w_up)
    hidden = hidden * combine.astype(u.dtype)[..., None]
    return jnp.einsum('blef,efd->bld', hidden, w_down)

def trunk_layer(x, mod, norms, mix_params, ffn, ctx):
    shift1, scale1, gate1, shift2, scale2, gate2 = jnp.split(mod, N_MOD, axis=-1)
    g_pre1, g_post1, g_pre2, g_post2 = norms
    h = rms_norm(x, g_pre1) * (1 + scale1) + shift1
    y, ctx_out = token_mixers(h, *mix_params, ctx=ctx)
    x = x + gate1 * rms_norm(y, g_post1)
    h = rms_norm(x, g_pre2) * (1 + scale2) + shift2
    x = x + gate2 * rms_norm(ffn(h), g_post2)
    return x, ctx_out

def setup_inputs(seed: int = 0) -> dict:
    key = jax.random.key(seed)
    ks = jax.random.split(key, 48)
    cnt = [0]

    def nk():
        cnt[0] += 1
        return ks[cnt[0]]

    def nrm(shape, scale=1.0):
        return jax.random.normal(nk(), shape, jnp.float32) * scale

    def gain(shape):
        return 1.0 + nrm(shape, 0.05)

    dt0 = jnp.exp(jax.random.uniform(nk(), (DEPTH, 2, SSD_HEADS), jnp.float32,
                                     minval=math.log(1e-3), maxval=math.log(1e-1)))
    dt_bias = dt0 + jnp.log(-jnp.expm1(-dt0))
    a_log = jnp.log(jax.random.uniform(nk(), (DEPTH, 2, SSD_HEADS), jnp.float32, minval=1.0, maxval=16.0))
    return {
        "x_prompt": nrm((BATCH, SEQ, D_MODEL)),
        "x_sample": nrm((DEC_BATCH, DEC_SEQ, D_MODEL)),
        "cache_ckv": nrm((DEC_BATCH, DEPTH, PAST_LEN, MLA_KV_RANK)),
        "cache_krope": nrm((DEC_BATCH, DEPTH, PAST_LEN, MLA_ROPE_DIM)),
        "state_ssm": nrm((DEC_BATCH, DEPTH, 2, SSD_HEADS, SSD_HEAD_DIM, SSD_STATE), 0.5),
        "c": nrm((DEC_BATCH, D_MODEL)),
        "c_ctx": nrm((D_MODEL,)),
        "w_mod": nrm((DEPTH, D_MODEL, N_MOD * D_MODEL), 0.5 * D_MODEL ** -0.5),
        "b_mod": nrm((DEPTH, N_MOD * D_MODEL), 0.02),
        "norm_pre_mix": gain((DEPTH, D_MODEL)),
        "norm_post_mix": gain((DEPTH, D_MODEL)),
        "norm_pre_ffn": gain((DEPTH, D_MODEL)),
        "norm_post_ffn": gain((DEPTH, D_MODEL)),
        "w_in": nrm((DEPTH, D_MODEL, IN_COLS), D_MODEL ** -0.5),
        "conv_w": nrm((DEPTH, SSD_CONV, SSD_XBC), SSD_CONV ** -0.5),
        "conv_b": nrm((DEPTH, SSD_XBC), 0.02),
        "dt_bias": dt_bias,
        "a_log": a_log,
        "d_skip": gain((DEPTH, SSD_HEADS)),
        "ssd_norm": gain((DEPTH, SSD_WIDTH)),
        "q_norm": gain((DEPTH, MLA_Q_RANK)),
        "w_uq": nrm((DEPTH, MLA_Q_RANK, MLA_HEADS * (MLA_NOPE_DIM + MLA_ROPE_DIM)), MLA_Q_RANK ** -0.5),
        "kv_norm": gain((DEPTH, MLA_KV_RANK)),
        "w_ukv": nrm((DEPTH, MLA_KV_RANK, MLA_HEADS * (MLA_NOPE_DIM + MLA_V_DIM)), MLA_KV_RANK ** -0.5),
        "mla_norm": gain((DEPTH, MLA_WIDTH)),
        "w_out": nrm((DEPTH, D_MIX, D_MODEL), D_MIX ** -0.5),
        "ffn_w_gate": nrm((N_DENSE_LAYERS, D_MODEL, D_FF), D_MODEL ** -0.5),
        "ffn_w_up": nrm((N_DENSE_LAYERS, D_MODEL, D_FF), D_MODEL ** -0.5),
        "ffn_w_down": nrm((N_DENSE_LAYERS, D_FF, D_MODEL), D_FF ** -0.5),
        "moe_router": nrm((N_MOE_LAYERS, D_MODEL, N_EXPERTS), D_MODEL ** -0.5),
        "moe_w_gate": nrm((N_MOE_LAYERS, N_EXPERTS, D_MODEL, D_FF_EXPERT), D_MODEL ** -0.5),
        "moe_w_up": nrm((N_MOE_LAYERS, N_EXPERTS, D_MODEL, D_FF_EXPERT), D_MODEL ** -0.5),
        "moe_w_down": nrm((N_MOE_LAYERS, N_EXPERTS, D_FF_EXPERT, D_MODEL), D_FF_EXPERT ** -0.5),
    }

def reference(x_prompt, x_sample, cache_ckv, cache_krope, state_ssm, c, c_ctx, w_mod, b_mod,
              norm_pre_mix, norm_post_mix, norm_pre_ffn, norm_post_ffn, w_in, conv_w, conv_b, dt_bias, a_log,
              d_skip, ssd_norm, q_norm, w_uq, kv_norm, w_ukv, mla_norm, w_out, ffn_w_gate, ffn_w_up, ffn_w_down,
              moe_router, moe_w_gate, moe_w_up, moe_w_down):
    xp = x_prompt
    xs = x_sample
    silu_c = jax.nn.silu(c)
    silu_ctx = jax.nn.silu(c_ctx)
    new_ckv, new_kr, new_ssm = [], [], []
    for i in range(DEPTH):
        norms = (norm_pre_mix[i], norm_post_mix[i], norm_pre_ffn[i], norm_post_ffn[i])
        mix_params = (w_in[i], conv_w[i], conv_b[i], dt_bias[i], a_log[i], d_skip[i], ssd_norm[i], q_norm[i],
                      w_uq[i], kv_norm[i], w_ukv[i], mla_norm[i], w_out[i])
        j = i // 2
        if i % 2 == 0:
            ffn = lambda u, j=j: swiglu(u, ffn_w_gate[j], ffn_w_up[j], ffn_w_down[j])
        else:
            ffn = lambda u, j=j: moe_swiglu(u, moe_router[j], moe_w_gate[j], moe_w_up[j], moe_w_down[j])
        mod_ctx = (silu_ctx @ w_mod[i] + b_mod[i])[None, None, :]
        xp, (ckv_i, kr_i, ssm_i) = trunk_layer(xp, mod_ctx, norms, mix_params, ffn, None)
        new_ckv.append(ckv_i)
        new_kr.append(kr_i)
        new_ssm.append(ssm_i)
        mod_lat = (silu_c @ w_mod[i] + b_mod[i])[:, None, :]
        xs, _ = trunk_layer(xs, mod_lat, norms, mix_params, ffn,
                            (cache_ckv[:, i], cache_krope[:, i], state_ssm[:, i]))
    return (xp, xs, jnp.stack(new_ckv, axis=1), jnp.stack(new_kr, axis=1), jnp.stack(new_ssm, axis=1))


_drawn_inputs = setup_inputs


def setup_inputs(seed=0):
    import zlib

    import numpy as np

    out = dict(_drawn_inputs(seed))
    spreads = {}
    factors = {'d_skip': 2.792, 'q_norm': 3.516}
    for name, (base, spread) in spreads.items():
        noise = np.random.default_rng([zlib.crc32(name.encode()), seed]).standard_normal(out[name].shape)
        drawn = base * np.exp(spread * noise) if base else spread * noise
        out[name] = __import__('jax').numpy.asarray(drawn.astype(out[name].dtype))
    for name, factor in factors.items():
        out[name] = (out[name] * factor).astype(out[name].dtype)
    return out
```

```python
from contextlib import ExitStack

import concourse.bass as bass
from concourse import mybir

F32 = mybir.dt.float32
F32R = mybir.dt.float32r
U32 = mybir.dt.uint32
ALU = mybir.AluOpType
ACT = mybir.ActivationFunctionType
AX_X = mybir.AxisListType.X

P = 128
D = 1024
KD = D // P
LAT = 512
CTX = 128
T = LAT + CTX
TB = T // P
LB = LAT // P
HT = T // 2
SEQ_OF = [0] * LB + [1]
SSDW, NH, HD, NG, NS = 512, 8, 64, 2, 64
XBC = SSDW + 2 * NG * NS
XF = XBC // P
TAPS = 5
PADW = 2 + LAT + 2 + 2 + CTX + 2
QR, KVR, ROPE, NOPE, VD = 384, 256, 32, 64, 64
QD = NOPE + ROPE
PAST = 128
KEYS = PAST + T
KB = KEYS // P
C_DT = SSDW + XBC
C_CQ = C_DT + 2 * NH
C_KV = C_CQ + QR
C_KR = C_KV + KVR
IN_COLS = C_KR + ROPE
NMOD = 6
FE = 1408
FT = FE // P
NE = 8
EPS = 1e-6
SCALE = float(QD) ** -0.5
FAR = -1e30


class Signal:

    def __init__(self, nc, ctx, name):
        self.sem = ctx.enter_context(nc.semaphore(name))
        self.base = 0
        self.sent = 0

    def up(self, n=1):
        self.sent += n
        return self.sem, n

    def at(self, n):
        return self.sem, self.base + n

    def close(self):
        self.base, self.sent = self.base + self.sent, 0


def insert_dim(ap, at, n):
    dims = [list(d) for d in ap.ap]
    dims.insert(at, [0, n])
    return bass.AP(tensor=ap.tensor, offset=ap.offset, ap=dims)


class Program:
    def __init__(self, nc, io, ctx):
        self.nc, self.io, self.ctx = nc, io, ctx
        self.signals = {}
        self.stage_no = 0
        sb = self.sb
        self.psum = ctx.enter_context(nc.psum_tensor("psum", [P, 8, 512], F32))
        self.x = sb("x", [P, TB, D])
        self.ident = sb("ident", [P, P])
        self.ones = sb("ones", [P, P])
        self.tri = sb("tri", [P, 2, P])
        self.far = sb("far", [P, 2, P])
        self.silu_c = sb("silu_c", [P, KD, 2])
        self.mod = sb("mod", [P, NMOD * KD, 2])
        self.gains = sb("gains", [P, 4, KD])
        self.scale_in = sb("scale_in", [P, 2, KD, 2])
        self.gate_out = sb("gate_out", [P, 2, KD, 2])
        self.stat = sb("stat", [P, TB])
        self.rstd = sb("rstd", [P, TB])

    def sb(self, name, shape, dt=F32, ctx=None):
        return (ctx or self.ctx).enter_context(self.nc.sbuf_tensor(name, shape, dt))

    def sig(self, name):
        if name not in self.signals:
            self.signals[name] = Signal(self.nc, self.ctx, name)
        return self.signals[name]

    def close_stage(self):
        for s in self.signals.values():
            s.close()


def chained(signal):
    count = [0]

    def link(eng, ins):
        count[0] += 1
        ins.then_inc(*signal.up())
        eng.wait_ge(*signal.at(count[0]))
    return link


def stage_setup(p):
    nc, io = p.nc, p.io
    x_in, c_in = p.sig("x_in"), p.sig("c_in")
    consts, pool_chain, silu_done = p.sig("consts"), p.sig("pool_chain"), p.sig("silu_done")
    with nc.Block() as block:
        @block.sync
        def _(sp):
            with nc.allow_non_contiguous_dma(reason="2048 conditioning values, one per partition row"):
                sp.dma_start(p.silu_c[:, :, 0], io["c"].rearrange("o (k p) -> p (o k)", p=P)).then_inc(*c_in.up(16))
                sp.dma_start(p.silu_c[:, :, 1], io["c_ctx"].rearrange("(k p) -> p k", p=P)).then_inc(*c_in.up(16))
            sp.dma_start(p.x[:, 0:LB], io["x_sample"].rearrange("o (b p) d -> p (o b) d", p=P)).then_inc(*x_in.up(16))
            sp.dma_start(p.x[:, LB], io["x_prompt"].rearrange("o p d -> p (o d)")).then_inc(*x_in.up(16))

        @block.gpsimd
        def _(pool):
            link = chained(pool_chain)
            pool.memset(p.ident[:], 0.0)
            pool.memset(p.ones[:], 1.0)
            pool.memset(p.tri[:], 1.0)
            link(pool, pool.memset(p.far[:], 0.0))
            pool.affine_select(out=p.ident[:], in_=p.ident[:], compare_op=ALU.not_equal, fill=1.0, base=0,
                               pattern=[[-1, P]], channel_multiplier=1)
            for tile, fill in ((p.tri, 0.0), (p.far, FAR)):
                pool.affine_select(out=tile[:, 0], in_=tile[:, 0], compare_op=ALU.is_ge, fill=fill, base=0,
                                   pattern=[[1, P]], channel_multiplier=-1)
                last = pool.affine_select(out=tile[:, 1], in_=tile[:, 1], compare_op=ALU.is_ge, fill=fill, base=0,
                                          pattern=[[-1, P]], channel_multiplier=1)
            last.then_inc(*consts.up())

        @block.scalar
        def _(act):
            act.wait_ge(*c_in.at(32))
            act.activation(p.silu_c[:], p.silu_c[:], ACT.Silu).then_inc(*silu_done.up())
            act.wait_ge(*silu_done.at(1))
            act.wait_ge(*x_in.at(32))
    p.close_stage()


def stage_modulation(p, l):
    nc, io = p.nc, p.io
    cols, ring = 256, 4
    n_chunks = NMOD * D // cols
    per = cols // P
    w_landed = [p.sig(f"wmod_landed{r}") for r in range(ring)]
    small, w_used, mod_ps, dve_c = p.sig("mod_small"), p.sig("wmod_used"), p.sig("mod_ps"), p.sig("dve_chain")
    with ExitStack() as own:
        w = p.sb(f"wmod{l}", [P, ring, KD, cols], ctx=own)
        b = p.sb(f"bmod{l}", [P, NMOD * KD], ctx=own)
        with nc.Block() as block:
            @block.sync
            def _(sp):
                with nc.allow_non_contiguous_dma(reason="bias and gains, feature-major"):
                    sp.dma_start(b[:], io["b_mod"][l].rearrange("(k p) -> p k", p=P)).then_inc(*small.up(16))
                    for j, name in enumerate(("norm_pre_mix", "norm_post_mix", "norm_pre_ffn", "norm_post_ffn")):
                        sp.dma_start(p.gains[:, j], io[name][l].rearrange("(k p) -> p k", p=P)).then_inc(*small.up(16))
                for i in range(n_chunks):
                    if i >= ring:
                        sp.wait_ge(*w_used.at(i - ring + 1))
                    sp.dma_start(w[:, i % ring], io["w_mod"][l, :, i * cols:(i + 1) * cols].rearrange(
                        "(k p) f -> p k f", p=P)).then_inc(*w_landed[i % ring].up(16))

            @block.tensor
            def _(pe):
                out = p.psum[:, 0, 0:NMOD * KD * 2].rearrange("p (m s) -> p m s", s=2)
                for i in range(n_chunks):
                    pe.wait_ge(*w_landed[i % ring].at(16 * (i // ring + 1)))
                    for j in range(per):
                        for k in range(KD):
                            last = pe.matmul(out[:, i * per + j, :], w[:, i % ring, k, j * P:(j + 1) * P],
                                             p.silu_c[:, k, :], start=(k == 0), stop=(k == KD - 1))
                    last.then_inc(*w_used.up())


            @block.vector
            def _(dve):
                link = chained(dve_c)
                dve.wait_ge(*small.at(80))
                dve.wait_ge(*w_used.at(n_chunks))
                link(dve, dve.tensor_tensor(
                    p.mod[:], p.psum[:, 0, 0:NMOD * KD * 2].rearrange("p (m s) -> p m s", s=2),
                    b[:].to_broadcast([P, NMOD * KD, 2]), ALU.add))
                for which in range(2):
                    scale = p.mod[:, (3 * which + 1) * KD:(3 * which + 2) * KD, :]
                    gate = p.mod[:, (3 * which + 2) * KD:(3 * which + 3) * KD, :]
                    link(dve, dve.scalar_tensor_tensor(
                        out=p.scale_in[:, which], in0=scale, scalar=1.0,
                        in1=p.gains[:, 2 * which].to_broadcast([P, KD, 2]), op0=ALU.add, op1=ALU.mult))
                    link(dve, dve.tensor_tensor(p.gate_out[:, which], gate,
                                                p.gains[:, 2 * which + 1].to_broadcast([P, KD, 2]), ALU.mult))
    p.close_stage()


def root_mean(p, act, dve_link, dve, act_in, rms_sum, rms_root, n, count):
    raise NotImplementedError


def stage_pre_norm(p, l, which, hT, split=None):
    nc = p.nc
    sq, mean, root, rs, xn, tr, ev = (p.sig(n) for n in (
        "pn_squares", "pn_mean", "pn_root", "pn_rstd", "pn_scaled", "pn_turned", "pn_evicted"))
    dve_c = p.sig("dve_chain")
    with ExitStack() as own:
        junk = p.sb(f"pn_junk{l}{which}", [P, D], ctx=own)
        xs = p.sb(f"pn_x{l}{which}", [P, 2, D], ctx=own)
        hf = p.sb(f"pn_h{l}{which}", [P, 2, KD, P], ctx=own) if split else None
        with nc.Block() as block:
            @block.scalar
            def _(act):
                for b in range(TB):
                    ins = act.activation(junk[:], p.x[:, b], ACT.Square, accum_out=p.stat[:, b:b + 1])
                    ins.then_inc(*sq.up())
                    act.wait_ge(*sq.at(b + 1))
                act.wait_ge(*mean.at(1))
                act.activation(p.rstd[:], p.stat[:], ACT.Sqrt).then_inc(*root.up())
                for b in range(TB):
                    act.wait_ge(*rs.at(1))
                    if b >= 2:
                        act.wait_ge(*tr.at(b - 1))
                    act.activation(xs[:, b % 2], p.x[:, b], ACT.Copy, scale=p.rstd[:, b:b + 1]).then_inc(*xn.up())

            @block.tensor
            def _(pe):
                for b in range(TB):
                    pe.wait_ge(*xn.at(b + 1))
                    if b >= 4:
                        pe.wait_ge(*ev.at(b - 3))
                    for k in range(KD):
                        last = pe.transpose(p.psum[:, 2 * (b % 4) + k // 4, (k % 4) * P:(k % 4 + 1) * P],
                                            xs[:, b % 2, k * P:(k + 1) * P], p.ident[:])
                    last.then_inc(*tr.up())

            @block.vector
            def _(dve):
                link = chained(dve_c)
                dve.wait_ge(*sq.at(TB))
                dve.tensor_scalar(p.stat[:], p.stat[:], 1.0 / D, EPS, ALU.mult, ALU.add).then_inc(*mean.up())
                dve.wait_ge(*root.at(1))
                dve.reciprocal(p.rstd[:], p.rstd[:]).then_inc(*rs.up())
                for b in range(TB):
                    s = SEQ_OF[b]
                    dve.wait_ge(*tr.at(b + 1))
                    for k in range(KD):
                        out = hf[:, b % 2, k] if split else hT[:, k, b * P:(b + 1) * P]
                        last = dve.tensor_scalar(
                            out, p.psum[:, 2 * (b % 4) + k // 4, (k % 4) * P:(k % 4 + 1) * P],
                            p.scale_in[:, which, k, s:s + 1], p.mod[:, 3 * which * KD + k, s:s + 1],
                            ALU.mult, ALU.add)
                    last.then_inc(*ev.up())
                    if split:
                        hi, lo = split
                        dve.wait_ge(*ev.at(b + 1))
                        link(dve, dve.tensor_copy(hi[:, :, b * P:(b + 1) * P], hf[:, b % 2]))
                        dve.tensor_tensor(lo[:, :, b * P:(b + 1) * P], hf[:, b % 2],
                                          hi[:, :, b * P:(b + 1) * P].bitcast(F32), ALU.subtract)
    p.close_stage()


def stage_in_proj(p, l, hT, t):
    nc, io = p.nc, p.io
    pieces = [(0, SSDW), (C_DT, C_KV), (C_KV, IN_COLS), (SSDW, SSDW + XBC // 2), (SSDW + XBC // 2, C_DT)]
    landed = [p.sig(f"win_landed{i}") for i in range(len(pieces))]
    mm, ev, pads = p.sig("win_ps"), p.sig("win_evicted"), p.sig("win_pads")
    token_out = [t["z"], t["dtcq"], t["ckr"]]
    with ExitStack() as own:
        w = p.sb(f"w_in{l}", [P, KD, IN_COLS], ctx=own)
        groups = [("tok", j, b) for j in range(3) for b in range(TB)] + \
                 [("feat", f, half) for f in range(XF) for half in range(2)]
        with nc.Block() as block:
            @block.sync
            def _(sp):
                for (lo, hi), s in zip(pieces, landed):
                    sp.dma_start(w[:, :, lo:hi], io["w_in"][l, :, lo:hi].rearrange(
                        "(k p) f -> p k f", p=P)).then_inc(*s.up(16))

            @block.tensor
            def _(pe):
                for g, (kind, j, b) in enumerate(groups):
                    piece = j if kind == "tok" else 3 + j * P // (XBC // 2)
                    pe.wait_ge(*landed[piece].at(16))
                    if g >= 8:
                        pe.wait_ge(*ev.at(g - 7))
                    for k in range(KD):
                        if kind == "tok":
                            lo, hi = pieces[j]
                            last = pe.matmul(p.psum[:, g % 8, 0:hi - lo], hT[:, k, b * P:(b + 1) * P],
                                             w[:, k, lo:hi], start=(k == 0), stop=(k == KD - 1))
                        else:
                            c = SSDW + j * P
                            last = pe.matmul(p.psum[:, g % 8, 0:HT], w[:, k, c:c + P],
                                             hT[:, k, b * HT:(b + 1) * HT], start=(k == 0), stop=(k == KD - 1))
                    last.then_inc(*mm.up())

            @block.gpsimd
            def _(pool):
                pad = t["pad"]
                pool.memset(pad[:, :, 0:2], 0.0)
                pool.memset(pad[:, :, 2 + LAT:6 + LAT], 0.0)
                pool.memset(pad[:, :, PADW - 2:PADW], 0.0).then_inc(*pads.up())

            @block.vector
            def _(dve):
                dve.wait_ge(*pads.at(1))
                for g, (kind, j, b) in enumerate(groups):
                    dve.wait_ge(*mm.at(g + 1))
                    if kind == "tok":
                        lo, hi = pieces[j]
                        last = dve.tensor_copy(token_out[j][:, b, :], p.psum[:, g % 8, 0:hi - lo])
                    elif b == 0:
                        last = dve.tensor_copy(t["pad"][:, j, 2:2 + HT], p.psum[:, g % 8, 0:HT])
                    else:
                        dve.tensor_copy(t["pad"][:, j, 2 + HT:2 + LAT], p.psum[:, g % 8, 0:LAT - HT])
                        last = dve.tensor_copy(t["pad"][:, j, 6 + LAT:6 + LAT + CTX],
                                               p.psum[:, g % 8, LAT - HT:HT])
                    last.then_inc(*ev.up())
    p.close_stage()


def stage_ssd(p, l, t):
    nc, io = p.nc, p.io
    small = p.sig("ssd_small")
    conv_done, silu_done = p.sig("conv_done"), p.sig("conv_silu_done")
    dve_c, act_c = p.sig("dve_chain"), p.sig("act_chain")
    dt_pre, e_neg, ln_u, a_exp, z_silu = (p.sig(n) for n in ("dt_pre", "dt_exp", "dt_log", "a_exp", "z_silu"))
    da_ready, la_ps, la_sb, la_exps = p.sig("da_ready"), p.sig("la_ps"), p.sig("la_sb"), p.sig("la_exps")
    turned, turned_out = p.sig("xs_turned"), p.sig("xs_turned_out")
    wx_ready, cs_ps, cs_used = p.sig("wx_ready"), p.sig("cs_ps"), p.sig("cs_used")
    st_in, st_turned, st_ready = p.sig("st_in"), p.sig("st_turned"), p.sig("st_ready")
    lab_ps, seg_ready, dec_ready, cb_ps, s_ready, y_ps, y_used = (p.sig(n) for n in (
        "lab_ps", "seg_ready", "decay_ready", "cb_ps", "scores_ready", "y_ps", "y_used"))
    fin_turned, fin_out, fin_stored = p.sig("fin_turned"), p.sig("fin_out"), p.sig("fin_stored")
    with ExitStack() as own:
        def sb(name, shape):
            return p.sb(f"ssd_{name}{l}", shape, ctx=own)
        cw, cb = sb("cw", [P, XF, TAPS]), sb("cb", [P, XF])
        dtb, alog, dsk = sb("dtb", [P, 2 * NH]), sb("alog", [P, 2 * NH]), sb("dsk", [P, NH])
        acc = sb("acc", [P, 2, PADW - 4])
        xbc = sb("xbc", [P, XF, T])
        btok = sb("btok", [P, TB, P])
        s5 = [P, TB, 2 * NH]
        v, neg, e, u, ln, dt, da, la, el, te, cd = (sb(n, s5) for n in (
            "v", "neg", "e", "u", "ln", "dt", "da", "la", "el", "te", "cd"))
        cdg = sb("cdg", [P, TB, 2, NH // 2])
        wx = sb("wx", [P, 2, SSDW])
        hs = sb("hs", [P, 2, TB, 256])
        stl = sb("stl", [P, 2, 2, P])
        hfin = sb("hfin", [P, 2, 256])
        seg = sb("seg", [P, 2, NH, P])
        cbs = sb("cbs", [P, NG, P])
        t1, t2 = sb("t1", [P, SSDW]), sb("t2", [P, SSDW])
        pad, z, xst, y = t["pad"], t["z"], t["xst"], t["y_ssd"]
        dtr = t["dtcq"][:, :, 0:2 * NH]
        with nc.Block() as block:
            @block.sync
            def _(sp):
                with nc.allow_non_contiguous_dma(reason="small per-channel vectors"):
                    for k in range(TAPS):
                        sp.dma_start(cw[:, :, k], io["conv_w"][l, k].rearrange("(f p) -> p f", p=P)).then_inc(*small.up(16))
                    sp.dma_start(cb[:], io["conv_b"][l].rearrange("(f p) -> p f", p=P)).then_inc(*small.up(16))
                for tile, name in ((dtb, "dt_bias"), (alog, "a_log"), (dsk, "d_skip")):
                    row = io[name][l].rearrange("a b -> (a b)") if name != "d_skip" else io[name][l]
                    sp.dma_start(tile[:], row.partition_broadcast(P)).then_inc(*small.up(16))
                for d in range(2):
                    for g in range(2):
                        sp.dma_start(stl[:, d, :, g * NS:(g + 1) * NS], io["state_ssm"][0, l, d, 4 * g:4 * g + 4].rearrange(
                            "(j h) q n -> (h q) j n", h=2)).then_inc(*st_in.up(16))
                sp.wait_ge(*fin_out.at(2))
                for d in range(2):
                    for g in range(2):
                        sp.dma_start(io["new_ssm"][0, l, d, 4 * g:4 * g + 4].rearrange("(j h) q n -> (h q) j n", h=2),
                                     stl[:, d, :, g * NS:(g + 1) * NS]).then_inc(*fin_stored.up(16))
                sp.wait_ge(*fin_stored.at(64))

            @block.scalar
            def _(act):
                act.wait_ge(*small.at(144))
                for f in range(XF):
                    act.wait_ge(*conv_done.at(f + 1))
                    act.activation(xbc[:, f, 0:LAT], acc[:, f % 2, 0:LAT], ACT.Silu, bias=cb[:, f:f + 1])
                    act.activation(xbc[:, f, LAT:T], acc[:, f % 2, 4 + LAT:4 + LAT + CTX], ACT.Silu,
                                   bias=cb[:, f:f + 1]).then_inc(*silu_done.up())
                act.activation(z[:], z[:], ACT.Silu).then_inc(*z_silu.up())
                act.wait_ge(*dt_pre.at(1))
                act.activation(e[:], neg[:], ACT.Exp).then_inc(*e_neg.up())
                act.activation(alog[:], alog[:], ACT.Exp).then_inc(*a_exp.up())
                act.wait_ge(*dt_pre.at(2))
                act.activation(ln[:], u[:], ACT.Ln).then_inc(*ln_u.up())
                act.wait_ge(*la_sb.at(1))
                act.activation(el[:], la[:], ACT.Exp)
                act.activation(cd[:], cd[:], ACT.Exp)
                act.activation(te[:], te[:], ACT.Exp).then_inc(*la_exps.up())
                for b in range(TB):
                    for d in range(2):
                        act.wait_ge(*seg_ready.at(2 * b + d + 1))
                        act.activation(seg[:, d], seg[:, d], ACT.Exp).then_inc(*dec_ready.up())

            @block.tensor
            def _(pe):
                def turn_state(bank, src):
                    for d in range(2):
                        for j in range(2):
                            last = pe.transpose(p.psum[:, bank, (2 * d + j) * P:(2 * d + j + 1) * P],
                                                src(d, j), p.ident[:])
                    return last
                pe.wait_ge(*st_in.at(64))
                turn_state(7, lambda d, j: stl[:, d, j, :]).then_inc(*st_turned.up())
                pe.wait_ge(*da_ready.at(1))
                lap = p.psum[:, 6, 0:4 * NH * TB].rearrange("p (b c) -> p b c", b=TB)
                for b in range(TB):
                    pe.matmul(lap[:, b, 0:NH], p.tri[:, 0], da[:, b, 0:NH], start=True, stop=True)
                    pe.matmul(lap[:, b, NH:2 * NH], p.tri[:, 1], da[:, b, NH:2 * NH], start=True, stop=True)
                    last = pe.matmul(lap[:, b, 2 * NH:4 * NH], p.ones[:], da[:, b, :], start=True, stop=True)
                last.then_inc(*la_ps.up())
                pe.wait_ge(*silu_done.at(XF - 1))
                for b in range(TB):
                    if b >= 2:
                        pe.wait_ge(*turned_out.at(b - 1))
                    for f in range(4):
                        pe.transpose(p.psum[:, b % 2, f * P:(f + 1) * P], xbc[:, f, b * P:(b + 1) * P], p.ident[:])
                    pe.transpose(p.psum[:, 2 + b % 2, 0:P], xbc[:, 4, b * P:(b + 1) * P],
                                 p.ident[:]).then_inc(*turned.up())
                pe.wait_ge(*silu_done.at(XF))
                for b in range(TB):
                    pe.wait_ge(*wx_ready.at(b + 1))
                    if b >= 2:
                        pe.wait_ge(*cs_used.at(b - 1))
                    for d in range(2):
                        for g in range(NG):
                            last = pe.matmul(p.psum[g * NS:(g + 1) * NS, 4 + b % 2, d * 256:(d + 1) * 256],
                                             btok[:, b, g * NS:(g + 1) * NS], wx[:, d, g * 256:(g + 1) * 256],
                                             start=(d == 0), stop=True, skip_group_check=True)
                    last.then_inc(*cs_ps.up())
                pe.wait_ge(*st_ready.at(1))
                for b in range(TB):
                    for d in range(2):
                        if b >= 1:
                            pe.wait_ge(*seg_ready.at(2 * (b - 1) + d + 1))
                        for h in range(NH):
                            last = pe.matmul(p.psum[:, 2 * d + h // 4, (h % 4) * P:(h % 4 + 1) * P],
                                             da[:, b, d * NH + h:d * NH + h + 1].to_broadcast([P, P]),
                                             p.tri[:, d], start=True, stop=True)
                        last.then_inc(*lab_ps.up())
                    if b >= 1:
                        pe.wait_ge(*y_used.at(b))
                    for g in range(NG):
                        part = slice(g * NS, (g + 1) * NS)
                        last = pe.matmul(p.psum[:, 7 - 3 * g, 0:P], xbc[part, 4, b * P:(b + 1) * P],
                                         xbc[part, 5, b * P:(b + 1) * P], start=True, stop=True)
                    last.then_inc(*cb_ps.up())
                    for d in range(2):
                        for g in range(NG):
                            part = slice(g * NS, (g + 1) * NS)
                            pe.matmul(p.psum[:, 5 + g, d * 256:(d + 1) * 256], xbc[part, 5, b * P:(b + 1) * P],
                                      hs[part, d, b, :], start=True, stop=True)
                    pe.wait_ge(*s_ready.at(b + 1))
                    for h in range(NH):
                        last = pe.matmul(p.psum[:, 4, h * HD:(h + 1) * HD], seg[:, 0, h],
                                         xst[:, b, h * HD:(h + 1) * HD], start=True, stop=True)
                    last.then_inc(*y_ps.up())
                pe.wait_ge(*y_used.at(TB))
                turn_state(7, lambda d, j: hfin[:, d, j * P:(j + 1) * P]).then_inc(*fin_turned.up())

            @block.vector
            def _(dve):
                link = chained(dve_c)
                dve.wait_ge(*small.at(144))
                link(dve, dve.tensor_tensor(v[:], dtr, insert_dim(dtb[:], 1, TB), ALU.add))
                dve.scalar_tensor_tensor(out=neg[:], in0=v[:], scalar=-1.0, in1=v[:], op0=ALU.mult,
                                         op1=ALU.min).then_inc(*dt_pre.up())
                for f in range(XF):
                    width = PADW - 4
                    if f >= 2:
                        dve.wait_ge(*silu_done.at(f - 1))
                    link(dve, dve.tensor_scalar(acc[:, f % 2], pad[:, f, 0:width], cw[:, f, 0:1], None, ALU.mult))
                    for k in range(1, TAPS):
                        ins = dve.scalar_tensor_tensor(out=acc[:, f % 2], in0=pad[:, f, k:k + width],
                                                       scalar=cw[:, f, k:k + 1], in1=acc[:, f % 2],
                                                       op0=ALU.mult, op1=ALU.add)
                        if k < TAPS - 1:
                            link(dve, ins)
                    ins.then_inc(*conv_done.up())
                dve.wait_ge(*e_neg.at(1))
                link(dve, dve.tensor_scalar(u[:], e[:], 1.0, None, ALU.add))
                link(dve, dve.tensor_scalar(dt[:], u[:], -1.0, None, ALU.add))
                link(dve, dve.tensor_tensor(dt[:], e[:], dt[:], ALU.subtract))
                dve.scalar_tensor_tensor(out=v[:], in0=v[:], scalar=0.0, in1=dt[:], op0=ALU.max,
                                         op1=ALU.add).then_inc(*dt_pre.up())
                dve.wait_ge(*dt_pre.at(2))
                dve.wait_ge(*ln_u.at(1))
                link(dve, dve.tensor_tensor(dt[:], v[:], ln[:], ALU.add))
                dve.wait_ge(*a_exp.at(1))
                dve.scalar_tensor_tensor(out=da[:], in0=dt[:], scalar=-1.0, in1=insert_dim(alog[:], 1, TB),
                                         op0=ALU.mult, op1=ALU.mult).then_inc(*da_ready.up())
                dve.wait_ge(*st_turned.at(1))
                link(dve, dve.tensor_copy(hs[:, 0, 0, :], p.psum[:, 7, 0:256]))
                link(dve, dve.tensor_copy(hs[:, 1, LB - 1, :], p.psum[:, 7, 256:512]))
                link(dve, dve.memset(hs[:, :, LB, :], 0.0))
                dve.wait_ge(*la_ps.at(1))
                lap = p.psum[:, 6, 0:4 * NH * TB].rearrange("p (b c) -> p b c", b=TB)
                link(dve, dve.tensor_copy(la[:], lap[:, :, 0:2 * NH]))
                link(dve, dve.tensor_copy(cd[:], lap[:, :, 2 * NH:4 * NH]))
                dve.tensor_tensor(te[:], cd[:], la[:], ALU.subtract).then_inc(*la_sb.up())
                dve.wait_ge(*la_exps.at(1))
                link(dve, dve.tensor_tensor(te[:], te[:], dt[:], ALU.mult))
                for g in range(NG):
                    for d in range(2):
                        link(dve, dve.tensor_copy(cdg[g * NS:(g + 1) * NS, :, d],
                                                  cd[g * NS:(g + 1) * NS, :, d * NH + 4 * g:d * NH + 4 * g + 4]))
                for b in range(TB):
                    dve.wait_ge(*turned.at(b + 1))
                    link(dve, dve.tensor_copy(xst[:, b], p.psum[:, b % 2]))
                    dve.tensor_copy(btok[:, b], p.psum[:, 2 + b % 2, 0:P]).then_inc(*turned_out.up())

                def advance(b, d, out):
                    link(dve, dve.tensor_tensor(out.rearrange("p (h q) -> p h q", h=4),
                                                hs[:, d, b].rearrange("p (h q) -> p h q", h=4),
                                                cdg[:, b, d].to_broadcast([P, 4, HD]), ALU.mult))
                    link(dve, dve.tensor_tensor(out, out, hadd(b, d), ALU.add))

                def hadd(b, d):
                    return adds[:, b, d, :]
                adds = t["qkv_room"][:, 0:TB * 512].rearrange("p (b d c) -> p b d c", b=TB, d=2)
                for b in range(TB):
                    if b >= 1:
                        dve.wait_ge(*cs_ps.at(b))
                    for d in range(2):
                        last = dve.tensor_tensor(wx[:, d].rearrange("p (h q) -> p h q", h=NH),
                                                 xst[:, b].rearrange("p (h q) -> p h q", h=NH),
                                                 te[:, b, d * NH:(d + 1) * NH].to_broadcast([P, NH, HD]), ALU.mult)
                    last.then_inc(*wx_ready.up())
                    dve.wait_ge(*cs_ps.at(b + 1))
                    dve.tensor_copy(adds[:, b], p.psum[:, 4 + b % 2].rearrange(
                        "p (d c) -> p d c", d=2)).then_inc(*cs_used.up())
                dve.wait_ge(*cs_used.at(TB))
                for b in range(LB - 1):
                    advance(b, 0, hs[:, 0, b + 1])
                for b in range(LB - 1, 0, -1):
                    advance(b, 1, hs[:, 1, b - 1])
                dve.tensor_copy(hfin[:], adds[:, LB]).then_inc(*st_ready.up())
                for b in range(TB):
                    for d in range(2):
                        dve.wait_ge(*lab_ps.at(2 * b + d + 1))
                        if b >= 1:
                            dve.wait_ge(*y_ps.at(b))
                        for h in range(NH):
                            last = dve.scalar_tensor_tensor(
                                out=seg[:, d, h], in0=p.psum[:, 2 * d + h // 4, (h % 4) * P:(h % 4 + 1) * P],
                                scalar=la[:, b, d * NH + h:d * NH + h + 1], in1=p.far[:, d],
                                op0=ALU.subtract, op1=ALU.add)
                        last.then_inc(*seg_ready.up())
                    dve.wait_ge(*cb_ps.at(b + 1))
                    dve.tensor_copy(cbs[:, 0], p.psum[:, 7, 0:P])
                    link(dve, dve.tensor_copy(cbs[:, 1], p.psum[:, 4, 0:P]))
                    dve.wait_ge(*dec_ready.at(2 * b + 1))
                    for h in range(NH):
                        last = dve.tensor_scalar(seg[:, 0, h], seg[:, 0, h], dt[:, b, h:h + 1], None, ALU.mult)
                    link(dve, last)
                    dve.wait_ge(*dec_ready.at(2 * b + 2))
                    for h in range(NH):
                        last = dve.scalar_tensor_tensor(
                            out=seg[:, 0, h], in0=seg[:, 1, h], scalar=dt[:, b, NH + h:NH + h + 1],
                            in1=seg[:, 0, h], op0=ALU.mult, op1=ALU.add)
                    link(dve, last)
                    for g in range(NG):
                        last = dve.tensor_tensor(seg[:, 0, 4 * g:4 * g + 4], seg[:, 0, 4 * g:4 * g + 4],
                                                 insert_dim(cbs[:, g], 1, 4), ALU.mult)
                    last.then_inc(*s_ready.up())

                    def heads(ap):
                        return ap.rearrange("p (h q) -> p h q", h=NH)

                    def by_group(ap):
                        return ap.rearrange("p (g h q) -> p g h q", g=NG, q=HD)

                    def inter(d):
                        return p.psum[:, 5:7, d * 256:(d + 1) * 256].rearrange("p g (h q) -> p g h q", q=HD)

                    def heads_la(d):
                        la_exp = el[:, b, d * NH:(d + 1) * NH].rearrange("p (g h) -> p g h", g=NG)
                        return la_exp.to_broadcast([P, NG, NH // NG, HD])
                    dve.wait_ge(*y_ps.at(b + 1))
                    link(dve, dve.tensor_tensor(by_group(t1[:]), inter(0), heads_la(0), ALU.mult))
                    link(dve, dve.tensor_tensor(by_group(t2[:]), inter(1), heads_la(1), ALU.mult))
                    link(dve, dve.tensor_tensor(t1[:], t1[:], t2[:], ALU.add))
                    link(dve, dve.tensor_tensor(heads(t2[:]), heads(xst[:, b]), dsk[:].to_broadcast([P, NH, HD]),
                                                ALU.mult))
                    link(dve, dve.tensor_tensor(t2[:], p.psum[:, 4], t2[:], ALU.add))
                    link(dve, dve.tensor_tensor(t1[:], t1[:], t2[:], ALU.add))
                    if b == 0:
                        dve.wait_ge(*z_silu.at(1))
                    dve.tensor_tensor(y[:, b], t1[:], z[:, b], ALU.mult).then_inc(*y_used.up())
                dve.wait_ge(*fin_turned.at(1))
                dve.tensor_copy(stl[:, 0], p.psum[:, 7, 0:256].rearrange("p (j c) -> p j c", j=2)).then_inc(*fin_out.up())
                dve.tensor_copy(stl[:, 1], p.psum[:, 7, 256:512].rearrange("p (j c) -> p j c", j=2)).then_inc(*fin_out.up())
    p.close_stage()


def stage_attention(p, l, t):
    nc, io = p.nc, p.io
    w_in, gains_in, cache_in = p.sig("at_w_in"), p.sig("at_gains_in"), p.sig("at_cache_in")
    sq, mean, root, rs = p.sig("at_squares"), p.sig("at_mean"), p.sig("at_root"), p.sig("at_rstd")
    kvn, krt_ready, lat_tr, lat_ev = p.sig("at_kvn"), p.sig("at_krt"), p.sig("at_lat_turned"), p.sig("at_lat_out")
    new_out = p.sig("at_new_stored")
    gm_ps, gm_ev, qt_ready = p.sig("at_gemm_ps"), p.sig("at_gemm_out"), p.sig("at_q_ready")
    tr_ps, tr_ev = p.sig("at_turned"), p.sig("at_turned_out")
    sc_ps, mx_ready, e_ready, pt_ps, pt_ev, o_ps, o_ev = (p.sig(n) for n in (
        "at_scores_ps", "at_max", "at_exp", "at_probs_turned", "at_probs_out", "at_o_ps", "at_o_out"))
    zeroed = p.sig("at_zeroed")
    dve_c, act_c = p.sig("dve_chain"), p.sig("act_chain")
    QF, VF = QR // P, KVR // P
    with ExitStack() as own:
        def sb(name, shape):
            return p.sb(f"at_{name}{l}", shape, ctx=own)
        wq = sb("wq", [P, QF, NH * QD])
        wkv = sb("wkv", [P, VF, NH * (NOPE + VD)])
        gq, kvrow = sb("gq", [P, QF]), sb("kvrow", [P, KVR])
        cos, sin = sb("cos", [P, LB, ROPE]), sb("sin", [P, LB, ROPE])
        past = sb("past", [P, KVR])
        krt = sb("krt", [P, KB, QD])
        junk = sb("junk", [P, QR])
        stat, rstd = sb("stat", [P, 2, TB]), sb("rstd", [P, 2, TB])
        cqT = sb("cqT", [P, QF, T])
        ckvT = sb("ckvT", [P, VF, KEYS])
        qtok = sb("qtok", [P, 2, NH * QD])
        ra, rb = sb("ra", [P, NH, ROPE]), sb("rb", [P, NH, ROPE])
        qT = sb("qT", [P, NH, T])
        kT = t["qkv_room"].rearrange("p (h k) -> p h k", h=NH)
        vt = sb("vt", [P, KB, NH * VD])
        prob = sb("prob", [P, 2, LAT + PAST])
        probT = sb("probT", [P, 2, LAT + PAST])
        mx = sb("mx", [P, 2 * NH, 2])
        total = sb("total", [P, 2, NH])
        cq, ckr, o = t["dtcq"][:, :, 2 * NH:], t["ckr"], t["o"]
        ck, kr = ckr[:, :, 0:KVR], ckr[:, :, KVR:KVR + ROPE]
        turns = [("past", 0)] + [("tok", b) for b in range(TB)]
        items = [(b, h) for b in range(TB) for h in range(NH)]

        def keys_of(b):
            return (0, PAST + LAT) if b < LB else (PAST + LAT, KEYS)
        with nc.Block() as block:
            @block.sync
            def _(sp):
                sp.dma_start(wq[:], io["w_uq"][l].rearrange("(k p) f -> p k f", p=P)).then_inc(*w_in.up(16))
                sp.dma_start(wkv[:], io["w_ukv"][l].rearrange("(k p) f -> p k f", p=P)).then_inc(*w_in.up(16))
                with nc.allow_non_contiguous_dma(reason="one gain per partition"):
                    sp.dma_start(gq[:], io["q_norm"][l].rearrange("(k p) -> p k", p=P)).then_inc(*gains_in.up(16))
                sp.dma_start(kvrow[:], io["kv_norm"][l].partition_broadcast(P)).then_inc(*gains_in.up(16))
                sp.dma_start(cos[:], io["rope_cos"].rearrange("(b p) r -> p b r", p=P)).then_inc(*gains_in.up(16))
                sp.dma_start(sin[:], io["rope_sin"].rearrange("(b p) r -> p b r", p=P)).then_inc(*gains_in.up(16))
                sp.dma_start(past[:], io["cache_ckv"][0, l]).then_inc(*cache_in.up(16))
                sp.wait_ge(*zeroed.at(1))
                sp.dma_start(krt[:, 0, NOPE:QD], io["cache_krope"][0, l]).then_inc(*cache_in.up(16))
                sp.dma_start(io["new_krope"][0, l], kr[:, LB]).then_inc(*new_out.up(16))
                sp.wait_ge(*kvn.at(TB))
                sp.dma_start(io["new_ckv"][0, l], ck[:, LB]).then_inc(*new_out.up(16))
                sp.wait_ge(*new_out.at(32))

            @block.gpsimd
            def _(pool):
                pool.memset(krt[:], 0.0).then_inc(*zeroed.up())

            @block.scalar
            def _(act):
                for b in range(TB):
                    act.activation(junk[:], cq[:, b], ACT.Square, accum_out=stat[:, 0, b:b + 1]).then_inc(*sq.up())
                    act.wait_ge(*sq.at(2 * b + 1))
                    act.activation(junk[:, 0:KVR], ck[:, b], ACT.Square, accum_out=stat[:, 1, b:b + 1]).then_inc(*sq.up())
                    act.wait_ge(*sq.at(2 * b + 2))
                act.wait_ge(*mean.at(1))
                act.activation(rstd[:], stat[:], ACT.Sqrt).then_inc(*root.up())
                for n, (b, h) in enumerate(items):
                    lo, hi = keys_of(b)
                    act.wait_ge(*mx_ready.at(n + 1))
                    if n >= 2:
                        act.wait_ge(*pt_ps.at(n - 1))
                    if b >= 2 and h == 0:
                        act.wait_ge(*o_ev.at(b - 1))
                    w = (hi - lo) // 2
                    act.activation(prob[:, n % 2, 0:hi - lo].rearrange("p (a k) -> p a k", a=2),
                                   p.psum[:, 2 * (n % 2):2 * (n % 2) + 2, 0:w], ACT.Exp,
                                   bias=mx[:, n % (2 * NH), 1:2], scale=SCALE,
                                   accum_out=total[:, b % 2, h:h + 1]).then_inc(*e_ready.up())

            @block.tensor
            def _(pe):
                def turn_queries(pe, b):
                    pe.wait_ge(*qt_ready.at(b + 1))
                    if b >= 2:
                        pe.wait_ge(*tr_ev.at(b - 1))
                    for h in range(NH):
                        last = pe.transpose(p.psum[0:QD, 4 + 2 * (b % 2) + h // 4, (h % 4) * P:(h % 4 + 1) * P],
                                            qtok[:, b % 2, h * QD:(h + 1) * QD], p.ident[:])
                    last.then_inc(*tr_ps.up())

                pe.wait_ge(*cache_in.at(32))
                for n, (kind, b) in enumerate(turns):
                    if kind == "tok":
                        pe.wait_ge(*kvn.at(b + 1))
                    if n >= 4:
                        pe.wait_ge(*lat_ev.at(n - 3))
                    for k in range(VF):
                        src = past[:, k * P:(k + 1) * P] if kind == "past" else ck[:, b, k * P:(k + 1) * P]
                        last = pe.transpose(p.psum[:, 2 * (n % 4), k * P:(k + 1) * P], src, p.ident[:])
                    if kind == "tok":
                        for k in range(QF):
                            last = pe.transpose(p.psum[:, 2 * (n % 4) + 1, k * P:(k + 1) * P],
                                                cq[:, b, k * P:(k + 1) * P], p.ident[:])
                    last.then_inc(*lat_tr.up())
                pe.wait_ge(*w_in.at(32))
                pe.wait_ge(*lat_ev.at(len(turns)))
                g = 0
                for b in range(TB):
                    if b >= 2:
                        pe.wait_ge(*gm_ev.at(b - 1))
                    for part, (lo, hi) in enumerate(((0, 512), (512, NH * QD))):
                        for k in range(QF):
                            last = pe.matmul(p.psum[:, 2 * (b % 2) + part, 0:hi - lo], cqT[:, k, b * P:(b + 1) * P],
                                             wq[:, k, lo:hi], start=(k == 0), stop=(k == QF - 1))
                    last.then_inc(*gm_ps.up())
                    if b >= 1:
                        turn_queries(pe, b - 1)
                turn_queries(pe, TB - 1)
                for h in range(NH):
                    if h < 2:
                        pe.wait_ge(*gm_ev.at(TB - 1 + h))
                    else:
                        pe.wait_ge(*gm_ev.at(TB + h - 1))
                    for part in range(2):
                        for k in range(VF):
                            last = pe.matmul(p.psum[0:NOPE, 2 * (h % 2) + part, 0:KEYS // 2],
                                             wkv[:, k, h * (NOPE + VD):h * (NOPE + VD) + NOPE],
                                             ckvT[:, k, part * KEYS // 2:(part + 1) * KEYS // 2],
                                             start=(k == 0), stop=(k == VF - 1))
                    last.then_inc(*gm_ps.up())
                for n in range(KB):
                    pe.wait_ge(*gm_ev.at(TB + NH + n - 1))
                    for k in range(VF):
                        last = pe.matmul(p.psum[:, 2 * (n % 2), 0:NH * VD], ckvT[:, k, n * P:(n + 1) * P],
                                         wkv[:, k].rearrange("p (h c) -> p h c", h=NH)[:, :, NOPE:NOPE + VD],
                                         start=(k == 0), stop=(k == VF - 1))
                    last.then_inc(*gm_ps.up())
                pe.wait_ge(*krt_ready.at(1))
                pe.wait_ge(*tr_ev.at(TB))
                for n in range(KB):
                    last = pe.transpose(p.psum[0:QD, 4 + n // 3, (n % 3) * P:(n % 3 + 1) * P], krt[:, n, :], p.ident[:])
                last.then_inc(*tr_ps.up())
                pe.wait_ge(*gm_ev.at(TB + NH + KB))
                pe.wait_ge(*tr_ev.at(TB + 1))

                def scores(n):
                    b, h = items[n]
                    lo, hi = keys_of(b)
                    w = (hi - lo) // 2
                    if n >= 2:
                        pe.wait_ge(*e_ready.at(n - 1))
                    for part in range(2):
                        last = pe.matmul(p.psum[:, 2 * (n % 2) + part, 0:w], qT[0:QD, h, b * P:(b + 1) * P],
                                         kT[0:QD, h, lo + part * w:lo + (part + 1) * w], start=True, stop=True)
                    last.then_inc(*sc_ps.up())

                def turn_probs(n):
                    b, h = items[n]
                    lo, hi = keys_of(b)
                    pe.wait_ge(*e_ready.at(n + 1))
                    if n >= 1:
                        pe.wait_ge(*pt_ev.at(n))
                    for k in range((hi - lo) // P):
                        last = pe.transpose(p.psum[:, 4 + k // 4, (k % 4) * P:(k % 4 + 1) * P],
                                            prob[:, n % 2, k * P:(k + 1) * P], p.ident[:])
                    last.then_inc(*pt_ps.up())

                def outputs(n):
                    b, h = items[n]
                    lo, hi = keys_of(b)
                    pe.wait_ge(*pt_ev.at(n + 1))
                    if h == 0 and b >= 2:
                        pe.wait_ge(*o_ev.at(b - 1))
                    nk = (hi - lo) // P
                    for k in range(nk):
                        last = pe.matmul(p.psum[:, 6 + b % 2, h * VD:(h + 1) * VD], probT[:, n % 2, k * P:(k + 1) * P],
                                         vt[:, lo // P + k, h * VD:(h + 1) * VD], start=(k == 0), stop=(k == nk - 1))
                    last.then_inc(*o_ps.up())
                scores(0)
                for n in range(len(items)):
                    if n + 1 < len(items):
                        scores(n + 1)
                    if n >= 1:
                        outputs(n - 1)
                    turn_probs(n)
                outputs(len(items) - 1)

            @block.vector
            def _(dve):
                link = chained(dve_c)

                def rotate(u, b, n):
                    def quarters(ap):
                        return ap.rearrange("p n (a s r) -> p (n a) s r", a=2, s=2) if n == 1 else \
                            ap.rearrange("p n (a s r) -> p n a s r", a=2, s=2)
                    c, s = insert_dim(cos[:, b], 1, n), insert_dim(sin[:, b], 1, n)
                    link(dve, dve.tensor_tensor(ra[:, 0:n], u, c, ALU.mult))
                    for side in range(2):
                        for a in range(2):
                            dst = slice(16 * a + 8 * side, 16 * a + 8 * side + 8)
                            src = slice(16 * a + 8 * (1 - side), 16 * a + 8 * (1 - side) + 8)
                            last = dve.tensor_tensor(rb[:, 0:n, dst], u[:, :, src], s[:, :, dst], ALU.mult)
                    link(dve, last)
                    return dve.tensor_tensor(u, ra[:, 0:n], rb[:, 0:n], ALU.add)
                dve.wait_ge(*sq.at(2 * TB))
                dve.tensor_scalar(stat[:, 0], stat[:, 0], 1.0 / QR, EPS, ALU.mult, ALU.add)
                dve.tensor_scalar(stat[:, 1], stat[:, 1], 1.0 / KVR, EPS, ALU.mult, ALU.add).then_inc(*mean.up())
                dve.wait_ge(*root.at(1))
                dve.reciprocal(rstd[:], rstd[:]).then_inc(*rs.up())
                dve.wait_ge(*rs.at(1))
                dve.wait_ge(*gains_in.at(64))
                for b in range(TB):
                    dve.scalar_tensor_tensor(out=ck[:, b], in0=ck[:, b], scalar=rstd[:, 1, b:b + 1], in1=kvrow[:],
                                             op0=ALU.mult, op1=ALU.mult)
                    dve.tensor_scalar(cq[:, b], cq[:, b], rstd[:, 0, b:b + 1], None, ALU.mult).then_inc(*kvn.up())
                dve.wait_ge(*zeroed.at(1))
                for b in range(LB):
                    link(dve, dve.tensor_copy(krt[:, 1 + b, NOPE:QD], kr[:, b]))
                    link(dve, rotate(krt[:, 1 + b:2 + b, NOPE:QD], b, 1))
                dve.tensor_copy(krt[:, 1 + LB, NOPE:QD], kr[:, LB]).then_inc(*krt_ready.up())
                for n, (kind, b) in enumerate(turns):
                    dve.wait_ge(*lat_tr.at(n + 1))
                    last = dve.tensor_copy(ckvT[:, :, n * P:(n + 1) * P],
                                           p.psum[:, 2 * (n % 4), 0:KVR].rearrange("p (k c) -> p k c", k=VF))
                    if kind == "tok":
                        for k in range(QF):
                            last = dve.tensor_scalar(cqT[:, k, b * P:(b + 1) * P],
                                                     p.psum[:, 2 * (n % 4) + 1, k * P:(k + 1) * P],
                                                     gq[:, k:k + 1], None, ALU.mult)
                    last.then_inc(*lat_ev.up())

                def take_turned(b):
                    dve.wait_ge(*tr_ps.at(b + 1))
                    dve.tensor_copy(qT[0:QD, :, b * P:(b + 1) * P].rearrange("p (a h) c -> p a h c", a=2),
                                    p.psum[0:QD, 4 + 2 * (b % 2):6 + 2 * (b % 2)].rearrange(
                                        "p a (h c) -> p a h c", h=4)).then_inc(*tr_ev.up())
                for b in range(TB):
                    dve.wait_ge(*gm_ps.at(b + 1))
                    if b >= 2:
                        dve.wait_ge(*tr_ps.at(b - 1))
                    dve.tensor_copy(qtok[:, b % 2, 0:512], p.psum[:, 2 * (b % 2)])
                    dve.tensor_copy(qtok[:, b % 2, 512:NH * QD],
                                    p.psum[:, 2 * (b % 2) + 1, 0:NH * QD - 512]).then_inc(*gm_ev.up())
                    dve.wait_ge(*gm_ev.at(b + 1))
                    if b < LB:
                        rotate(qtok[:, b % 2].rearrange("p (h c) -> p h c", h=NH)[:, :, NOPE:QD], b,
                               NH).then_inc(*qt_ready.up())
                    else:
                        dve.engine_nop().then_inc(*qt_ready.up())
                    if b >= 1:
                        take_turned(b - 1)
                take_turned(TB - 1)
                for h in range(NH):
                    dve.wait_ge(*gm_ps.at(TB + h + 1))
                    dve.tensor_copy(kT[0:NOPE, h].rearrange("p (a k) -> p a k", a=2),
                                    p.psum[0:NOPE, 2 * (h % 2):2 * (h % 2) + 2, 0:KEYS // 2]).then_inc(*gm_ev.up())
                for n in range(KB):
                    dve.wait_ge(*gm_ps.at(TB + NH + n + 1))
                    dve.tensor_copy(vt[:, n], p.psum[:, 2 * (n % 2)]).then_inc(*gm_ev.up())
                dve.wait_ge(*tr_ps.at(TB + 1))
                for part in range(2):
                    last = dve.tensor_copy(kT[NOPE:QD, :, part * 3 * P:(part + 1) * 3 * P],
                                           insert_dim(p.psum[NOPE:QD, 4 + part, 0:3 * P], 1, NH))
                last.then_inc(*tr_ev.up())

                def largest(n):
                    b, h = items[n]
                    lo, hi = keys_of(b)
                    w = (hi - lo) // 2
                    dve.wait_ge(*sc_ps.at(n + 1))
                    m = mx[:, n % (2 * NH)]
                    link(dve, dve.tensor_reduce(m[:, 0:1], p.psum[:, 2 * (n % 2):2 * (n % 2) + 2, 0:w],
                                                mybir.AxisListType.XY, ALU.max))
                    dve.tensor_scalar(m[:, 1:2], m[:, 0:1], -SCALE, None, ALU.mult).then_inc(*mx_ready.up())

                def take_block(b):
                    dve.wait_ge(*o_ps.at(NH * (b + 1)))
                    link(dve, dve.reciprocal(total[:, b % 2], total[:, b % 2]))
                    dve.tensor_tensor(o[:, b].rearrange("p (h c) -> p h c", h=NH),
                                      p.psum[:, 6 + b % 2].rearrange("p (h c) -> p h c", h=NH),
                                      total[:, b % 2].to_broadcast([P, NH, VD]), ALU.mult).then_inc(*o_ev.up())
                largest(0)
                for n, (b, h) in enumerate(items):
                    if n + 1 < len(items):
                        largest(n + 1)
                    lo, hi = keys_of(b)
                    dve.wait_ge(*pt_ps.at(n + 1))
                    if n >= 2:
                        dve.wait_ge(*o_ps.at(n - 1))
                    nk = (hi - lo) // P
                    first = min(nk, 4) * P
                    last = dve.tensor_copy(probT[:, n % 2, 0:first], p.psum[:, 4, 0:first])
                    if nk > 4:
                        last = dve.tensor_copy(probT[:, n % 2, first:nk * P], p.psum[:, 5, 0:nk * P - first])
                    last.then_inc(*pt_ev.up())
                    if h == 1 and b >= 1:
                        take_block(b - 1)
                take_block(TB - 1)
    p.close_stage()


def residual_tail(p, l, which, own, block_parts):
    raise NotImplementedError


def gate_rows(p, pe, which, gr_ps, gr_ev, first_bank=0):
    for s in range(2):
        if s >= 1:
            pass
        for k in range(KD):
            last = pe.matmul(p.psum[:, first_bank + 2 * s + k // 4, (k % 4) * P:(k % 4 + 1) * P],
                             p.gate_out[:, which, k, s:s + 1].to_broadcast([P, P]), p.ident[:], start=True, stop=True)
    last.then_inc(*gr_ps.up())


def stage_out_proj(p, l, t):
    nc, io = p.nc, p.io
    w_in, small = p.sig("wo_in"), p.sig("wo_small")
    sq, mean, root, rs, yn, tr, ev = (p.sig(n) for n in (
        "pn_squares", "pn_mean", "pn_root", "pn_rstd", "pn_scaled", "pn_turned", "pn_evicted"))
    gr_ps, gr_ev, mm, sq2, m2, r2, res = (p.sig(n) for n in (
        "gate_ps", "gate_out", "out_ps", "out_squares", "out_mean", "out_root", "residual"))
    dve_c = p.sig("dve_chain")
    with ExitStack() as own:
        def sb(name, shape):
            return p.sb(f"op_{name}{l}", shape, ctx=own)
        w = sb("w", [P, KD, D])
        gain = sb("gain", [P, KD])
        junk = sb("junk", [P, D])
        stat, rstd = sb("stat", [P, TB, 2]), sb("rstd", [P, TB, 2])
        stat2, rstd2 = sb("stat2", [P, TB, 2]), sb("rstd2", [P, TB])
        yT = sb("yT", [P, KD, T])
        rows = sb("rows", [P, 2, D])
        upd = sb("upd", [P, 2, D])
        parts = (t["y_ssd"], t["o"])
        with nc.Block() as block:
            @block.sync
            def _(sp):
                for half in range(2):
                    sp.dma_start(w[:, :, half * 512:(half + 1) * 512], io["w_out"][l, :, half * 512:(half + 1) * 512].rearrange(
                        "(k p) f -> p k f", p=P)).then_inc(*w_in.up(16))
                with nc.allow_non_contiguous_dma(reason="one gain per partition"):
                    sp.dma_start(gain[:, 0:4], io["ssd_norm"][l].rearrange("(k p) -> p k", p=P)).then_inc(*small.up(16))
                    sp.dma_start(gain[:, 4:8], io["mla_norm"][l].rearrange("(k p) -> p k", p=P)).then_inc(*small.up(16))

            @block.scalar
            def _(act):
                n = 0
                for b in range(TB):
                    for j, part in enumerate(parts):
                        act.activation(junk[:, 0:512], part[:, b], ACT.Square, accum_out=stat[:, b, j:j + 1]).then_inc(*sq.up())
                        n += 1
                        act.wait_ge(*sq.at(n))
                act.wait_ge(*mean.at(1))
                act.activation(rstd[:], stat[:], ACT.Sqrt).then_inc(*root.up())
                for b in range(TB):
                    act.wait_ge(*rs.at(1))
                    for j, part in enumerate(parts):
                        last = act.activation(part[:, b], part[:, b], ACT.Copy, scale=rstd[:, b, j:j + 1])
                    last.then_inc(*yn.up())
                for b in range(TB):
                    act.wait_ge(*mm.at(b + 1))
                    for half in range(2):
                        act.activation(junk[:, 0:512], p.psum[:, 4 + 2 * (b % 2) + half], ACT.Square,
                                       accum_out=stat2[:, b, half:half + 1]).then_inc(*sq2.up())
                        act.wait_ge(*sq2.at(2 * b + half + 1))
                    act.wait_ge(*m2.at(b + 1))
                    act.activation(rstd2[:, b:b + 1], stat2[:, b, 0:1], ACT.Sqrt).then_inc(*r2.up())

            @block.tensor
            def _(pe):
                gate_rows(p, pe, 0, gr_ps, gr_ev)
                pe.wait_ge(*gr_ev.at(1))
                for b in range(TB):
                    pe.wait_ge(*yn.at(b + 1))
                    if b >= 2:
                        pe.wait_ge(*ev.at(b - 1))
                    for k in range(KD):
                        part = parts[k // 4]
                        last = pe.transpose(p.psum[:, 2 * (b % 2) + k // 4, (k % 4) * P:(k % 4 + 1) * P],
                                            part[:, b, (k % 4) * P:(k % 4 + 1) * P], p.ident[:])
                    last.then_inc(*tr.up())
                    if b == 1:
                        pe.wait_ge(*w_in.at(32))
                for b in range(TB):
                    pe.wait_ge(*ev.at(b + 1))
                    pe.wait_ge(*w_in.at(32))
                    if b >= 2:
                        pe.wait_ge(*res.at(b - 1))
                    for half in range(2):
                        for k in range(KD):
                            last = pe.matmul(p.psum[:, 4 + 2 * (b % 2) + half], yT[:, k, b * P:(b + 1) * P],
                                             w[:, k, half * 512:(half + 1) * 512], start=(k == 0), stop=(k == KD - 1))
                    last.then_inc(*mm.up())

            @block.vector
            def _(dve):
                link = chained(dve_c)
                dve.wait_ge(*gr_ps.at(1))
                dve.tensor_copy(rows[:].rearrange("p s (a c) -> p (s a) c", a=2), p.psum[:, 0:4]).then_inc(*gr_ev.up())
                dve.wait_ge(*sq.at(2 * TB))
                dve.tensor_scalar(stat[:], stat[:], 1.0 / 512, EPS, ALU.mult, ALU.add).then_inc(*mean.up())
                dve.wait_ge(*root.at(1))
                dve.reciprocal(rstd[:], rstd[:]).then_inc(*rs.up())
                dve.wait_ge(*small.at(32))
                for b in range(TB):
                    dve.wait_ge(*tr.at(b + 1))
                    for k in range(KD):
                        last = dve.tensor_scalar(yT[:, k, b * P:(b + 1) * P],
                                                 p.psum[:, 2 * (b % 2) + k // 4, (k % 4) * P:(k % 4 + 1) * P],
                                                 gain[:, k:k + 1], None, ALU.mult)
                    last.then_inc(*ev.up())
                for b in range(TB):
                    take_residual(p, dve, link, b, p.psum[:, 4 + 2 * (b % 2):6 + 2 * (b % 2)], rows, upd,
                                  stat2, rstd2, sq2, m2, r2, res)
    p.close_stage()


def take_residual(p, dve, link, b, src, rows, upd, stat2, rstd2, sq2, m2, r2, res):
    s = SEQ_OF[b]
    dve.wait_ge(*sq2.at(2 * b + 2))
    link(dve, dve.tensor_tensor(stat2[:, b, 0:1], stat2[:, b, 0:1], stat2[:, b, 1:2], ALU.add))
    dve.tensor_scalar(stat2[:, b, 0:1], stat2[:, b, 0:1], 1.0 / D, EPS, ALU.mult, ALU.add).then_inc(*m2.up())
    dve.wait_ge(*r2.at(b + 1))
    link(dve, dve.reciprocal(rstd2[:, b:b + 1], rstd2[:, b:b + 1]))
    link(dve, dve.scalar_tensor_tensor(
        out=upd[:, b % 2].rearrange("p (a c) -> p a c", a=2), in0=src, scalar=rstd2[:, b:b + 1],
        in1=rows[:, s].rearrange("p (a c) -> p a c", a=2), op0=ALU.mult, op1=ALU.mult))
    dve.tensor_tensor(p.x[:, b], p.x[:, b], upd[:, b % 2], ALU.add).then_inc(*res.up())


def stage_router(p, l, hi, lo, comb_dram):
    nc, io = p.nc, p.io
    r_in, lg_ps, best, e2_done, made, turned, rows_out, stored, iota_done = (p.sig(n) for n in (
        "router_in", "router_ps", "router_best", "router_exp", "router_made", "router_turned", "router_rows",
        "router_stored", "router_iota"))
    dve_c = p.sig("dve_chain")
    with ExitStack() as own:
        def sb(name, shape, dt=F32):
            return p.sb(f"rt_{name}{l}", shape, dt, ctx=own)
        wr = sb("wr", [P, KD, NE])
        lg, top = sb("lg", [P, TB, NE]), sb("top", [P, TB, 8])
        idx, idf = sb("idx", [P, TB, 8], U32), sb("idf", [P, TB, 8])
        iota = sb("iota", [P, NE])
        diff, e2, w1, w2 = (sb(n, [P, TB]) for n in ("diff", "e2", "w1", "w2"))
        hit = sb("hit", [P, 2, TB, NE])
        rows = sb("rows", [NE, T])
        with nc.Block() as block:
            @block.sync
            def _(sp):
                sp.dma_start(wr[:], io["moe_router"][0].rearrange("(k p) e -> p k e", p=P)).then_inc(*r_in.up(16))
                sp.wait_ge(*rows_out.at(1))
                sp.dma_start(comb_dram, rows[:]).then_inc(*stored.up(16))
                sp.wait_ge(*stored.at(16))

            @block.gpsimd
            def _(pool):
                pool.iota(iota[:], pattern=[[1, NE]], base=0, channel_multiplier=0,
                          allow_small_or_imprecise_dtypes=True).then_inc(*iota_done.up())

            @block.tensor
            def _(pe):
                pe.wait_ge(*r_in.at(16))
                for b in range(TB):
                    for k in range(KD):
                        for n, part in enumerate((hi, lo)):
                            last = pe.matmul(p.psum[:, 0, b * NE:(b + 1) * NE],
                                             part[:, k, b * P:(b + 1) * P].bitcast(F32), wr[:, k, :],
                                             start=(k == 0 and n == 0), stop=(k == KD - 1 and n == 1))
                last.then_inc(*lg_ps.up())
                pe.wait_ge(*made.at(1))
                for b in range(TB):
                    last = pe.transpose(p.psum[0:NE, 1 + b // 4, (b % 4) * P:(b % 4 + 1) * P], hit[:, 0, b, :], p.ident[:])
                last.then_inc(*turned.up())

            @block.scalar
            def _(act):
                act.wait_ge(*best.at(1))
                act.activation(e2[:], diff[:], ACT.Exp).then_inc(*e2_done.up())

            @block.vector
            def _(dve):
                link = chained(dve_c)
                dve.wait_ge(*lg_ps.at(1))
                link(dve, dve.tensor_copy(lg[:], p.psum[:, 0, 0:TB * NE].rearrange("p (b e) -> p b e", b=TB)))
                for b in range(TB):
                    link(dve, dve.max(top[:, b], lg[:, b]))
                    link(dve, dve.max_index(idx[:, b], top[:, b], lg[:, b]))
                link(dve, dve.tensor_copy(idf[:], idx[:]))
                dve.tensor_tensor(diff[:], top[:, :, 1], top[:, :, 0], ALU.subtract).then_inc(*best.up())
                dve.wait_ge(*e2_done.at(1))
                link(dve, dve.tensor_scalar(w1[:], e2[:], 1.0, None, ALU.add))
                link(dve, dve.reciprocal(w1[:], w1[:]))
                link(dve, dve.tensor_tensor(w2[:], e2[:], w1[:], ALU.mult))
                dve.wait_ge(*iota_done.at(1))
                for n, w in enumerate((w1, w2)):
                    link(dve, dve.tensor_tensor(hit[:, n], insert_dim(iota[:], 1, TB),
                                                idf[:, :, n].to_broadcast([P, TB, NE]), ALU.is_equal))
                    link(dve, dve.tensor_tensor(hit[:, n], hit[:, n], w[:].to_broadcast([P, TB, NE]), ALU.mult))
                dve.tensor_tensor(hit[:, 0], hit[:, 0], hit[:, 1], ALU.add).then_inc(*made.up())
                dve.wait_ge(*turned.at(1))
                link(dve, dve.tensor_copy(rows[:, 0:512], p.psum[0:NE, 1]))
                dve.tensor_copy(rows[:, 512:T], p.psum[0:NE, 2, 0:T - 512]).then_inc(*rows_out.up())
    p.close_stage()


G_PIECES = 2 * FT
PIECES = G_PIECES + KD
SLOT = [i % 4 for i in range(G_PIECES)] + [2, 3, 0, 1, 2, 3, 2, 3]
PAIR = [i % 4 for i in range(G_PIECES)] + [2, 3, 0, 1, 2, 3, 2, 3]


def last_user(table, i):
    for j in range(i - 1, i - 1 - PIECES, -1):
        if table[j % PIECES] == table[i]:
            return j


def stage_experts(p, l, hi, lo, acc, comb_dram):
    nc, io = p.nc, p.io
    moe = comb_dram is not None
    n_exp = NE if moe else 2
    sem = lambda name: p.ctx.enter_context(nc.semaphore(f"{name}{l}"))
    raw_in = [sem(f"ex_raw_in{r}") for r in range(2)]
    hi_done, lo_done, piece_done, taken = sem("ex_hi_done"), sem("ex_lo_done"), sem("ex_piece_done"), sem("ex_taken")
    gate_act, hid_ready, comb_in, chain, zeroed = sem("ex_gate_act"), sem("ex_hid"), sem("ex_comb"), sem("ex_dve"), sem("ex_zero")
    n_link = FT * (3 if moe else 2)
    with ExitStack() as own:
        def sb(name, shape, dt=F32):
            return p.sb(f"ex_{name}{l}", shape, dt, ctx=own)
        raw = sb("raw", [P, 2, FE])
        wh, wl = sb("wh", [P, 4, FE], F32R), sb("wl", [P, 4, FE], F32R)
        hh, hl = sb("hh", [P, FT, T], F32R), sb("hl", [P, FT, T], F32R)
        sg, hf = sb("sg", [P, T]), sb("hf", [P, T])
        ce = sb("ce", [P, T]) if moe else None

        def size(i):
            return D if i < G_PIECES else FE

        def source(e, i):
            if i < G_PIECES:
                name, f = ("gate", "up")[i % 2], i // 2
                if moe:
                    return io[f"moe_w_{name}"][0, bass.ds(e, 1), :, f * P:(f + 1) * P].rearrange("o (k p) c -> p (o k) c", p=P)
                return io[f"ffn_w_{name}"][0, :, bass.ds(e * FE + f * P, P)].rearrange("(k p) c -> p k c", p=P)
            m = i - G_PIECES
            if moe:
                return io["moe_w_down"][0, bass.ds(e, 1), :, m * P:(m + 1) * P].rearrange("o (k p) c -> p (o k) c", p=P)
            return io["ffn_w_down"][0, bass.ds(e * FE, FE), m * P:(m + 1) * P].rearrange("(k p) c -> p k c", p=P)

        with nc.Block() as block:
            @block.sync
            def _(sp):
                with sp.Fori(0, n_exp) as e:
                    for i in range(PIECES):
                        if moe and i == 1:
                            sp.wait_ge(taken, (e + 1) * PIECES)
                            sp.dma_start(ce[:], comb_dram[bass.ds(e, 1)].rearrange("o t -> (o t)").partition_broadcast(P)
                                         ).then_inc(comb_in, 16)
                        sp.wait_ge(lo_done, (e + 1) * PIECES + i - 1)
                        sp.dma_start(raw[:, i % 2, 0:size(i)].rearrange("p (k c) -> p k c", c=P),
                                     source(e, i)).then_inc(raw_in[i % 2], 16)

            @block.scalar
            def _(act):
                with act.Fori(0, n_exp) as e:
                    for i in range(PIECES):
                        act.wait_ge(raw_in[i % 2], e * (8 * PIECES) + 16 * (i // 2 + 1))
                        act.wait_ge(piece_done, (e + 1) * PIECES + last_user(SLOT, i) + 1)
                        act.activation(wh[:, SLOT[i], 0:size(i)], raw[:, i % 2, 0:size(i)], ACT.Copy).then_inc(hi_done, 1)
                        f = (i - 3) // 2
                        if i % 2 == 1 and 0 <= f < FT:
                            act.wait_ge(piece_done, (e + 1) * PIECES + 2 * f + 1)

                            act.wait_ge(taken, (e + 1) * PIECES + 2 * f)
                            act.activation(sg[:].rearrange("p (a c) -> p a c", a=2),
                                           p.psum[:, 2 * PAIR[2 * f]:2 * PAIR[2 * f] + 2, 0:HT],
                                           ACT.Silu).then_inc(gate_act, 1)

            @block.gpsimd
            def _(pool):
                with pool.Fori(0, n_exp) as e:
                    for i in range(PIECES):
                        pool.wait_ge(hi_done, e * PIECES + i + 1)
                        ins = pool.tensor_tensor(wl[:, SLOT[i], 0:size(i)], raw[:, i % 2, 0:size(i)],
                                                 wh[:, SLOT[i], 0:size(i)].bitcast(F32), ALU.subtract)
                        ins.then_inc(lo_done, 1)

            @block.tensor
            def _(pe):
                pe.wait_ge(zeroed, 1)
                with pe.Fori(0, n_exp) as e:
                    for i in range(PIECES):
                        pe.wait_ge(lo_done, (e + 1) * PIECES + i + 1)
                        pe.wait_ge(taken, (e + 1) * PIECES + last_user(PAIR, i) + 1)
                        if i == G_PIECES:
                            pe.wait_ge(hid_ready, (e + 1) * FT)
                        steps = KD if i < G_PIECES else FT
                        mh, ml = (hi, lo) if i < G_PIECES else (hh, hl)
                        for k in range(steps):
                            cols = slice(k * P, (k + 1) * P)
                            for n, (w, m) in enumerate(((wh, mh), (wh, ml), (wl, mh))):
                                for half in range(2):
                                    last = pe.matmul(p.psum[:, 2 * PAIR[i] + half, 0:HT], w[:, SLOT[i], cols],
                                                     m[:, k, half * HT:(half + 1) * HT],
                                                     start=(k == 0 and n == 0), stop=(k == steps - 1 and n == 2))
                        last.then_inc(piece_done, 1)

            @block.vector
            def _(dve):
                dve.memset(acc[:], 0.0).then_inc(zeroed, 1)
                dve.wait_ge(zeroed, 1)
                dve.memset(sg[:, 0:1], 0.0).then_inc(lo_done, PIECES)
                dve.memset(sg[:, 1:2], 0.0).then_inc(piece_done, PIECES)
                dve.memset(sg[:, 2:3], 0.0).then_inc(taken, PIECES)
                with dve.Fori(0, n_exp) as e:
                    links = 0

                    def link(ins):
                        nonlocal links
                        links += 1
                        ins.then_inc(chain, 1)
                        dve.wait_ge(chain, e * n_link + links)
                    if moe:
                        dve.wait_ge(comb_in, (e + 1) * 16)
                    for i in range(PIECES):
                        if i < G_PIECES and i % 2 == 0:
                            continue
                        dve.wait_ge(piece_done, (e + 1) * PIECES + i + 1)
                        halves = p.psum[:, 2 * PAIR[i]:2 * PAIR[i] + 2, 0:HT]
                        if i < G_PIECES:
                            f = i // 2
                            dve.wait_ge(gate_act, e * FT + f + 1)
                            ins = dve.tensor_tensor(hf[:].rearrange("p (a c) -> p a c", a=2), halves,
                                                    sg[:].rearrange("p (a c) -> p a c", a=2), ALU.mult)
                            link(ins)
                            if moe:
                                link(dve.tensor_tensor(hf[:], hf[:], ce[:], ALU.mult))
                            link(dve.tensor_copy(hh[:, f], hf[:]))
                            dve.tensor_tensor(hl[:, f], hf[:], hh[:, f].bitcast(F32), ALU.subtract).then_inc(hid_ready, 1)
                            dve.wait_ge(hid_ready, e * FT + f + 1)
                            dve.engine_nop().then_inc(taken, 2)
                        else:
                            m = acc[:, i - G_PIECES].rearrange("p (a c) -> p a c", a=2)
                            dve.tensor_tensor(m, m, halves, ALU.add).then_inc(taken, 1)
    p.close_stage()


def stage_ffn_out(p, l, acc):
    nc, io = p.nc, p.io
    gr_ps, gr_ev, mm, sq2, m2, r2, res = (p.sig(n) for n in (
        "gate_ps", "gate_out", "out_ps", "out_squares", "out_mean", "out_root", "residual"))
    dve_c = p.sig("dve_chain")
    with ExitStack() as own:
        def sb(name, shape):
            return p.sb(f"fo_{name}{l}", shape, ctx=own)
        junk, rows, upd = sb("junk", [P, 512]), sb("rows", [P, 2, D]), sb("upd", [P, 2, D])
        stat2, rstd2 = sb("stat2", [P, TB, 2]), sb("rstd2", [P, TB])
        with nc.Block() as block:
            @block.scalar
            def _(act):
                for b in range(TB):
                    act.wait_ge(*mm.at(b + 1))
                    for half in range(2):
                        act.activation(junk[:], p.psum[:, 4 + 2 * (b % 2) + half], ACT.Square,
                                       accum_out=stat2[:, b, half:half + 1]).then_inc(*sq2.up())
                        act.wait_ge(*sq2.at(2 * b + half + 1))
                    act.wait_ge(*m2.at(b + 1))
                    act.activation(rstd2[:, b:b + 1], stat2[:, b, 0:1], ACT.Sqrt).then_inc(*r2.up())

            @block.tensor
            def _(pe):
                gate_rows(p, pe, 1, gr_ps, gr_ev)
                for b in range(TB):
                    if b >= 2:
                        pe.wait_ge(*res.at(b - 1))
                    for k in range(KD):
                        last = pe.transpose(p.psum[:, 4 + 2 * (b % 2) + k // 4, (k % 4) * P:(k % 4 + 1) * P],
                                            acc[:, k, b * P:(b + 1) * P], p.ident[:])
                    last.then_inc(*mm.up())

            @block.vector
            def _(dve):
                link = chained(dve_c)
                dve.wait_ge(*gr_ps.at(1))
                link(dve, dve.tensor_copy(rows[:].rearrange("p s (a c) -> p (s a) c", a=2), p.psum[:, 0:4]))
                for b in range(TB):
                    take_residual(p, dve, link, b, p.psum[:, 4 + 2 * (b % 2):6 + 2 * (b % 2)], rows, upd,
                                  stat2, rstd2, sq2, m2, r2, res)
    p.close_stage()


def stage_store(p):
    nc, io = p.nc, p.io
    out = p.sig("y_stored")
    with nc.Block() as block:
        @block.sync
        def _(sp):
            sp.dma_start(io["y_sample"].rearrange("o (b p) d -> p (o b) d", p=P), p.x[:, 0:LB]).then_inc(*out.up(16))
            sp.dma_start(io["y_prompt"].rearrange("o p d -> p (o d)"), p.x[:, LB]).then_inc(*out.up(16))
            sp.wait_ge(*out.at(32))
    p.close_stage()


DBG = None


def build(nc, io):
    with ExitStack() as ctx:
        p = Program(nc, io, ctx)
        comb_dram = nc.dram_tensor("combine", (NE, T), F32, kind="Internal").ap()
        stage_setup(p)
        for l in range(2):
            stage_modulation(p, l)
            with ExitStack() as mixer:
                def sb(name, shape, where=mixer):
                    return p.sb(f"mx_{name}{l}", shape, ctx=where)
                t = {"z": sb("z", [P, TB, SSDW]), "dtcq": sb("dtcq", [P, TB, 2 * NH + QR]),
                     "ckr": sb("ckr", [P, TB, KVR + ROPE]), "pad": sb("pad", [P, XF, PADW]),
                     "xst": sb("xst", [P, TB, SSDW]), "qkv_room": sb("qkv_room", [P, NH * KEYS])}
                t["y_ssd"] = t["z"]
                t["o"] = t["xst"]
                with ExitStack() as inner:
                    hT = p.sb(f"hT{l}", [P, KD, T], ctx=inner)
                    stage_pre_norm(p, l, 0, hT)
                    stage_in_proj(p, l, hT, t)
                stage_ssd(p, l, t)
                stage_attention(p, l, t)
                stage_out_proj(p, l, t)
            with ExitStack() as ffn:
                acc = p.sb(f"acc{l}", [P, KD, T], ctx=ffn)
                with ExitStack() as inner:
                    hi = p.sb(f"h_hi{l}", [P, KD, T], F32R, ctx=inner)
                    lo = p.sb(f"h_lo{l}", [P, KD, T], F32R, ctx=inner)
                    stage_pre_norm(p, l, 1, None, (hi, lo))
                    if l == 1:
                        stage_router(p, l, hi, lo, comb_dram)
                    stage_experts(p, l, hi, lo, acc, comb_dram if l == 1 else None)
                stage_ffn_out(p, l, acc)
        stage_store(p)


def rope_tables():
    import numpy as np
    rows = LAT // 64
    row = np.repeat(np.arange(rows, dtype=np.float32), 64)
    col = np.tile(np.arange(64, dtype=np.float32), rows)
    half = ROPE // 2
    inv = (np.float32(10000.0) ** (-np.arange(0, half, 2, dtype=np.float32) / half)).astype(np.float32)
    ar, ac = row[:, None] * inv[None, :], col[:, None] * inv[None, :]
    ang = np.concatenate([ar, ar, ac, ac], axis=-1).astype(np.float32)
    sign = np.repeat(np.array([-1, 1, -1, 1], np.float32), half // 2)
    return np.cos(ang).astype(np.float32), (np.sin(ang) * sign).astype(np.float32)


_OUTS = {"y_prompt": (1, CTX, D), "y_sample": (1, LAT, D), "new_ckv": (1, 2, CTX, KVR),
         "new_krope": (1, 2, CTX, ROPE), "new_ssm": (1, 2, 2, NH, HD, NS)}


def kernel(**inputs):
    import numpy as np
    import concourse.bacc as _bacc
    from concourse.bass_utils import run_bass_kernel_spmd as _run

    nc = _bacc.Bacc("TRN2", target_bir_lowering=False, num_devices=1)
    arrays = {k: np.ascontiguousarray(v) for k, v in inputs.items()}
    arrays["rope_cos"], arrays["rope_sin"] = rope_tables()
    io = {}
    for name, a in arrays.items():
        io[name] = nc.dram_tensor(name, a.shape, mybir.dt.from_np(a.dtype), kind="ExternalInput").ap()
    for name, shape in _OUTS.items():
        io[name] = nc.dram_tensor(f"out_{name}", shape, F32, kind="ExternalOutput").ap()
    build(nc, io)
    r = _run(nc, [arrays], core_ids=[0])
    return tuple(r.results[0][f"out_{name}"] for name in _OUTS)
```

```python
from contextlib import ExitStack

import concourse.bass as bass
from concourse import mybir

F32 = mybir.dt.float32
F32R = mybir.dt.float32r
U32 = mybir.dt.uint32
ALU = mybir.AluOpType
ACT = mybir.ActivationFunctionType
AX_X = mybir.AxisListType.X

P = 128
D = 1024
KD = D // P
LAT = 512
CTX = 128
T = LAT + CTX
TB = T // P
LB = LAT // P
HT = T // 2
SEQ_OF = [0] * LB + [1]
SSDW, NH, HD, NG, NS = 512, 8, 64, 2, 64
XBC = SSDW + 2 * NG * NS
XF = XBC // P
TAPS = 5
PADW = 2 + LAT + 2 + 2 + CTX + 2
QR, KVR, ROPE, NOPE, VD = 384, 256, 32, 64, 64
QD = NOPE + ROPE
PAST = 128
KEYS = PAST + T
KB = KEYS // P
C_DT = SSDW + XBC
C_CQ = C_DT + 2 * NH
C_KV = C_CQ + QR
C_KR = C_KV + KVR
IN_COLS = C_KR + ROPE
NMOD = 6
FE = 1408
FT = FE // P
NE = 8
EPS = 1e-6
SCALE = float(QD) ** -0.5
FAR = -1e30


class Signal:

    def __init__(self, nc, ctx, name):
        self.sem = ctx.enter_context(nc.semaphore(name))
        self.base = 0
        self.sent = 0

    def up(self, n=1):
        self.sent += n
        return self.sem, n

    def at(self, n):
        return self.sem, self.base + n

    def close(self):
        self.base, self.sent = self.base + self.sent, 0


def insert_dim(ap, at, n):
    dims = [list(d) for d in ap.ap]
    dims.insert(at, [0, n])
    return bass.AP(tensor=ap.tensor, offset=ap.offset, ap=dims)


class Program:
    def __init__(self, nc, io, ctx):
        self.nc, self.io, self.ctx = nc, io, ctx
        self.signals = {}
        self.stage_no = 0
        sb = self.sb
        self.psum = ctx.enter_context(nc.psum_tensor("psum", [P, 8, 512], F32))
        self.x = sb("x", [P, TB, D])
        self.ident = sb("ident", [P, P])
        self.ones = sb("ones", [P, P])
        self.tri = sb("tri", [P, 2, P])
        self.far = sb("far", [P, 2, P])
        self.silu_c = sb("silu_c", [P, KD, 2])
        self.mod = sb("mod", [P, 2, NMOD * KD, 2])
        self.b_mod = sb("b_mod_t", [P, 2, NMOD * KD])
        self.gains = sb("gains", [P, 2, 4, KD])
        self.scale_in = sb("scale_in", [P, 2, 2, KD, 2])
        self.gate_out = sb("gate_out", [P, 2, 2, KD, 2])
        self.stat = sb("stat", [P, TB])
        self.rstd = sb("rstd", [P, TB])

    def sb(self, name, shape, dt=F32, ctx=None):
        return (ctx or self.ctx).enter_context(self.nc.sbuf_tensor(name, shape, dt))

    def sig(self, name):
        if name not in self.signals:
            self.signals[name] = Signal(self.nc, self.ctx, name)
        return self.signals[name]

    def close_stage(self):
        for s in self.signals.values():
            s.close()


def chained(signal):
    count = [0]

    def link(eng, ins):
        count[0] += 1
        ins.then_inc(*signal.up())
        eng.wait_ge(*signal.at(count[0]))
    return link


def stage_setup(p):
    nc, io = p.nc, p.io
    x_in, c_in = p.sig("x_in"), p.sig("c_in")
    consts, pool_chain, silu_done = p.sig("consts"), p.sig("pool_chain"), p.sig("silu_done")
    with nc.Block() as block:
        @block.sync
        def _(sp):
            with nc.allow_non_contiguous_dma(reason="2048 conditioning values, one per partition row"):
                sp.dma_start(p.silu_c[:, :, 0], io["c"].rearrange("o (k p) -> p (o k)", p=P)).then_inc(*c_in.up(16))
                sp.dma_start(p.silu_c[:, :, 1], io["c_ctx"].rearrange("(k p) -> p k", p=P)).then_inc(*c_in.up(16))
            sp.dma_start(p.x[:, 0:LB], io["x_sample"].rearrange("o (b p) d -> p (o b) d", p=P)).then_inc(*x_in.up(16))
            sp.dma_start(p.x[:, LB], io["x_prompt"].rearrange("o p d -> p (o d)")).then_inc(*x_in.up(16))

        @block.gpsimd
        def _(pool):
            link = chained(pool_chain)
            pool.memset(p.ident[:], 0.0)
            pool.memset(p.ones[:], 1.0)
            pool.memset(p.tri[:], 1.0)
            link(pool, pool.memset(p.far[:], 0.0))
            pool.affine_select(out=p.ident[:], in_=p.ident[:], compare_op=ALU.not_equal, fill=1.0, base=0,
                               pattern=[[-1, P]], channel_multiplier=1)
            for tile, fill in ((p.tri, 0.0), (p.far, FAR)):
                pool.affine_select(out=tile[:, 0], in_=tile[:, 0], compare_op=ALU.is_ge, fill=fill, base=0,
                                   pattern=[[1, P]], channel_multiplier=-1)
                last = pool.affine_select(out=tile[:, 1], in_=tile[:, 1], compare_op=ALU.is_ge, fill=fill, base=0,
                                          pattern=[[-1, P]], channel_multiplier=1)
            last.then_inc(*consts.up())

        @block.scalar
        def _(act):
            act.wait_ge(*c_in.at(32))
            act.activation(p.silu_c[:], p.silu_c[:], ACT.Silu).then_inc(*silu_done.up())
            act.wait_ge(*silu_done.at(1))
            act.wait_ge(*x_in.at(32))
    p.close_stage()


UNIT = 512
UNITS = NMOD * D // UNIT
HALF_K = KD // 2


class Modulation:

    def __init__(self, p, units, bank, own, tag):
        self.p, self.units, self.bank = p, units, bank
        self.w = p.sb(f"wmod_{tag}", [P, 2, HALF_K, UNIT], ctx=own)
        self.row = p.sb(f"modrow_{tag}", [2, UNIT], ctx=own)
        self.landed = [p.sig(f"wmod_landed{r}") for r in range(2)]
        self.used, self.row_out, self.turned, self.taken = (p.sig(n) for n in (
            "wmod_used", "mod_row_out", "mod_turned", "mod_taken"))
        self.steps = [(kind, n) for n in range(len(units)) for kind in "abt"]

    def load(self, sp):
        for i in range(2 * len(self.units)):
            l, u = self.units[i // 2]
            if i >= 2:
                sp.wait_ge(*self.used.at(i - 1))
            sp.dma_start(self.w[:, i % 2], self.p.io["w_mod"][l, (i % 2) * HALF_K * P:(i % 2 + 1) * HALF_K * P,
                                                              u * UNIT:(u + 1) * UNIT].rearrange(
                "(k p) f -> p k f", p=P)).then_inc(*self.landed[i % 2].up(16))

    def on_tensor(self, pe, step):
        p, (kind, n) = self.p, self.steps[step]
        if kind == "t":
            pe.wait_ge(*self.row_out.at(n + 1))
            for j in range(UNIT // P):
                last = pe.transpose(p.psum[:, self.bank, 2 * j:2 * j + 2], self.row[0:2, j * P:(j + 1) * P],
                                    p.ident[0:2, 0:2])
            last.then_inc(*self.turned.up())
            return
        half = "ab".index(kind)
        pe.wait_ge(*self.landed[half].at(16 * (n + 1)))
        if kind == "a" and n >= 1:
            pe.wait_ge(*self.taken.at(n))
        for k in range(HALF_K):
            last = pe.matmul(p.psum[0:2, self.bank, :], p.silu_c[:, half * HALF_K + k, :], self.w[:, half, k],
                             start=(half == 0 and k == 0), stop=(half == 1 and k == HALF_K - 1))
        last.then_inc(*self.used.up())

    def on_vector(self, dve, step):
        p, (kind, n) = self.p, self.steps[step]
        l, u = self.units[n]
        if kind == "b":
            dve.wait_ge(*self.used.at(2 * n + 2))
            dve.tensor_copy(self.row[:], p.psum[0:2, self.bank, :]).then_inc(*self.row_out.up())
        elif kind == "t":
            dve.wait_ge(*self.turned.at(n + 1))
            per = UNIT // P
            dve.tensor_tensor(p.mod[:, l, u * per:(u + 1) * per, :],
                              p.psum[:, self.bank, 0:2 * per].rearrange("p (m s) -> p m s", s=2),
                              p.b_mod[:, l, u * per:(u + 1) * per].to_broadcast([P, per, 2]),
                              ALU.add).then_inc(*self.taken.up())

    def vectors(self, dve, link, l, which, kinds):
        p = self.p
        dve.wait_ge(*self.taken.at(len(self.units)))
        if "scale" in kinds:
            scale = p.mod[:, l, (3 * which + 1) * KD:(3 * which + 2) * KD, :]
            link(dve, dve.scalar_tensor_tensor(
                out=p.scale_in[:, l, which], in0=scale, scalar=1.0,
                in1=p.gains[:, l, 2 * which].to_broadcast([P, KD, 2]), op0=ALU.add, op1=ALU.mult))
        if "gate" in kinds:
            gate = p.mod[:, l, (3 * which + 2) * KD:(3 * which + 3) * KD, :]
            link(dve, dve.tensor_tensor(p.gate_out[:, l, which], gate,
                                        p.gains[:, l, 2 * which + 1].to_broadcast([P, KD, 2]), ALU.mult))


def stage_first_modulation(p):
    nc, io = p.nc, p.io
    small, dve_c = p.sig("mod_small"), p.sig("dve_chain")
    with ExitStack() as own:
        mod = Modulation(p, [(0, u) for u in range(2 * D // UNIT)], 0, own, "first")
        with nc.Block() as block:
            @block.sync
            def _(sp):
                mod.load(sp)

            @block.scalar
            def _(act):
                with nc.allow_non_contiguous_dma(reason="bias and gains, feature-major"):
                    for l in range(2):
                        act.dma_start(p.b_mod[:, l], io["b_mod"][l].rearrange("(k p) -> p k", p=P)).then_inc(*small.up(16))
                        for j, name in enumerate(("norm_pre_mix", "norm_post_mix", "norm_pre_ffn", "norm_post_ffn")):
                            act.dma_start(p.gains[:, l, j], io[name][l].rearrange("(k p) -> p k", p=P)
                                          ).then_inc(*small.up(16))

            @block.tensor
            def _(pe):
                for step in range(len(mod.steps)):
                    mod.on_tensor(pe, step)

            @block.vector
            def _(dve):
                dve.wait_ge(*small.at(160))
                for step in range(len(mod.steps)):
                    mod.on_vector(dve, step)
                mod.vectors(dve, chained(dve_c), 0, 0, ("scale",))
    p.close_stage()


def stage_pre_norm(p, l, which, hT, split=None):
    nc = p.nc
    sq, mean, root, rs, xn, tr, ev = (p.sig(n) for n in (
        "pn_squares", "pn_mean", "pn_root", "pn_rstd", "pn_scaled", "pn_turned", "pn_evicted"))
    dve_c = p.sig("dve_chain")
    with ExitStack() as own:
        junk = p.sb(f"pn_junk{l}{which}", [P, D], ctx=own)
        xs = p.sb(f"pn_x{l}{which}", [P, 2, D], ctx=own)
        hf = p.sb(f"pn_h{l}{which}", [P, 2, KD, P], ctx=own) if split else None
        with nc.Block() as block:
            @block.scalar
            def _(act):
                for b in range(TB):
                    ins = act.activation(junk[:], p.x[:, b], ACT.Square, accum_out=p.stat[:, b:b + 1])
                    ins.then_inc(*sq.up())
                    act.wait_ge(*sq.at(b + 1))
                act.wait_ge(*mean.at(1))
                act.activation(p.rstd[:], p.stat[:], ACT.Sqrt).then_inc(*root.up())
                for b in range(TB):
                    act.wait_ge(*rs.at(1))
                    if b >= 2:
                        act.wait_ge(*tr.at(b - 1))
                    act.activation(xs[:, b % 2], p.x[:, b], ACT.Copy, scale=p.rstd[:, b:b + 1]).then_inc(*xn.up())

            @block.tensor
            def _(pe):
                for b in range(TB):
                    pe.wait_ge(*xn.at(b + 1))
                    if b >= 4:
                        pe.wait_ge(*ev.at(b - 3))
                    for k in range(KD):
                        last = pe.transpose(p.psum[:, 2 * (b % 4) + k // 4, (k % 4) * P:(k % 4 + 1) * P],
                                            xs[:, b % 2, k * P:(k + 1) * P], p.ident[:])
                    last.then_inc(*tr.up())

            @block.vector
            def _(dve):
                link = chained(dve_c)
                dve.wait_ge(*sq.at(TB))
                dve.tensor_scalar(p.stat[:], p.stat[:], 1.0 / D, EPS, ALU.mult, ALU.add).then_inc(*mean.up())
                dve.wait_ge(*root.at(1))
                dve.reciprocal(p.rstd[:], p.rstd[:]).then_inc(*rs.up())
                for b in range(TB):
                    s = SEQ_OF[b]
                    dve.wait_ge(*tr.at(b + 1))
                    for k in range(KD):
                        out = hf[:, b % 2, k] if split else hT[:, k, b * P:(b + 1) * P]
                        last = dve.tensor_scalar(
                            out, p.psum[:, 2 * (b % 4) + k // 4, (k % 4) * P:(k % 4 + 1) * P],
                            p.scale_in[:, l, which, k, s:s + 1], p.mod[:, l, 3 * which * KD + k, s:s + 1],
                            ALU.mult, ALU.add)
                    last.then_inc(*ev.up())
                    if split:
                        hi, lo = split
                        dve.wait_ge(*ev.at(b + 1))
                        link(dve, dve.tensor_copy(hi[:, :, b * P:(b + 1) * P], hf[:, b % 2]))
                        dve.tensor_tensor(lo[:, :, b * P:(b + 1) * P], hf[:, b % 2],
                                          hi[:, :, b * P:(b + 1) * P].bitcast(F32), ALU.subtract)
    p.close_stage()


def stage_in_proj(p, l, hT, t):
    nc, io = p.nc, p.io
    pieces = [(0, SSDW), (C_DT, C_KV), (C_KV, IN_COLS), (SSDW, SSDW + XBC // 2), (SSDW + XBC // 2, C_DT)]
    landed = [p.sig(f"win_landed{i}") for i in range(len(pieces))]
    mm, ev, pads = p.sig("win_ps"), p.sig("win_evicted"), p.sig("win_pads")
    token_out = [t["z"], t["dtcq"], t["ckr"]]
    with ExitStack() as own:
        w = p.sb(f"w_in{l}", [P, KD, IN_COLS], ctx=own)
        groups = [("tok", j, b) for j in range(3) for b in range(TB)] + \
                 [("feat", f, half) for f in range(XF) for half in range(2)]
        with nc.Block() as block:
            @block.sync
            def _(sp):
                for (lo, hi), s in zip(pieces, landed):
                    sp.dma_start(w[:, :, lo:hi], io["w_in"][l, :, lo:hi].rearrange(
                        "(k p) f -> p k f", p=P)).then_inc(*s.up(16))

            @block.tensor
            def _(pe):
                for g, (kind, j, b) in enumerate(groups):
                    piece = j if kind == "tok" else 3 + j * P // (XBC // 2)
                    pe.wait_ge(*landed[piece].at(16))
                    if g >= 8:
                        pe.wait_ge(*ev.at(g - 7))
                    for k in range(KD):
                        if kind == "tok":
                            lo, hi = pieces[j]
                            last = pe.matmul(p.psum[:, g % 8, 0:hi - lo], hT[:, k, b * P:(b + 1) * P],
                                             w[:, k, lo:hi], start=(k == 0), stop=(k == KD - 1))
                        else:
                            c = SSDW + j * P
                            last = pe.matmul(p.psum[:, g % 8, 0:HT], w[:, k, c:c + P],
                                             hT[:, k, b * HT:(b + 1) * HT], start=(k == 0), stop=(k == KD - 1))
                    last.then_inc(*mm.up())

            @block.gpsimd
            def _(pool):
                pad = t["pad"]
                pool.memset(pad[:, :, 0:2], 0.0)
                pool.memset(pad[:, :, 2 + LAT:6 + LAT], 0.0)
                pool.memset(pad[:, :, PADW - 2:PADW], 0.0).then_inc(*pads.up())

            @block.vector
            def _(dve):
                dve.wait_ge(*pads.at(1))
                for g, (kind, j, b) in enumerate(groups):
                    dve.wait_ge(*mm.at(g + 1))
                    if kind == "tok":
                        lo, hi = pieces[j]
                        last = dve.tensor_copy(token_out[j][:, b, :], p.psum[:, g % 8, 0:hi - lo])
                    elif b == 0:
                        last = dve.tensor_copy(t["pad"][:, j, 2:2 + HT], p.psum[:, g % 8, 0:HT])
                    else:
                        dve.tensor_copy(t["pad"][:, j, 2 + HT:2 + LAT], p.psum[:, g % 8, 0:LAT - HT])
                        last = dve.tensor_copy(t["pad"][:, j, 6 + LAT:6 + LAT + CTX],
                                               p.psum[:, g % 8, LAT - HT:HT])
                    last.then_inc(*ev.up())
    p.close_stage()


def stage_ssd(p, l, t):
    nc, io = p.nc, p.io
    small = p.sig("ssd_small")
    conv_done, silu_done = p.sig("conv_done"), p.sig("conv_silu_done")
    dve_c, act_c = p.sig("dve_chain"), p.sig("act_chain")
    dt_pre, e_neg, ln_u, a_exp, z_silu = (p.sig(n) for n in ("dt_pre", "dt_exp", "dt_log", "a_exp", "z_silu"))
    da_ready, la_ps, la_sb, la_exps = p.sig("da_ready"), p.sig("la_ps"), p.sig("la_sb"), p.sig("la_exps")
    turned, turned_out = p.sig("xs_turned"), p.sig("xs_turned_out")
    wx_ready, cs_ps, cs_used = p.sig("wx_ready"), p.sig("cs_ps"), p.sig("cs_used")
    st_in, st_turned, st_ready = p.sig("st_in"), p.sig("st_turned"), p.sig("st_ready")
    lab_ps, seg_ready, dec_ready, cb_ps, s_ready, y_ps, y_used = (p.sig(n) for n in (
        "lab_ps", "seg_ready", "decay_ready", "cb_ps", "scores_ready", "y_ps", "y_used"))
    fin_turned, fin_out, fin_stored = p.sig("fin_turned"), p.sig("fin_out"), p.sig("fin_stored")
    with ExitStack() as own:
        def sb(name, shape):
            return p.sb(f"ssd_{name}{l}", shape, ctx=own)
        cw, cb = sb("cw", [P, XF, TAPS]), sb("cb", [P, XF])
        dtb, alog, dsk = sb("dtb", [P, 2 * NH]), sb("alog", [P, 2 * NH]), sb("dsk", [P, NH])
        acc = sb("acc", [P, 2, PADW - 4])
        xbc = sb("xbc", [P, XF, T])
        btok = sb("btok", [P, TB, P])
        s5 = [P, TB, 2 * NH]
        v, neg, e, u, ln, dt, da, la, el, te, cd = (sb(n, s5) for n in (
            "v", "neg", "e", "u", "ln", "dt", "da", "la", "el", "te", "cd"))
        cdg = sb("cdg", [P, TB, 2, NH // 2])
        wx = sb("wx", [P, 2, SSDW])
        hs = sb("hs", [P, 2, TB, 256])
        stl = sb("stl", [P, 2, 2, P])
        hfin = sb("hfin", [P, 2, 256])
        seg = sb("seg", [P, 2, NH, P])
        cbs = sb("cbs", [P, NG, P])
        t1, t2 = sb("t1", [P, SSDW]), sb("t2", [P, SSDW])
        pad, z, xst, y = t["pad"], t["z"], t["xst"], t["y_ssd"]
        dtr = t["dtcq"][:, :, 0:2 * NH]
        with nc.Block() as block:
            @block.sync
            def _(sp):
                with nc.allow_non_contiguous_dma(reason="small per-channel vectors"):
                    for k in range(TAPS):
                        sp.dma_start(cw[:, :, k], io["conv_w"][l, k].rearrange("(f p) -> p f", p=P)).then_inc(*small.up(16))
                    sp.dma_start(cb[:], io["conv_b"][l].rearrange("(f p) -> p f", p=P)).then_inc(*small.up(16))
                for tile, name in ((dtb, "dt_bias"), (alog, "a_log"), (dsk, "d_skip")):
                    row = io[name][l].rearrange("a b -> (a b)") if name != "d_skip" else io[name][l]
                    sp.dma_start(tile[:], row.partition_broadcast(P)).then_inc(*small.up(16))
                for d in range(2):
                    for g in range(2):
                        sp.dma_start(stl[:, d, :, g * NS:(g + 1) * NS], io["state_ssm"][0, l, d, 4 * g:4 * g + 4].rearrange(
                            "(j h) q n -> (h q) j n", h=2)).then_inc(*st_in.up(16))
                sp.wait_ge(*fin_out.at(2))
                for d in range(2):
                    for g in range(2):
                        sp.dma_start(io["new_ssm"][0, l, d, 4 * g:4 * g + 4].rearrange("(j h) q n -> (h q) j n", h=2),
                                     stl[:, d, :, g * NS:(g + 1) * NS]).then_inc(*fin_stored.up(16))
                sp.wait_ge(*fin_stored.at(64))

            @block.scalar
            def _(act):
                act.wait_ge(*small.at(144))
                for f in range(XF):
                    act.wait_ge(*conv_done.at(f + 1))
                    act.activation(xbc[:, f, 0:LAT], acc[:, f % 2, 0:LAT], ACT.Silu, bias=cb[:, f:f + 1])
                    act.activation(xbc[:, f, LAT:T], acc[:, f % 2, 4 + LAT:4 + LAT + CTX], ACT.Silu,
                                   bias=cb[:, f:f + 1]).then_inc(*silu_done.up())
                act.activation(z[:], z[:], ACT.Silu).then_inc(*z_silu.up())
                act.wait_ge(*dt_pre.at(1))
                act.activation(e[:], neg[:], ACT.Exp).then_inc(*e_neg.up())
                act.activation(alog[:], alog[:], ACT.Exp).then_inc(*a_exp.up())
                act.wait_ge(*dt_pre.at(2))
                act.activation(ln[:], u[:], ACT.Ln).then_inc(*ln_u.up())
                act.wait_ge(*la_sb.at(1))
                act.activation(el[:], la[:], ACT.Exp)
                act.activation(cd[:], cd[:], ACT.Exp)
                act.activation(te[:], te[:], ACT.Exp).then_inc(*la_exps.up())
                for b in range(TB):
                    for d in range(2):
                        act.wait_ge(*seg_ready.at(2 * b + d + 1))
                        act.activation(seg[:, d], seg[:, d], ACT.Exp).then_inc(*dec_ready.up())

            @block.tensor
            def _(pe):
                def turn_state(bank, src):
                    for d in range(2):
                        for j in range(2):
                            last = pe.transpose(p.psum[:, bank, (2 * d + j) * P:(2 * d + j + 1) * P],
                                                src(d, j), p.ident[:])
                    return last
                pe.wait_ge(*st_in.at(64))
                turn_state(7, lambda d, j: stl[:, d, j, :]).then_inc(*st_turned.up())
                pe.wait_ge(*da_ready.at(1))
                lap = p.psum[:, 6, 0:4 * NH * TB].rearrange("p (b c) -> p b c", b=TB)
                for b in range(TB):
                    pe.matmul(lap[:, b, 0:NH], p.tri[:, 0], da[:, b, 0:NH], start=True, stop=True)
                    pe.matmul(lap[:, b, NH:2 * NH], p.tri[:, 1], da[:, b, NH:2 * NH], start=True, stop=True)
                    last = pe.matmul(lap[:, b, 2 * NH:4 * NH], p.ones[:], da[:, b, :], start=True, stop=True)
                last.then_inc(*la_ps.up())
                pe.wait_ge(*silu_done.at(XF - 1))
                for b in range(TB):
                    if b >= 2:
                        pe.wait_ge(*turned_out.at(b - 1))
                    for f in range(4):
                        pe.transpose(p.psum[:, b % 2, f * P:(f + 1) * P], xbc[:, f, b * P:(b + 1) * P], p.ident[:])
                    pe.transpose(p.psum[:, 2 + b % 2, 0:P], xbc[:, 4, b * P:(b + 1) * P],
                                 p.ident[:]).then_inc(*turned.up())
                pe.wait_ge(*silu_done.at(XF))
                for b in range(TB):
                    pe.wait_ge(*wx_ready.at(b + 1))
                    if b >= 2:
                        pe.wait_ge(*cs_used.at(b - 1))
                    for d in range(2):
                        for g in range(NG):
                            last = pe.matmul(p.psum[g * NS:(g + 1) * NS, 4 + b % 2, d * 256:(d + 1) * 256],
                                             btok[:, b, g * NS:(g + 1) * NS], wx[:, d, g * 256:(g + 1) * 256],
                                             start=(d == 0), stop=True, skip_group_check=True)
                    last.then_inc(*cs_ps.up())
                pe.wait_ge(*st_ready.at(1))
                for b in range(TB):
                    for d in range(2):
                        if b >= 1:
                            pe.wait_ge(*seg_ready.at(2 * (b - 1) + d + 1))
                        for h in range(NH):
                            last = pe.matmul(p.psum[:, 2 * d + h // 4, (h % 4) * P:(h % 4 + 1) * P],
                                             da[:, b, d * NH + h:d * NH + h + 1].to_broadcast([P, P]),
                                             p.tri[:, d], start=True, stop=True)
                        last.then_inc(*lab_ps.up())
                    if b >= 1:
                        pe.wait_ge(*y_used.at(b))
                    for g in range(NG):
                        part = slice(g * NS, (g + 1) * NS)
                        last = pe.matmul(p.psum[:, 7 - 3 * g, 0:P], xbc[part, 4, b * P:(b + 1) * P],
                                         xbc[part, 5, b * P:(b + 1) * P], start=True, stop=True)
                    last.then_inc(*cb_ps.up())
                    for d in range(2):
                        for g in range(NG):
                            part = slice(g * NS, (g + 1) * NS)
                            pe.matmul(p.psum[:, 5 + g, d * 256:(d + 1) * 256], xbc[part, 5, b * P:(b + 1) * P],
                                      hs[part, d, b, :], start=True, stop=True)
                    pe.wait_ge(*s_ready.at(b + 1))
                    for h in range(NH):
                        last = pe.matmul(p.psum[:, 4, h * HD:(h + 1) * HD], seg[:, 0, h],
                                         xst[:, b, h * HD:(h + 1) * HD], start=True, stop=True)
                    last.then_inc(*y_ps.up())
                pe.wait_ge(*y_used.at(TB))
                turn_state(7, lambda d, j: hfin[:, d, j * P:(j + 1) * P]).then_inc(*fin_turned.up())

            @block.vector
            def _(dve):
                link = chained(dve_c)
                dve.wait_ge(*small.at(144))
                link(dve, dve.tensor_tensor(v[:], dtr, insert_dim(dtb[:], 1, TB), ALU.add))
                dve.scalar_tensor_tensor(out=neg[:], in0=v[:], scalar=-1.0, in1=v[:], op0=ALU.mult,
                                         op1=ALU.min).then_inc(*dt_pre.up())
                for f in range(XF):
                    width = PADW - 4
                    if f >= 2:
                        dve.wait_ge(*silu_done.at(f - 1))
                    link(dve, dve.tensor_scalar(acc[:, f % 2], pad[:, f, 0:width], cw[:, f, 0:1], None, ALU.mult))
                    for k in range(1, TAPS):
                        ins = dve.scalar_tensor_tensor(out=acc[:, f % 2], in0=pad[:, f, k:k + width],
                                                       scalar=cw[:, f, k:k + 1], in1=acc[:, f % 2],
                                                       op0=ALU.mult, op1=ALU.add)
                        if k < TAPS - 1:
                            link(dve, ins)
                    ins.then_inc(*conv_done.up())
                dve.wait_ge(*e_neg.at(1))
                link(dve, dve.tensor_scalar(u[:], e[:], 1.0, None, ALU.add))
                link(dve, dve.tensor_scalar(dt[:], u[:], -1.0, None, ALU.add))
                link(dve, dve.tensor_tensor(dt[:], e[:], dt[:], ALU.subtract))
                dve.scalar_tensor_tensor(out=v[:], in0=v[:], scalar=0.0, in1=dt[:], op0=ALU.max,
                                         op1=ALU.add).then_inc(*dt_pre.up())
                dve.wait_ge(*dt_pre.at(2))
                dve.wait_ge(*ln_u.at(1))
                link(dve, dve.tensor_tensor(dt[:], v[:], ln[:], ALU.add))
                dve.wait_ge(*a_exp.at(1))
                dve.scalar_tensor_tensor(out=da[:], in0=dt[:], scalar=-1.0, in1=insert_dim(alog[:], 1, TB),
                                         op0=ALU.mult, op1=ALU.mult).then_inc(*da_ready.up())
                dve.wait_ge(*st_turned.at(1))
                link(dve, dve.tensor_copy(hs[:, 0, 0, :], p.psum[:, 7, 0:256]))
                link(dve, dve.tensor_copy(hs[:, 1, LB - 1, :], p.psum[:, 7, 256:512]))
                link(dve, dve.memset(hs[:, :, LB, :], 0.0))
                dve.wait_ge(*la_ps.at(1))
                lap = p.psum[:, 6, 0:4 * NH * TB].rearrange("p (b c) -> p b c", b=TB)
                link(dve, dve.tensor_copy(la[:], lap[:, :, 0:2 * NH]))
                link(dve, dve.tensor_copy(cd[:], lap[:, :, 2 * NH:4 * NH]))
                dve.tensor_tensor(te[:], cd[:], la[:], ALU.subtract).then_inc(*la_sb.up())
                dve.wait_ge(*la_exps.at(1))
                link(dve, dve.tensor_tensor(te[:], te[:], dt[:], ALU.mult))
                for g in range(NG):
                    for d in range(2):
                        link(dve, dve.tensor_copy(cdg[g * NS:(g + 1) * NS, :, d],
                                                  cd[g * NS:(g + 1) * NS, :, d * NH + 4 * g:d * NH + 4 * g + 4]))
                for b in range(TB):
                    dve.wait_ge(*turned.at(b + 1))
                    link(dve, dve.tensor_copy(xst[:, b], p.psum[:, b % 2]))
                    dve.tensor_copy(btok[:, b], p.psum[:, 2 + b % 2, 0:P]).then_inc(*turned_out.up())

                def advance(b, d, out):
                    link(dve, dve.tensor_tensor(out.rearrange("p (h q) -> p h q", h=4),
                                                hs[:, d, b].rearrange("p (h q) -> p h q", h=4),
                                                cdg[:, b, d].to_broadcast([P, 4, HD]), ALU.mult))
                    link(dve, dve.tensor_tensor(out, out, hadd(b, d), ALU.add))

                def hadd(b, d):
                    return adds[:, b, d, :]
                adds = t["qkv_room"][:, 0:TB * 512].rearrange("p (b d c) -> p b d c", b=TB, d=2)
                for b in range(TB):
                    if b >= 1:
                        dve.wait_ge(*cs_ps.at(b))
                    for d in range(2):
                        last = dve.tensor_tensor(wx[:, d].rearrange("p (h q) -> p h q", h=NH),
                                                 xst[:, b].rearrange("p (h q) -> p h q", h=NH),
                                                 te[:, b, d * NH:(d + 1) * NH].to_broadcast([P, NH, HD]), ALU.mult)
                    last.then_inc(*wx_ready.up())
                    dve.wait_ge(*cs_ps.at(b + 1))
                    dve.tensor_copy(adds[:, b], p.psum[:, 4 + b % 2].rearrange(
                        "p (d c) -> p d c", d=2)).then_inc(*cs_used.up())
                dve.wait_ge(*cs_used.at(TB))
                for b in range(LB - 1):
                    advance(b, 0, hs[:, 0, b + 1])
                for b in range(LB - 1, 0, -1):
                    advance(b, 1, hs[:, 1, b - 1])
                dve.tensor_copy(hfin[:], adds[:, LB]).then_inc(*st_ready.up())
                for b in range(TB):
                    for d in range(2):
                        dve.wait_ge(*lab_ps.at(2 * b + d + 1))
                        if b >= 1:
                            dve.wait_ge(*y_ps.at(b))
                        for h in range(NH):
                            last = dve.scalar_tensor_tensor(
                                out=seg[:, d, h], in0=p.psum[:, 2 * d + h // 4, (h % 4) * P:(h % 4 + 1) * P],
                                scalar=la[:, b, d * NH + h:d * NH + h + 1], in1=p.far[:, d],
                                op0=ALU.subtract, op1=ALU.add)
                        last.then_inc(*seg_ready.up())
                    dve.wait_ge(*cb_ps.at(b + 1))
                    dve.tensor_copy(cbs[:, 0], p.psum[:, 7, 0:P])
                    link(dve, dve.tensor_copy(cbs[:, 1], p.psum[:, 4, 0:P]))
                    dve.wait_ge(*dec_ready.at(2 * b + 1))
                    for h in range(NH):
                        last = dve.tensor_scalar(seg[:, 0, h], seg[:, 0, h], dt[:, b, h:h + 1], None, ALU.mult)
                    link(dve, last)
                    dve.wait_ge(*dec_ready.at(2 * b + 2))
                    for h in range(NH):
                        last = dve.scalar_tensor_tensor(
                            out=seg[:, 0, h], in0=seg[:, 1, h], scalar=dt[:, b, NH + h:NH + h + 1],
                            in1=seg[:, 0, h], op0=ALU.mult, op1=ALU.add)
                    link(dve, last)
                    for g in range(NG):
                        last = dve.tensor_tensor(seg[:, 0, 4 * g:4 * g + 4], seg[:, 0, 4 * g:4 * g + 4],
                                                 insert_dim(cbs[:, g], 1, 4), ALU.mult)
                    last.then_inc(*s_ready.up())

                    def heads(ap):
                        return ap.rearrange("p (h q) -> p h q", h=NH)

                    def by_group(ap):
                        return ap.rearrange("p (g h q) -> p g h q", g=NG, q=HD)

                    def inter(d):
                        return p.psum[:, 5:7, d * 256:(d + 1) * 256].rearrange("p g (h q) -> p g h q", q=HD)

                    def heads_la(d):
                        la_exp = el[:, b, d * NH:(d + 1) * NH].rearrange("p (g h) -> p g h", g=NG)
                        return la_exp.to_broadcast([P, NG, NH // NG, HD])
                    dve.wait_ge(*y_ps.at(b + 1))
                    link(dve, dve.tensor_tensor(by_group(t1[:]), inter(0), heads_la(0), ALU.mult))
                    link(dve, dve.tensor_tensor(by_group(t2[:]), inter(1), heads_la(1), ALU.mult))
                    link(dve, dve.tensor_tensor(t1[:], t1[:], t2[:], ALU.add))
                    link(dve, dve.tensor_tensor(heads(t2[:]), heads(xst[:, b]), dsk[:].to_broadcast([P, NH, HD]),
                                                ALU.mult))
                    link(dve, dve.tensor_tensor(t2[:], p.psum[:, 4], t2[:], ALU.add))
                    link(dve, dve.tensor_tensor(t1[:], t1[:], t2[:], ALU.add))
                    if b == 0:
                        dve.wait_ge(*z_silu.at(1))
                    dve.tensor_tensor(y[:, b], t1[:], z[:, b], ALU.mult).then_inc(*y_used.up())
                dve.wait_ge(*fin_turned.at(1))
                dve.tensor_copy(stl[:, 0], p.psum[:, 7, 0:256].rearrange("p (j c) -> p j c", j=2)).then_inc(*fin_out.up())
                dve.tensor_copy(stl[:, 1], p.psum[:, 7, 256:512].rearrange("p (j c) -> p j c", j=2)).then_inc(*fin_out.up())
    p.close_stage()


def stage_attention(p, l, t):
    nc, io = p.nc, p.io
    w_in, gains_in, cache_in = p.sig("at_w_in"), p.sig("at_gains_in"), p.sig("at_cache_in")
    sq, mean, root, rs = p.sig("at_squares"), p.sig("at_mean"), p.sig("at_root"), p.sig("at_rstd")
    kvn, krt_ready, lat_tr, lat_ev = p.sig("at_kvn"), p.sig("at_krt"), p.sig("at_lat_turned"), p.sig("at_lat_out")
    new_out = p.sig("at_new_stored")
    gm_ps, gm_ev, qt_ready = p.sig("at_gemm_ps"), p.sig("at_gemm_out"), p.sig("at_q_ready")
    tr_ps, tr_ev = p.sig("at_turned"), p.sig("at_turned_out")
    sc_ps, mx_ready, e_ready, pt_ps, pt_ev, o_ps, o_ev = (p.sig(n) for n in (
        "at_scores_ps", "at_max", "at_exp", "at_probs_turned", "at_probs_out", "at_o_ps", "at_o_out"))
    zeroed = p.sig("at_zeroed")
    dve_c, act_c = p.sig("dve_chain"), p.sig("act_chain")
    QF, VF = QR // P, KVR // P
    with ExitStack() as own:
        def sb(name, shape):
            return p.sb(f"at_{name}{l}", shape, ctx=own)
        wq = sb("wq", [P, QF, NH * QD])
        wkv = sb("wkv", [P, VF, NH * (NOPE + VD)])
        gq, kvrow = sb("gq", [P, QF]), sb("kvrow", [P, KVR])
        cos, sin = sb("cos", [P, LB, ROPE]), sb("sin", [P, LB, ROPE])
        past = sb("past", [P, KVR])
        krt = sb("krt", [P, KB, QD])
        junk = sb("junk", [P, QR])
        stat, rstd = sb("stat", [P, 2, TB]), sb("rstd", [P, 2, TB])
        cqT = sb("cqT", [P, QF, T])
        ckvT = sb("ckvT", [P, VF, KEYS])
        qtok = sb("qtok", [P, 2, NH * QD])
        ra, rb = sb("ra", [P, NH, ROPE]), sb("rb", [P, NH, ROPE])
        qT = sb("qT", [P, NH, T])
        kT = t["qkv_room"].rearrange("p (h k) -> p h k", h=NH)
        vt = sb("vt", [P, KB, NH * VD])
        prob = sb("prob", [P, 2, LAT + PAST])
        probT = sb("probT", [P, 2, LAT + PAST])
        mx = sb("mx", [P, 2 * NH, 2])
        total = sb("total", [P, 2, NH])
        cq, ckr, o = t["dtcq"][:, :, 2 * NH:], t["ckr"], t["o"]
        ck, kr = ckr[:, :, 0:KVR], ckr[:, :, KVR:KVR + ROPE]
        mod = Modulation(p, [(l, u) for u in range(2 * D // UNIT, UNITS)] +
                         ([(1, u) for u in range(2 * D // UNIT)] if l == 0 else []), 7, own, f"at{l}")
        turns = [("past", 0)] + [("tok", b) for b in range(TB)]
        items = [(b, h) for b in range(TB) for h in range(NH)]

        def keys_of(b):
            return (0, PAST + LAT) if b < LB else (PAST + LAT, KEYS)
        with nc.Block() as block:
            @block.sync
            def _(sp):
                sp.dma_start(wq[:], io["w_uq"][l].rearrange("(k p) f -> p k f", p=P)).then_inc(*w_in.up(16))
                sp.dma_start(wkv[:], io["w_ukv"][l].rearrange("(k p) f -> p k f", p=P)).then_inc(*w_in.up(16))
                with nc.allow_non_contiguous_dma(reason="one gain per partition"):
                    sp.dma_start(gq[:], io["q_norm"][l].rearrange("(k p) -> p k", p=P)).then_inc(*gains_in.up(16))
                sp.dma_start(kvrow[:], io["kv_norm"][l].partition_broadcast(P)).then_inc(*gains_in.up(16))
                sp.dma_start(cos[:], io["rope_cos"].rearrange("(b p) r -> p b r", p=P)).then_inc(*gains_in.up(16))
                sp.dma_start(sin[:], io["rope_sin"].rearrange("(b p) r -> p b r", p=P)).then_inc(*gains_in.up(16))
                sp.dma_start(past[:], io["cache_ckv"][0, l]).then_inc(*cache_in.up(16))
                sp.wait_ge(*zeroed.at(1))
                sp.dma_start(krt[:, 0, NOPE:QD], io["cache_krope"][0, l]).then_inc(*cache_in.up(16))
                sp.dma_start(io["new_krope"][0, l], kr[:, LB]).then_inc(*new_out.up(16))
                sp.wait_ge(*kvn.at(TB))
                sp.dma_start(io["new_ckv"][0, l], ck[:, LB]).then_inc(*new_out.up(16))
                mod.load(sp)
                sp.wait_ge(*new_out.at(32))

            @block.gpsimd
            def _(pool):
                pool.memset(krt[:], 0.0).then_inc(*zeroed.up())

            @block.scalar
            def _(act):
                for b in range(TB):
                    act.activation(junk[:], cq[:, b], ACT.Square, accum_out=stat[:, 0, b:b + 1]).then_inc(*sq.up())
                    act.wait_ge(*sq.at(2 * b + 1))
                    act.activation(junk[:, 0:KVR], ck[:, b], ACT.Square, accum_out=stat[:, 1, b:b + 1]).then_inc(*sq.up())
                    act.wait_ge(*sq.at(2 * b + 2))
                act.wait_ge(*mean.at(1))
                act.activation(rstd[:], stat[:], ACT.Sqrt).then_inc(*root.up())
                for n, (b, h) in enumerate(items):
                    lo, hi = keys_of(b)
                    act.wait_ge(*mx_ready.at(n + 1))
                    if n >= 2:
                        act.wait_ge(*pt_ps.at(n - 1))
                    if b >= 2 and h == 0:
                        act.wait_ge(*o_ev.at(b - 1))
                    w = (hi - lo) // 2
                    act.activation(prob[:, n % 2, 0:hi - lo].rearrange("p (a k) -> p a k", a=2),
                                   p.psum[:, 2 * (n % 2):2 * (n % 2) + 2, 0:w], ACT.Exp,
                                   bias=mx[:, n % (2 * NH), 1:2], scale=SCALE,
                                   accum_out=total[:, b % 2, h:h + 1]).then_inc(*e_ready.up())

            @block.tensor
            def _(pe):
                def turn_queries(pe, b):
                    pe.wait_ge(*qt_ready.at(b + 1))
                    if b >= 2:
                        pe.wait_ge(*tr_ev.at(b - 1))
                    for h in range(NH):
                        last = pe.transpose(p.psum[0:QD, 4 + 2 * (b % 2) + h // 4, (h % 4) * P:(h % 4 + 1) * P],
                                            qtok[:, b % 2, h * QD:(h + 1) * QD], p.ident[:])
                    last.then_inc(*tr_ps.up())

                pe.wait_ge(*cache_in.at(32))
                for n, (kind, b) in enumerate(turns):
                    if kind == "tok":
                        pe.wait_ge(*kvn.at(b + 1))
                    if n >= 4:
                        pe.wait_ge(*lat_ev.at(n - 3))
                    for k in range(VF):
                        src = past[:, k * P:(k + 1) * P] if kind == "past" else ck[:, b, k * P:(k + 1) * P]
                        last = pe.transpose(p.psum[:, 2 * (n % 4), k * P:(k + 1) * P], src, p.ident[:])
                    if kind == "tok":
                        for k in range(QF):
                            last = pe.transpose(p.psum[:, 2 * (n % 4) + 1, k * P:(k + 1) * P],
                                                cq[:, b, k * P:(k + 1) * P], p.ident[:])
                    last.then_inc(*lat_tr.up())
                pe.wait_ge(*w_in.at(32))
                pe.wait_ge(*lat_ev.at(len(turns)))
                g = 0
                for b in range(TB):
                    if b >= 2:
                        pe.wait_ge(*gm_ev.at(b - 1))
                    for part, (lo, hi) in enumerate(((0, 512), (512, NH * QD))):
                        for k in range(QF):
                            last = pe.matmul(p.psum[:, 2 * (b % 2) + part, 0:hi - lo], cqT[:, k, b * P:(b + 1) * P],
                                             wq[:, k, lo:hi], start=(k == 0), stop=(k == QF - 1))
                    last.then_inc(*gm_ps.up())
                    if b >= 1:
                        turn_queries(pe, b - 1)
                turn_queries(pe, TB - 1)
                for h in range(NH):
                    if h < 2:
                        pe.wait_ge(*gm_ev.at(TB - 1 + h))
                    else:
                        pe.wait_ge(*gm_ev.at(TB + h - 1))
                    for part in range(2):
                        for k in range(VF):
                            last = pe.matmul(p.psum[0:NOPE, 2 * (h % 2) + part, 0:KEYS // 2],
                                             wkv[:, k, h * (NOPE + VD):h * (NOPE + VD) + NOPE],
                                             ckvT[:, k, part * KEYS // 2:(part + 1) * KEYS // 2],
                                             start=(k == 0), stop=(k == VF - 1))
                    last.then_inc(*gm_ps.up())
                for n in range(KB):
                    pe.wait_ge(*gm_ev.at(TB + NH + n - 1))
                    for k in range(VF):
                        last = pe.matmul(p.psum[:, 2 * (n % 2), 0:NH * VD], ckvT[:, k, n * P:(n + 1) * P],
                                         wkv[:, k].rearrange("p (h c) -> p h c", h=NH)[:, :, NOPE:NOPE + VD],
                                         start=(k == 0), stop=(k == VF - 1))
                    last.then_inc(*gm_ps.up())
                pe.wait_ge(*krt_ready.at(1))
                pe.wait_ge(*tr_ev.at(TB))
                for n in range(KB):
                    last = pe.transpose(p.psum[0:QD, 4 + n // 3, (n % 3) * P:(n % 3 + 1) * P], krt[:, n, :], p.ident[:])
                last.then_inc(*tr_ps.up())
                pe.wait_ge(*gm_ev.at(TB + NH + KB))
                pe.wait_ge(*tr_ev.at(TB + 1))

                def scores(n):
                    b, h = items[n]
                    lo, hi = keys_of(b)
                    w = (hi - lo) // 2
                    if n >= 2:
                        pe.wait_ge(*e_ready.at(n - 1))
                    for part in range(2):
                        last = pe.matmul(p.psum[:, 2 * (n % 2) + part, 0:w], qT[0:QD, h, b * P:(b + 1) * P],
                                         kT[0:QD, h, lo + part * w:lo + (part + 1) * w], start=True, stop=True)
                    last.then_inc(*sc_ps.up())

                def turn_probs(n):
                    b, h = items[n]
                    lo, hi = keys_of(b)
                    pe.wait_ge(*e_ready.at(n + 1))
                    if n >= 1:
                        pe.wait_ge(*pt_ev.at(n))
                    for k in range((hi - lo) // P):
                        last = pe.transpose(p.psum[:, 4 + k // 4, (k % 4) * P:(k % 4 + 1) * P],
                                            prob[:, n % 2, k * P:(k + 1) * P], p.ident[:])
                    last.then_inc(*pt_ps.up())

                def outputs(n):
                    b, h = items[n]
                    lo, hi = keys_of(b)
                    pe.wait_ge(*pt_ev.at(n + 1))
                    if h == 0 and b >= 1:
                        pe.wait_ge(*o_ev.at(b))
                    nk = (hi - lo) // P
                    for k in range(nk):
                        last = pe.matmul(p.psum[:, 6, h * VD:(h + 1) * VD], probT[:, n % 2, k * P:(k + 1) * P],
                                         vt[:, lo // P + k, h * VD:(h + 1) * VD], start=(k == 0), stop=(k == nk - 1))
                    last.then_inc(*o_ps.up())
                scores(0)
                for n in range(len(items)):
                    if n + 1 < len(items):
                        scores(n + 1)
                    if n >= 1:
                        outputs(n - 1)
                    turn_probs(n)
                    if n < len(mod.steps):
                        mod.on_tensor(pe, n)
                outputs(len(items) - 1)

            @block.vector
            def _(dve):
                link = chained(dve_c)

                def rotate(u, b, n):
                    def quarters(ap):
                        return ap.rearrange("p n (a s r) -> p (n a) s r", a=2, s=2) if n == 1 else \
                            ap.rearrange("p n (a s r) -> p n a s r", a=2, s=2)
                    c, s = insert_dim(cos[:, b], 1, n), insert_dim(sin[:, b], 1, n)
                    link(dve, dve.tensor_tensor(ra[:, 0:n], u, c, ALU.mult))
                    for side in range(2):
                        for a in range(2):
                            dst = slice(16 * a + 8 * side, 16 * a + 8 * side + 8)
                            src = slice(16 * a + 8 * (1 - side), 16 * a + 8 * (1 - side) + 8)
                            last = dve.tensor_tensor(rb[:, 0:n, dst], u[:, :, src], s[:, :, dst], ALU.mult)
                    link(dve, last)
                    return dve.tensor_tensor(u, ra[:, 0:n], rb[:, 0:n], ALU.add)
                dve.wait_ge(*sq.at(2 * TB))
                dve.tensor_scalar(stat[:, 0], stat[:, 0], 1.0 / QR, EPS, ALU.mult, ALU.add)
                dve.tensor_scalar(stat[:, 1], stat[:, 1], 1.0 / KVR, EPS, ALU.mult, ALU.add).then_inc(*mean.up())
                dve.wait_ge(*root.at(1))
                dve.reciprocal(rstd[:], rstd[:]).then_inc(*rs.up())
                dve.wait_ge(*rs.at(1))
                dve.wait_ge(*gains_in.at(64))
                for b in range(TB):
                    dve.scalar_tensor_tensor(out=ck[:, b], in0=ck[:, b], scalar=rstd[:, 1, b:b + 1], in1=kvrow[:],
                                             op0=ALU.mult, op1=ALU.mult)
                    dve.tensor_scalar(cq[:, b], cq[:, b], rstd[:, 0, b:b + 1], None, ALU.mult).then_inc(*kvn.up())
                dve.wait_ge(*zeroed.at(1))
                for b in range(LB):
                    link(dve, dve.tensor_copy(krt[:, 1 + b, NOPE:QD], kr[:, b]))
                    link(dve, rotate(krt[:, 1 + b:2 + b, NOPE:QD], b, 1))
                dve.tensor_copy(krt[:, 1 + LB, NOPE:QD], kr[:, LB]).then_inc(*krt_ready.up())
                for n, (kind, b) in enumerate(turns):
                    dve.wait_ge(*lat_tr.at(n + 1))
                    last = dve.tensor_copy(ckvT[:, :, n * P:(n + 1) * P],
                                           p.psum[:, 2 * (n % 4), 0:KVR].rearrange("p (k c) -> p k c", k=VF))
                    if kind == "tok":
                        for k in range(QF):
                            last = dve.tensor_scalar(cqT[:, k, b * P:(b + 1) * P],
                                                     p.psum[:, 2 * (n % 4) + 1, k * P:(k + 1) * P],
                                                     gq[:, k:k + 1], None, ALU.mult)
                    last.then_inc(*lat_ev.up())

                def take_turned(b):
                    dve.wait_ge(*tr_ps.at(b + 1))
                    dve.tensor_copy(qT[0:QD, :, b * P:(b + 1) * P].rearrange("p (a h) c -> p a h c", a=2),
                                    p.psum[0:QD, 4 + 2 * (b % 2):6 + 2 * (b % 2)].rearrange(
                                        "p a (h c) -> p a h c", h=4)).then_inc(*tr_ev.up())
                for b in range(TB):
                    dve.wait_ge(*gm_ps.at(b + 1))
                    if b >= 2:
                        dve.wait_ge(*tr_ps.at(b - 1))
                    dve.tensor_copy(qtok[:, b % 2, 0:512], p.psum[:, 2 * (b % 2)])
                    dve.tensor_copy(qtok[:, b % 2, 512:NH * QD],
                                    p.psum[:, 2 * (b % 2) + 1, 0:NH * QD - 512]).then_inc(*gm_ev.up())
                    dve.wait_ge(*gm_ev.at(b + 1))
                    if b < LB:
                        rotate(qtok[:, b % 2].rearrange("p (h c) -> p h c", h=NH)[:, :, NOPE:QD], b,
                               NH).then_inc(*qt_ready.up())
                    else:
                        dve.engine_nop().then_inc(*qt_ready.up())
                    if b >= 1:
                        take_turned(b - 1)
                take_turned(TB - 1)
                for h in range(NH):
                    dve.wait_ge(*gm_ps.at(TB + h + 1))
                    dve.tensor_copy(kT[0:NOPE, h].rearrange("p (a k) -> p a k", a=2),
                                    p.psum[0:NOPE, 2 * (h % 2):2 * (h % 2) + 2, 0:KEYS // 2]).then_inc(*gm_ev.up())
                for n in range(KB):
                    dve.wait_ge(*gm_ps.at(TB + NH + n + 1))
                    dve.tensor_copy(vt[:, n], p.psum[:, 2 * (n % 2)]).then_inc(*gm_ev.up())
                dve.wait_ge(*tr_ps.at(TB + 1))
                for part in range(2):
                    last = dve.tensor_copy(kT[NOPE:QD, :, part * 3 * P:(part + 1) * 3 * P],
                                           insert_dim(p.psum[NOPE:QD, 4 + part, 0:3 * P], 1, NH))
                last.then_inc(*tr_ev.up())

                def largest(n):
                    b, h = items[n]
                    lo, hi = keys_of(b)
                    w = (hi - lo) // 2
                    dve.wait_ge(*sc_ps.at(n + 1))
                    m = mx[:, n % (2 * NH)]
                    link(dve, dve.tensor_reduce(m[:, 0:1], p.psum[:, 2 * (n % 2):2 * (n % 2) + 2, 0:w],
                                                mybir.AxisListType.XY, ALU.max))
                    dve.tensor_scalar(m[:, 1:2], m[:, 0:1], -SCALE, None, ALU.mult).then_inc(*mx_ready.up())

                def take_block(b):
                    dve.wait_ge(*o_ps.at(NH * (b + 1)))
                    link(dve, dve.reciprocal(total[:, b % 2], total[:, b % 2]))
                    dve.tensor_tensor(o[:, b].rearrange("p (h c) -> p h c", h=NH),
                                      p.psum[:, 6].rearrange("p (h c) -> p h c", h=NH),
                                      total[:, b % 2].to_broadcast([P, NH, VD]), ALU.mult).then_inc(*o_ev.up())
                largest(0)
                for n, (b, h) in enumerate(items):
                    if n + 1 < len(items):
                        largest(n + 1)
                    lo, hi = keys_of(b)
                    dve.wait_ge(*pt_ps.at(n + 1))
                    if n >= 2:
                        dve.wait_ge(*o_ps.at(n - 1))
                    nk = (hi - lo) // P
                    first = min(nk, 4) * P
                    last = dve.tensor_copy(probT[:, n % 2, 0:first], p.psum[:, 4, 0:first])
                    if nk > 4:
                        last = dve.tensor_copy(probT[:, n % 2, first:nk * P], p.psum[:, 5, 0:nk * P - first])
                    last.then_inc(*pt_ev.up())
                    if h == 0 and b >= 1:
                        take_block(b - 1)
                    if 1 <= n <= len(mod.steps):
                        mod.on_vector(dve, n - 1)
                take_block(TB - 1)
                mod.vectors(dve, link, l, 0, ("gate",))
                mod.vectors(dve, link, l, 1, ("scale", "gate"))
                if l == 0:
                    mod.vectors(dve, link, 1, 0, ("scale",))
    p.close_stage()


def residual_tail(p, l, which, own, block_parts):
    raise NotImplementedError


def gate_rows(p, pe, l, which, gr_ps, gr_ev, first_bank=0):
    for s in range(2):
        if s >= 1:
            pass
        for k in range(KD):
            last = pe.matmul(p.psum[:, first_bank + 2 * s + k // 4, (k % 4) * P:(k % 4 + 1) * P],
                             p.gate_out[:, l, which, k, s:s + 1].to_broadcast([P, P]), p.ident[:], start=True, stop=True)
    last.then_inc(*gr_ps.up())


def stage_out_proj(p, l, t):
    nc, io = p.nc, p.io
    w_in, small = p.sig("wo_in"), p.sig("wo_small")
    sq, mean, root, rs, yn, tr, ev = (p.sig(n) for n in (
        "pn_squares", "pn_mean", "pn_root", "pn_rstd", "pn_scaled", "pn_turned", "pn_evicted"))
    gr_ps, gr_ev, mm, sq2, m2, r2, res = (p.sig(n) for n in (
        "gate_ps", "gate_out", "out_ps", "out_squares", "out_mean", "out_root", "residual"))
    dve_c = p.sig("dve_chain")
    with ExitStack() as own:
        def sb(name, shape):
            return p.sb(f"op_{name}{l}", shape, ctx=own)
        w = sb("w", [P, KD, D])
        gain = sb("gain", [P, KD])
        junk = sb("junk", [P, D])
        stat, rstd = sb("stat", [P, TB, 2]), sb("rstd", [P, TB, 2])
        stat2, rstd2 = sb("stat2", [P, TB, 2]), sb("rstd2", [P, TB])
        yT = sb("yT", [P, KD, T])
        rows = sb("rows", [P, 2, D])
        upd = sb("upd", [P, 2, D])
        parts = (t["y_ssd"], t["o"])
        with nc.Block() as block:
            @block.sync
            def _(sp):
                for half in range(2):
                    sp.dma_start(w[:, :, half * 512:(half + 1) * 512], io["w_out"][l, :, half * 512:(half + 1) * 512].rearrange(
                        "(k p) f -> p k f", p=P)).then_inc(*w_in.up(16))
                with nc.allow_non_contiguous_dma(reason="one gain per partition"):
                    sp.dma_start(gain[:, 0:4], io["ssd_norm"][l].rearrange("(k p) -> p k", p=P)).then_inc(*small.up(16))
                    sp.dma_start(gain[:, 4:8], io["mla_norm"][l].rearrange("(k p) -> p k", p=P)).then_inc(*small.up(16))

            @block.scalar
            def _(act):
                n = 0
                for b in range(TB):
                    for j, part in enumerate(parts):
                        act.activation(junk[:, 0:512], part[:, b], ACT.Square, accum_out=stat[:, b, j:j + 1]).then_inc(*sq.up())
                        n += 1
                        act.wait_ge(*sq.at(n))
                act.wait_ge(*mean.at(1))
                act.activation(rstd[:], stat[:], ACT.Sqrt).then_inc(*root.up())
                for b in range(TB):
                    act.wait_ge(*rs.at(1))
                    for j, part in enumerate(parts):
                        last = act.activation(part[:, b], part[:, b], ACT.Copy, scale=rstd[:, b, j:j + 1])
                    last.then_inc(*yn.up())
                for b in range(TB):
                    act.wait_ge(*mm.at(b + 1))
                    for half in range(2):
                        act.activation(junk[:, 0:512], p.psum[:, 4 + 2 * (b % 2) + half], ACT.Square,
                                       accum_out=stat2[:, b, half:half + 1]).then_inc(*sq2.up())
                        act.wait_ge(*sq2.at(2 * b + half + 1))
                    act.wait_ge(*m2.at(b + 1))
                    act.activation(rstd2[:, b:b + 1], stat2[:, b, 0:1], ACT.Sqrt).then_inc(*r2.up())

            @block.tensor
            def _(pe):
                gate_rows(p, pe, l, 0, gr_ps, gr_ev)
                pe.wait_ge(*gr_ev.at(1))
                for b in range(TB):
                    pe.wait_ge(*yn.at(b + 1))
                    if b >= 2:
                        pe.wait_ge(*ev.at(b - 1))
                    for k in range(KD):
                        part = parts[k // 4]
                        last = pe.transpose(p.psum[:, 2 * (b % 2) + k // 4, (k % 4) * P:(k % 4 + 1) * P],
                                            part[:, b, (k % 4) * P:(k % 4 + 1) * P], p.ident[:])
                    last.then_inc(*tr.up())
                    if b == 1:
                        pe.wait_ge(*w_in.at(32))
                for b in range(TB):
                    pe.wait_ge(*ev.at(b + 1))
                    pe.wait_ge(*w_in.at(32))
                    if b >= 2:
                        pe.wait_ge(*res.at(b - 1))
                    for half in range(2):
                        for k in range(KD):
                            last = pe.matmul(p.psum[:, 4 + 2 * (b % 2) + half], yT[:, k, b * P:(b + 1) * P],
                                             w[:, k, half * 512:(half + 1) * 512], start=(k == 0), stop=(k == KD - 1))
                    last.then_inc(*mm.up())

            @block.vector
            def _(dve):
                link = chained(dve_c)
                dve.wait_ge(*gr_ps.at(1))
                dve.tensor_copy(rows[:].rearrange("p s (a c) -> p (s a) c", a=2), p.psum[:, 0:4]).then_inc(*gr_ev.up())
                dve.wait_ge(*sq.at(2 * TB))
                dve.tensor_scalar(stat[:], stat[:], 1.0 / 512, EPS, ALU.mult, ALU.add).then_inc(*mean.up())
                dve.wait_ge(*root.at(1))
                dve.reciprocal(rstd[:], rstd[:]).then_inc(*rs.up())
                dve.wait_ge(*small.at(32))
                for b in range(TB):
                    dve.wait_ge(*tr.at(b + 1))
                    for k in range(KD):
                        last = dve.tensor_scalar(yT[:, k, b * P:(b + 1) * P],
                                                 p.psum[:, 2 * (b % 2) + k // 4, (k % 4) * P:(k % 4 + 1) * P],
                                                 gain[:, k:k + 1], None, ALU.mult)
                    last.then_inc(*ev.up())
                for b in range(TB):
                    take_residual(p, dve, link, b, p.psum[:, 4 + 2 * (b % 2):6 + 2 * (b % 2)], rows, upd,
                                  stat2, rstd2, sq2, m2, r2, res)
    p.close_stage()


def take_residual(p, dve, link, b, src, rows, upd, stat2, rstd2, sq2, m2, r2, res):
    s = SEQ_OF[b]
    dve.wait_ge(*sq2.at(2 * b + 2))
    link(dve, dve.tensor_tensor(stat2[:, b, 0:1], stat2[:, b, 0:1], stat2[:, b, 1:2], ALU.add))
    dve.tensor_scalar(stat2[:, b, 0:1], stat2[:, b, 0:1], 1.0 / D, EPS, ALU.mult, ALU.add).then_inc(*m2.up())
    dve.wait_ge(*r2.at(b + 1))
    link(dve, dve.reciprocal(rstd2[:, b:b + 1], rstd2[:, b:b + 1]))
    link(dve, dve.scalar_tensor_tensor(
        out=upd[:, b % 2].rearrange("p (a c) -> p a c", a=2), in0=src, scalar=rstd2[:, b:b + 1],
        in1=rows[:, s].rearrange("p (a c) -> p a c", a=2), op0=ALU.mult, op1=ALU.mult))
    dve.tensor_tensor(p.x[:, b], p.x[:, b], upd[:, b % 2], ALU.add).then_inc(*res.up())


I32 = mybir.dt.int32
SL = 256
SLB = SL // P
MAX_BLOCKS = (2 * T - NE) // SL + NE


def stage_router(p, l, hT, ht, r):
    nc, io = p.nc, p.io
    r_in, lg_ps, best, e2_done, made, turned, rows_out, stored, iota_done, pos_ps, ht_ps, ht_hi, ht_out = (
        p.sig(n) for n in ("router_in", "router_ps", "router_best", "router_exp", "router_made", "router_turned",
                           "router_rows", "router_stored", "router_iota", "router_pos", "router_ht_ps",
                           "router_ht_hi", "router_ht_out"))
    mask_ready, cols_out, strict_ready = p.sig("router_mask"), p.sig("router_cols"), p.sig("router_strict")
    dve_c = p.sig("dve_chain")
    hi, lo = ht
    with ExitStack() as own:
        def sb(name, shape, dt=F32):
            return p.sb(f"rt_{name}{l}", shape, dt, ctx=own)
        wr = sb("wr", [P, KD, NE])
        lg, top = sb("lg", [P, TB, NE]), sb("top", [P, TB, 8])
        idx, idf = sb("idx", [P, TB, 8], U32), sb("idf", [P, TB, 8])
        iota, iota_b = sb("iota", [P, NE]), sb("iota_b", [P, MAX_BLOCKS])
        strict = sb("strict", [P, P])
        diff, e2, w1, w2 = (sb(n, [P, TB]) for n in ("diff", "e2", "w1", "w2"))
        hit = sb("hit", [P, 2, TB, NE])
        mask = sb("mask", [P, TB, NE])
        cols = sb("cols", [P, NE, 2, TB])
        number = sb("number", [P, TB, NE])
        rows = sb("rows", [NE, T])
        cnt, nb, end, part = (sb(n, [P, NE]) for n in ("cnt", "nb", "end", "part"))
        before, before_nb = sb("before", [P, MAX_BLOCKS, NE]), sb("before_nb", [P, MAX_BLOCKS, NE])
        eb, sb_ = sb("eb", [P, MAX_BLOCKS]), sb("sb", [P, MAX_BLOCKS])
        with nc.Block() as block:
            @block.sync
            def _(sp):
                sp.dma_start(wr[:], io["moe_router"][0].rearrange("(k p) e -> p k e", p=P)).then_inc(*r_in.up(16))
                sp.wait_ge(*rows_out.at(1))
                sp.dma_start(r["row_dram"], rows[:]).then_inc(*stored.up(16))
                sp.wait_ge(*cols_out.at(1))
                sp.dma_start(r["col_dram"].rearrange("e p c -> p e c"),
                             cols[:].rearrange("p e c b -> p e (c b)")).then_inc(*stored.up(16))
                sp.wait_ge(*stored.at(32))

            @block.gpsimd
            def _(pool):
                for tile, n in ((iota, NE), (iota_b, MAX_BLOCKS), (r["iota_slot"], SL)):
                    pool.iota(tile[:], pattern=[[1, n]], base=0, channel_multiplier=0,
                              allow_small_or_imprecise_dtypes=True).then_inc(*iota_done.up())
                pool.iota(r["slot_of"][:], pattern=[[P, SLB]], base=0, channel_multiplier=1,
                          allow_small_or_imprecise_dtypes=True).then_inc(*iota_done.up())
                pool.tensor_tensor(strict[:], p.tri[:, 0], p.ident[:], ALU.subtract).then_inc(*strict_ready.up())

            @block.tensor
            def _(pe):
                pe.wait_ge(*r_in.at(16))
                for b in range(TB):
                    for k in range(KD):
                        last = pe.matmul(p.psum[:, 0, b * NE:(b + 1) * NE], hT[:, k, b * P:(b + 1) * P], wr[:, k, :],
                                         start=(k == 0), stop=(k == KD - 1))
                last.then_inc(*lg_ps.up())
                for b in range(TB):
                    if b >= 2:
                        pe.wait_ge(*ht_out.at(b - 1))
                    for k in range(KD):
                        last = pe.transpose(p.psum[:, 4 + 2 * (b % 2) + k // 4, (k % 4) * P:(k % 4 + 1) * P],
                                            hT[:, k, b * P:(b + 1) * P], p.ident[:])
                    last.then_inc(*ht_ps.up())
                pe.wait_ge(*mask_ready.at(1))
                pe.wait_ge(*strict_ready.at(1))
                for b in range(TB + 1):
                    for j in range(min(b + 1, TB)):
                        last = pe.matmul(p.psum[:, 1, b * NE:(b + 1) * NE], strict[:] if j == b else p.ones[:],
                                         mask[:, j, :], start=(j == 0), stop=(j == min(b, TB - 1)))
                last.then_inc(*pos_ps.up())
                pe.wait_ge(*made.at(1))
                for b in range(TB):
                    last = pe.transpose(p.psum[0:NE, 2 + b // 4, (b % 4) * P:(b % 4 + 1) * P], number[:, b, :], p.ident[:])
                last.then_inc(*turned.up())

            @block.scalar
            def _(act):
                for b in range(TB):
                    act.wait_ge(*ht_ps.at(b + 1))
                    act.activation(hi[:, b].rearrange("p (a c) -> p a c", a=2),
                                   p.psum[:, 4 + 2 * (b % 2):6 + 2 * (b % 2)], ACT.Copy).then_inc(*ht_hi.up())
                act.wait_ge(*best.at(1))
                act.activation(e2[:], diff[:], ACT.Exp).then_inc(*e2_done.up())

            @block.vector
            def _(dve):
                link = chained(dve_c)
                dve.wait_ge(*lg_ps.at(1))
                link(dve, dve.tensor_copy(lg[:], p.psum[:, 0, 0:TB * NE].rearrange("p (b e) -> p b e", b=TB)))
                for b in range(TB):
                    link(dve, dve.max(top[:, b], lg[:, b]))
                    link(dve, dve.max_index(idx[:, b], top[:, b], lg[:, b]))
                link(dve, dve.tensor_copy(idf[:], idx[:]))
                dve.tensor_tensor(diff[:], top[:, :, 1], top[:, :, 0], ALU.subtract).then_inc(*best.up())
                dve.wait_ge(*iota_done.at(4))
                for n in range(2):
                    link(dve, dve.tensor_tensor(hit[:, n], insert_dim(iota[:], 1, TB),
                                                idf[:, :, n].to_broadcast([P, TB, NE]), ALU.is_equal))
                dve.tensor_tensor(mask[:], hit[:, 0], hit[:, 1], ALU.add).then_inc(*mask_ready.up())
                for b in range(TB):
                    dve.wait_ge(*ht_hi.at(b + 1))
                    dve.tensor_tensor(lo[:, b].rearrange("p (a c) -> p a c", a=2),
                                      p.psum[:, 4 + 2 * (b % 2):6 + 2 * (b % 2)],
                                      hi[:, b].bitcast(F32).rearrange("p (a c) -> p a c", a=2),
                                      ALU.subtract).then_inc(*ht_out.up())
                dve.wait_ge(*e2_done.at(1))
                link(dve, dve.tensor_scalar(w1[:], e2[:], 1.0, None, ALU.add))
                link(dve, dve.reciprocal(w1[:], w1[:]))
                link(dve, dve.tensor_tensor(w2[:], e2[:], w1[:], ALU.mult))
                for n, w in enumerate((w1, w2)):
                    link(dve, dve.tensor_tensor(hit[:, n], hit[:, n], w[:].to_broadcast([P, TB, NE]), ALU.mult))
                link(dve, dve.tensor_tensor(cols[:, :, 1].rearrange("p e b -> p b e"), hit[:, 0], hit[:, 1], ALU.add))
                dve.wait_ge(*pos_ps.at(1))
                link(dve, dve.scalar_tensor_tensor(
                    out=number[:], in0=p.psum[:, 1, 0:TB * NE].rearrange("p (b e) -> p b e", b=TB), scalar=1.0,
                    in1=mask[:], op0=ALU.add, op1=ALU.mult))
                dve.tensor_scalar(number[:], number[:], -1.0, None, ALU.add).then_inc(*made.up())
                dve.wait_ge(*made.at(1))
                dve.tensor_copy(cols[:, :, 0].rearrange("p e b -> p b e"), number[:]).then_inc(*cols_out.up())
                link(dve, dve.tensor_copy(cnt[:], p.psum[:, 1, TB * NE:(TB + 1) * NE]))
                link(dve, dve.tensor_scalar(nb[:], cnt[:], 0.5, None, ALU.is_gt))
                for j in range(1, (T + SL - 1) // SL):
                    link(dve, dve.tensor_scalar(part[:], cnt[:], j * SL + 0.5, None, ALU.is_gt))
                    link(dve, dve.tensor_tensor(nb[:], nb[:], part[:], ALU.add))
                link(dve, dve.tensor_tensor_scan(end[:], p.ones[:, 0:NE], nb[:], 0.0, ALU.mult, ALU.add))
                link(dve, dve.tensor_tensor(before[:], insert_dim(end[:], 1, MAX_BLOCKS),
                                            iota_b[:].to_broadcast([P, MAX_BLOCKS, NE]), ALU.is_le))
                link(dve, dve.tensor_tensor(before_nb[:], before[:], insert_dim(nb[:], 1, MAX_BLOCKS), ALU.mult))
                link(dve, dve.tensor_reduce(eb[:], before[:], AX_X, ALU.add))
                link(dve, dve.tensor_reduce(sb_[:], before_nb[:], AX_X, ALU.add))
                link(dve, dve.tensor_scalar(eb[:], eb[:], float(NE - 1), None, ALU.min))
                link(dve, dve.tensor_tensor(sb_[:], iota_b[:], sb_[:], ALU.subtract))
                link(dve, dve.tensor_scalar(r["first"][:], sb_[:], float(SL), None, ALU.mult))
                link(dve, dve.tensor_copy(r["table"][:, 0:MAX_BLOCKS], eb[0:1, :]))
                link(dve, dve.tensor_copy(r["table"][:, MAX_BLOCKS:MAX_BLOCKS + 1], end[0:1, NE - 1:NE]))
                dve.wait_ge(*turned.at(1))
                link(dve, dve.tensor_copy(rows[:, 0:512], p.psum[0:NE, 2]))
                dve.tensor_copy(rows[:, 512:T], p.psum[0:NE, 3, 0:T - 512]).then_inc(*rows_out.up())
    p.close_stage()


G_PIECES = 2 * FT
PIECES = G_PIECES + KD
SLOT = [i % 4 for i in range(G_PIECES)] + [2, 3, 0, 1, 2, 3, 2, 3]
PAIR = [i % 4 for i in range(G_PIECES)] + [2, 3, 0, 1, 2, 3, 2, 3]


def last_user(table, i):
    for j in range(i - 1, i - 1 - PIECES, -1):
        if table[j % PIECES] == table[i]:
            return j


def stage_sparse_experts(p, l, ht, acc, r):
    nc, io = p.nc, p.io
    sem = lambda name: p.ctx.enter_context(nc.semaphore(f"{name}{l}"))
    RAWS = 3
    raw_in = [sem(f"ex_raw_in{j}") for j in range(RAWS)]
    hi_done, lo_done, piece_done, taken = sem("ex_hi_done"), sem("ex_lo_done"), sem("ex_piece_done"), sem("ex_taken")
    gate_act, hid_ready, chain, zeroed = sem("ex_gate_act"), sem("ex_hid"), sem("ex_dve"), sem("ex_zero")
    routes_in, gather_ready, scatter_ready, comb_kept = sem("ex_routes"), sem("ex_gather_m"), sem("ex_scatter_m"), sem("ex_comb")
    gathered, he_hi_done, he_lo_done = sem("ex_gathered"), sem("ex_he_hi"), sem("ex_he_lo")
    y_turned, y_hi_done, y_lo_done = sem("ex_y_turned"), sem("ex_y_hi"), sem("ex_y_lo")
    scattered, added = sem("ex_scattered"), sem("ex_added")
    SLOTS = 3
    slot_of = [i % SLOTS for i in range(PIECES)]
    GB = KD // 2
    credit = {lo_done: PIECES, piece_done: PIECES, taken: PIECES, gather_ready: 1, scatter_ready: 1, comb_kept: 1,
              gathered: GB, y_lo_done: 4, scattered: TB, added: TB}
    n_link = 2 * FT + 1
    with ExitStack() as own:
        def sb(name, shape, dt=F32):
            return p.sb(f"ex_{name}{l}", shape, dt, ctx=own)
        raw = sb("raw", [P, RAWS, FE])
        wh, wl = sb("wh", [P, SLOTS, FE], F32R), sb("wl", [P, SLOTS, FE], F32R)
        he_hi, he_lo = sb("he_hi", [P, KD, SL], F32R), sb("he_lo", [P, KD, SL], F32R)
        hh, hl = sb("hh", [P, FT, SL], F32R), sb("hl", [P, FT, SL], F32R)
        sg, hf = sb("sg", [P, SL]), sb("hf", [P, SL])
        yT = sb("yT", [P, KD, SL])
        y_hi, y_lo = sb("y_hi", [P, SLB, D], F32R), sb("y_lo", [P, SLB, D], F32R)
        matrix = sb("matrix", [P, TB * SL], F32R)
        take_m = matrix[:].rearrange("p (b s) -> p b s", b=TB)
        give_m = matrix[:].rearrange("p (s t) -> p s t", s=SLB)
        row, col = sb("row", [P, T]), sb("col", [P, 2, TB])
        number, comb = sb("number", [P, TB]), sb("comb", [P, TB])
        spare = sb("spare", [P, 16])
        bank_of = [4 + i % 4 for i in range(PIECES)]

        def size(i):
            return D if i < G_PIECES else FE

        def source(e, i):
            if i < G_PIECES:
                name, f = ("gate", "up")[i % 2], i // 2
                return io[f"moe_w_{name}"][0, bass.ds(e, 1), :, f * P:(f + 1) * P].rearrange("o (k p) c -> p (o k) c", p=P)
            m = i - G_PIECES
            return io["moe_w_down"][0, bass.ds(e, 1), :, m * P:(m + 1) * P].rearrange("o (k p) c -> p (o k) c", p=P)

        def n_blocks(eng):
            return eng.value_load(r["table"][0:1, MAX_BLOCKS:MAX_BLOCKS + 1], min_val=1, max_val=MAX_BLOCKS)

        with nc.Block() as block:
            @block.sync
            def _(sp):
                n = n_blocks(sp)
                with sp.Fori(0, MAX_BLOCKS) as b:
                    with sp.If(b < n):
                        e = sp.value_load(r["table"][0:1, bass.ds(b, 1)], min_val=0, max_val=NE - 1)
                        sp.wait_ge(scatter_ready, b + 1)
                        sp.wait_ge(gather_ready, b + 1)
                        sp.wait_ge(comb_kept, b + 1)
                        sp.dma_start(row[:], r["row_dram"][bass.ds(e, 1)].rearrange("o t -> (o t)").partition_broadcast(P)
                                     ).then_inc(routes_in, 16)
                        sp.dma_start(col[:].rearrange("p c b -> p (c b)"),
                                     r["col_dram"][bass.ds(e, 1)].rearrange("o p c -> p (o c)")).then_inc(routes_in, 16)
                        for i in range(PIECES):
                            sp.wait_ge(lo_done, (b + 1) * PIECES + i - RAWS + 1)
                            sp.dma_start(raw[:, i % RAWS, 0:size(i)].rearrange("p (k c) -> p k c", c=P),
                                         source(e, i)).then_inc(raw_in[i % RAWS], 16)

            @block.scalar
            def _(act):
                n = n_blocks(act)
                with act.Fori(0, MAX_BLOCKS) as b:
                    with act.If(b < n):
                        for i in range(PIECES):
                            act.wait_ge(raw_in[i % RAWS], b * (16 * PIECES // RAWS) + 16 * (i // RAWS + 1))
                            act.wait_ge(piece_done, (b + 1) * PIECES + last_user(slot_of, i) + 1)
                            act.activation(wh[:, slot_of[i], 0:size(i)], raw[:, i % RAWS, 0:size(i)], ACT.Copy).then_inc(hi_done, 1)
                            if i == SLOTS - 1:
                                for j in range(GB):
                                    act.wait_ge(gathered, (b + 1) * GB + j + 1)
                                    act.activation(he_hi[:, 2 * j:2 * j + 2].rearrange("p k s -> p (k s)"),
                                                   p.psum[:, j], ACT.Copy).then_inc(he_hi_done, 1)
                            f = (i - 3) // 2
                            if i % 2 == 1 and 0 <= f < FT:
                                act.wait_ge(piece_done, (b + 1) * PIECES + 2 * f + 1)
                                act.wait_ge(taken, (b + 1) * PIECES + 2 * f)
                                act.activation(sg[:], p.psum[:, bank_of[2 * f], 0:SL], ACT.Silu).then_inc(gate_act, 1)
                        for j in range(4):
                            act.wait_ge(y_turned, 2 * b + j // 2 + 1)
                            half, s = j // 2, j % 2
                            act.activation(y_hi[:, s, half * 512:(half + 1) * 512], p.psum[:, 2 * s + half],
                                           ACT.Copy).then_inc(y_hi_done, 1)

            @block.gpsimd
            def _(pool):
                n = n_blocks(pool)
                with pool.Fori(0, MAX_BLOCKS) as b:
                    with pool.If(b < n):
                        for i in range(PIECES):
                            pool.wait_ge(hi_done, b * PIECES + i + 1)
                            pool.tensor_tensor(wl[:, slot_of[i], 0:size(i)], raw[:, i % RAWS, 0:size(i)],
                                               wh[:, slot_of[i], 0:size(i)].bitcast(F32), ALU.subtract).then_inc(lo_done, 1)

            @block.tensor
            def _(pe):
                n = n_blocks(pe)
                pe.wait_ge(zeroed, len(credit))

                def turn_back(m):
                    for s in range(SLB):
                        last = pe.transpose(p.psum[:, 2 * s + m // 4, (m % 4) * P:(m % 4 + 1) * P],
                                            yT[:, m, s * P:(s + 1) * P], p.ident[:])
                    return last
                with pe.Fori(0, MAX_BLOCKS) as b:
                    with pe.If(b < n):
                        pe.wait_ge(gather_ready, b + 2)
                        pe.wait_ge(y_lo_done, (b + 1) * 4)
                        for k in range(KD):
                            for j in range(TB):
                                for m, part in enumerate(ht):
                                    last = pe.matmul(p.psum[:, k // 2, (k % 2) * SL:(k % 2 + 1) * SL],
                                                     part[:, j, k * P:(k + 1) * P], take_m[:, j],
                                                     start=(j == 0 and m == 0), stop=(j == TB - 1 and m == 1))
                            if k % 2:
                                last.then_inc(gathered, 1)
                        for i in range(PIECES):
                            pe.wait_ge(lo_done, (b + 1) * PIECES + i + 1)
                            if i < 4:
                                pe.wait_ge(added, (b + 1) * TB)
                            pe.wait_ge(taken, (b + 1) * PIECES + last_user(bank_of, i) + 1)
                            if i == 0:
                                pe.wait_ge(he_lo_done, (b + 1) * GB)
                            if i == G_PIECES:
                                pe.wait_ge(hid_ready, (b + 1) * FT)
                            steps = KD if i < G_PIECES else FT
                            mh, ml = (he_hi, he_lo) if i < G_PIECES else (hh, hl)
                            for k in range(steps):
                                cols = slice(k * P, (k + 1) * P)
                                for j, (w, m) in enumerate(((wh, mh), (wh, ml), (wl, mh))):
                                    last = pe.matmul(p.psum[:, bank_of[i], 0:SL], w[:, slot_of[i], cols], m[:, k],
                                                     start=(k == 0 and j == 0), stop=(k == steps - 1 and j == 2))
                            last.then_inc(piece_done, 1)
                            m = i - G_PIECES
                            if m >= 1:
                                pe.wait_ge(taken, (b + 1) * PIECES + G_PIECES + m)
                                last = turn_back(m - 1)
                                if m - 1 == 3:
                                    last.then_inc(y_turned, 1)
                        pe.wait_ge(taken, (b + 1) * PIECES + PIECES)
                        turn_back(KD - 1).then_inc(y_turned, 1)
                        pe.wait_ge(scatter_ready, b + 2)
                        pe.wait_ge(y_lo_done, (b + 1) * 4 + 4)
                        for j in range(TB):
                            pe.wait_ge(added, (b + 1) * TB + j - 1)
                            for half in range(2):
                                for s in range(SLB):
                                    for m, part in enumerate((y_hi, y_lo)):
                                        last = pe.matmul(p.psum[:, 4 + 2 * (j % 2) + half], give_m[:, s, j * P:(j + 1) * P],
                                                         part[:, s, half * 512:(half + 1) * 512],
                                                         start=(s == 0 and m == 0), stop=(s == SLB - 1 and m == 1))
                            last.then_inc(scattered, 1)

            @block.vector
            def _(dve):
                dve.memset(acc[:], 0.0).then_inc(chain, 1)
                dve.wait_ge(chain, 1)
                for j, (signal, count) in enumerate(credit.items()):
                    dve.memset(spare[:, j:j + 1], 0.0).then_inc(signal, count)
                dve.engine_nop().then_inc(zeroed, len(credit))
                n = n_blocks(dve)
                with dve.Fori(0, MAX_BLOCKS) as b:
                    with dve.If(b < n):
                        links = 1

                        def link(ins):
                            nonlocal links
                            ins.then_inc(chain, 1)
                            links += 1
                            dve.wait_ge(chain, b * n_link + links)
                        dve.wait_ge(routes_in, 32 * b + 32)
                        dve.wait_ge(scattered, (b + 1) * TB)
                        link(dve.tensor_scalar(number[:], col[:, 0], r["first"][:, bass.ds(b, 1)], None, ALU.subtract))
                        for j in range(TB):
                            last = dve.tensor_scalar(take_m[:, j], r["iota_slot"][:], number[:, j:j + 1], None, ALU.is_equal)
                        last.then_inc(gather_ready, 1)
                        dve.tensor_copy(comb[:], col[:, 1]).then_inc(comb_kept, 1)
                        for j in range(GB):
                            dve.wait_ge(he_hi_done, b * GB + j + 1)
                            part = slice(2 * j, 2 * j + 2)
                            dve.tensor_tensor(he_lo[:, part].rearrange("p k s -> p (k s)"), p.psum[:, j],
                                              he_hi[:, part].bitcast(F32).rearrange("p k s -> p (k s)"),
                                              ALU.subtract).then_inc(he_lo_done, 1)
                        for i in range(PIECES):
                            if i < G_PIECES and i % 2 == 0:
                                continue
                            dve.wait_ge(piece_done, (b + 1) * PIECES + i + 1)
                            res = p.psum[:, bank_of[i], 0:SL]
                            if i < G_PIECES:
                                f = i // 2
                                dve.wait_ge(gate_act, b * FT + f + 1)
                                ins = dve.tensor_tensor(hf[:], res, sg[:], ALU.mult)
                                link(ins)
                                link(dve.tensor_copy(hh[:, f], hf[:]))
                                dve.tensor_tensor(hl[:, f], hf[:], hh[:, f].bitcast(F32), ALU.subtract).then_inc(hid_ready, 1)
                                dve.wait_ge(hid_ready, b * FT + f + 1)
                                dve.engine_nop().then_inc(taken, 2)
                            else:
                                dve.tensor_copy(yT[:, i - G_PIECES], res).then_inc(taken, 1)
                            if i == 5:
                                for s in range(SLB):
                                    last = dve.tensor_scalar(give_m[:, s], row[:], r["first"][:, bass.ds(b, 1)],
                                                             r["slot_of"][:, s:s + 1], ALU.subtract, ALU.is_equal)
                                last.then_inc(scatter_ready, 1)
                        for j in range(4):
                            half, s = j // 2, j % 2
                            dve.wait_ge(y_hi_done, 4 * b + j + 1)
                            cols = slice(half * 512, (half + 1) * 512)
                            dve.tensor_tensor(y_lo[:, s, cols], p.psum[:, 2 * s + half], y_hi[:, s, cols].bitcast(F32),
                                              ALU.subtract).then_inc(y_lo_done, 1)
                        dve.wait_ge(comb_kept, b + 2)
                        for j in range(TB):
                            dve.wait_ge(scattered, (b + 1) * TB + j + 1)
                            a = acc[:, j].rearrange("p (a c) -> p a c", a=2)
                            dve.scalar_tensor_tensor(out=a, in0=p.psum[:, 4 + 2 * (j % 2):6 + 2 * (j % 2)],
                                                     scalar=comb[:, j:j + 1], in1=a, op0=ALU.mult,
                                                     op1=ALU.add).then_inc(added, 1)
    p.close_stage()


def stage_experts(p, l, hi, lo, acc, comb_dram):
    nc, io = p.nc, p.io
    moe = comb_dram is not None
    n_exp = NE if moe else 2
    sem = lambda name: p.ctx.enter_context(nc.semaphore(f"{name}{l}"))
    raw_in = [sem(f"ex_raw_in{r}") for r in range(2)]
    hi_done, lo_done, piece_done, taken = sem("ex_hi_done"), sem("ex_lo_done"), sem("ex_piece_done"), sem("ex_taken")
    gate_act, hid_ready, comb_in, chain, zeroed = sem("ex_gate_act"), sem("ex_hid"), sem("ex_comb"), sem("ex_dve"), sem("ex_zero")
    n_link = FT * (3 if moe else 2)
    with ExitStack() as own:
        def sb(name, shape, dt=F32):
            return p.sb(f"ex_{name}{l}", shape, dt, ctx=own)
        raw = sb("raw", [P, 2, FE])
        wh, wl = sb("wh", [P, 4, FE], F32R), sb("wl", [P, 4, FE], F32R)
        hh, hl = sb("hh", [P, FT, T], F32R), sb("hl", [P, FT, T], F32R)
        sg, hf = sb("sg", [P, T]), sb("hf", [P, T])
        ce = sb("ce", [P, T]) if moe else None

        def size(i):
            return D if i < G_PIECES else FE

        def source(e, i):
            if i < G_PIECES:
                name, f = ("gate", "up")[i % 2], i // 2
                if moe:
                    return io[f"moe_w_{name}"][0, bass.ds(e, 1), :, f * P:(f + 1) * P].rearrange("o (k p) c -> p (o k) c", p=P)
                return io[f"ffn_w_{name}"][0, :, bass.ds(e * FE + f * P, P)].rearrange("(k p) c -> p k c", p=P)
            m = i - G_PIECES
            if moe:
                return io["moe_w_down"][0, bass.ds(e, 1), :, m * P:(m + 1) * P].rearrange("o (k p) c -> p (o k) c", p=P)
            return io["ffn_w_down"][0, bass.ds(e * FE, FE), m * P:(m + 1) * P].rearrange("(k p) c -> p k c", p=P)

        with nc.Block() as block:
            @block.sync
            def _(sp):
                with sp.Fori(0, n_exp) as e:
                    for i in range(PIECES):
                        if moe and i == 1:
                            sp.wait_ge(taken, (e + 1) * PIECES)
                            sp.dma_start(ce[:], comb_dram[bass.ds(e, 1)].rearrange("o t -> (o t)").partition_broadcast(P)
                                         ).then_inc(comb_in, 16)
                        sp.wait_ge(lo_done, (e + 1) * PIECES + i - 1)
                        sp.dma_start(raw[:, i % 2, 0:size(i)].rearrange("p (k c) -> p k c", c=P),
                                     source(e, i)).then_inc(raw_in[i % 2], 16)

            @block.scalar
            def _(act):
                with act.Fori(0, n_exp) as e:
                    for i in range(PIECES):
                        act.wait_ge(raw_in[i % 2], e * (8 * PIECES) + 16 * (i // 2 + 1))
                        act.wait_ge(piece_done, (e + 1) * PIECES + last_user(SLOT, i) + 1)
                        act.activation(wh[:, SLOT[i], 0:size(i)], raw[:, i % 2, 0:size(i)], ACT.Copy).then_inc(hi_done, 1)
                        f = (i - 3) // 2
                        if i % 2 == 1 and 0 <= f < FT:
                            act.wait_ge(piece_done, (e + 1) * PIECES + 2 * f + 1)

                            act.wait_ge(taken, (e + 1) * PIECES + 2 * f)
                            act.activation(sg[:].rearrange("p (a c) -> p a c", a=2),
                                           p.psum[:, 2 * PAIR[2 * f]:2 * PAIR[2 * f] + 2, 0:HT],
                                           ACT.Silu).then_inc(gate_act, 1)

            @block.gpsimd
            def _(pool):
                with pool.Fori(0, n_exp) as e:
                    for i in range(PIECES):
                        pool.wait_ge(hi_done, e * PIECES + i + 1)
                        ins = pool.tensor_tensor(wl[:, SLOT[i], 0:size(i)], raw[:, i % 2, 0:size(i)],
                                                 wh[:, SLOT[i], 0:size(i)].bitcast(F32), ALU.subtract)
                        ins.then_inc(lo_done, 1)

            @block.tensor
            def _(pe):
                pe.wait_ge(zeroed, 1)
                with pe.Fori(0, n_exp) as e:
                    for i in range(PIECES):
                        pe.wait_ge(lo_done, (e + 1) * PIECES + i + 1)
                        pe.wait_ge(taken, (e + 1) * PIECES + last_user(PAIR, i) + 1)
                        if i == G_PIECES:
                            pe.wait_ge(hid_ready, (e + 1) * FT)
                        steps = KD if i < G_PIECES else FT
                        mh, ml = (hi, lo) if i < G_PIECES else (hh, hl)
                        for k in range(steps):
                            cols = slice(k * P, (k + 1) * P)
                            for n, (w, m) in enumerate(((wh, mh), (wh, ml), (wl, mh))):
                                for half in range(2):
                                    last = pe.matmul(p.psum[:, 2 * PAIR[i] + half, 0:HT], w[:, SLOT[i], cols],
                                                     m[:, k, half * HT:(half + 1) * HT],
                                                     start=(k == 0 and n == 0), stop=(k == steps - 1 and n == 2))
                        last.then_inc(piece_done, 1)

            @block.vector
            def _(dve):
                dve.memset(acc[:], 0.0).then_inc(zeroed, 1)
                dve.wait_ge(zeroed, 1)
                dve.memset(sg[:, 0:1], 0.0).then_inc(lo_done, PIECES)
                dve.memset(sg[:, 1:2], 0.0).then_inc(piece_done, PIECES)
                dve.memset(sg[:, 2:3], 0.0).then_inc(taken, PIECES)
                with dve.Fori(0, n_exp) as e:
                    links = 0

                    def link(ins):
                        nonlocal links
                        links += 1
                        ins.then_inc(chain, 1)
                        dve.wait_ge(chain, e * n_link + links)
                    if moe:
                        dve.wait_ge(comb_in, (e + 1) * 16)
                    for i in range(PIECES):
                        if i < G_PIECES and i % 2 == 0:
                            continue
                        dve.wait_ge(piece_done, (e + 1) * PIECES + i + 1)
                        halves = p.psum[:, 2 * PAIR[i]:2 * PAIR[i] + 2, 0:HT]
                        if i < G_PIECES:
                            f = i // 2
                            dve.wait_ge(gate_act, e * FT + f + 1)
                            ins = dve.tensor_tensor(hf[:].rearrange("p (a c) -> p a c", a=2), halves,
                                                    sg[:].rearrange("p (a c) -> p a c", a=2), ALU.mult)
                            link(ins)
                            if moe:
                                link(dve.tensor_tensor(hf[:], hf[:], ce[:], ALU.mult))
                            link(dve.tensor_copy(hh[:, f], hf[:]))
                            dve.tensor_tensor(hl[:, f], hf[:], hh[:, f].bitcast(F32), ALU.subtract).then_inc(hid_ready, 1)
                            dve.wait_ge(hid_ready, e * FT + f + 1)
                            dve.engine_nop().then_inc(taken, 2)
                        else:
                            m = acc[:, i - G_PIECES].rearrange("p (a c) -> p a c", a=2)
                            dve.tensor_tensor(m, m, halves, ALU.add).then_inc(taken, 1)
    p.close_stage()


def stage_ffn_out(p, l, acc, token_major):
    nc, io = p.nc, p.io
    gr_ps, gr_ev, mm, sq2, m2, r2, res = (p.sig(n) for n in (
        "gate_ps", "gate_out", "out_ps", "out_squares", "out_mean", "out_root", "residual"))
    dve_c = p.sig("dve_chain")
    with ExitStack() as own:
        def sb(name, shape):
            return p.sb(f"fo_{name}{l}", shape, ctx=own)
        junk, rows, upd = sb("junk", [P, 512]), sb("rows", [P, 2, D]), sb("upd", [P, 2, D])
        stat2, rstd2 = sb("stat2", [P, TB, 2]), sb("rstd2", [P, TB])

        def source(b):
            if token_major:
                return acc[:, b].rearrange("p (a c) -> p a c", a=2)
            return p.psum[:, 4 + 2 * (b % 2):6 + 2 * (b % 2)]
        with nc.Block() as block:
            @block.scalar
            def _(act):
                for b in range(TB):
                    if not token_major:
                        act.wait_ge(*mm.at(b + 1))
                    for half in range(2):
                        act.activation(junk[:], source(b)[:, half], ACT.Square,
                                       accum_out=stat2[:, b, half:half + 1]).then_inc(*sq2.up())
                        act.wait_ge(*sq2.at(2 * b + half + 1))
                    act.wait_ge(*m2.at(b + 1))
                    act.activation(rstd2[:, b:b + 1], stat2[:, b, 0:1], ACT.Sqrt).then_inc(*r2.up())

            @block.tensor
            def _(pe):
                gate_rows(p, pe, l, 1, gr_ps, gr_ev)
                for b in range(0 if token_major else TB):
                    if b >= 2:
                        pe.wait_ge(*res.at(b - 1))
                    for k in range(KD):
                        last = pe.transpose(p.psum[:, 4 + 2 * (b % 2) + k // 4, (k % 4) * P:(k % 4 + 1) * P],
                                            acc[:, k, b * P:(b + 1) * P], p.ident[:])
                    last.then_inc(*mm.up())

            @block.vector
            def _(dve):
                link = chained(dve_c)
                dve.wait_ge(*gr_ps.at(1))
                link(dve, dve.tensor_copy(rows[:].rearrange("p s (a c) -> p (s a) c", a=2), p.psum[:, 0:4]))
                for b in range(TB):
                    take_residual(p, dve, link, b, source(b), rows, upd,
                                  stat2, rstd2, sq2, m2, r2, res)
    p.close_stage()


def stage_store(p):
    nc, io = p.nc, p.io
    out = p.sig("y_stored")
    with nc.Block() as block:
        @block.sync
        def _(sp):
            sp.dma_start(io["y_sample"].rearrange("o (b p) d -> p (o b) d", p=P), p.x[:, 0:LB]).then_inc(*out.up(16))
            sp.dma_start(io["y_prompt"].rearrange("o p d -> p (o d)"), p.x[:, LB]).then_inc(*out.up(16))
            sp.wait_ge(*out.at(32))
    p.close_stage()


DBG = None


def build(nc, io):
    with ExitStack() as ctx:
        p = Program(nc, io, ctx)
        row_dram = nc.dram_tensor("token_numbers", (NE, T), F32, kind="Internal").ap()
        col_dram = nc.dram_tensor("token_columns", (NE, P, 2 * TB), F32, kind="Internal").ap()
        stage_setup(p)
        stage_first_modulation(p)
        for l in range(2):
            with ExitStack() as mixer:
                def sb(name, shape, where=mixer):
                    return p.sb(f"mx_{name}{l}", shape, ctx=where)
                t = {"z": sb("z", [P, TB, SSDW]), "dtcq": sb("dtcq", [P, TB, 2 * NH + QR]),
                     "ckr": sb("ckr", [P, TB, KVR + ROPE]), "pad": sb("pad", [P, XF, PADW]),
                     "xst": sb("xst", [P, TB, SSDW]), "qkv_room": sb("qkv_room", [P, NH * KEYS])}
                t["y_ssd"] = t["z"]
                t["o"] = t["xst"]
                with ExitStack() as inner:
                    hT = p.sb(f"hT{l}", [P, KD, T], ctx=inner)
                    stage_pre_norm(p, l, 0, hT)
                    stage_in_proj(p, l, hT, t)
                stage_ssd(p, l, t)
                stage_attention(p, l, t)
                stage_out_proj(p, l, t)
            with ExitStack() as ffn:
                if l % 2 == 0:
                    acc = p.sb(f"acc{l}", [P, KD, T], ctx=ffn)
                    with ExitStack() as inner:
                        hi = p.sb(f"h_hi{l}", [P, KD, T], F32R, ctx=inner)
                        lo = p.sb(f"h_lo{l}", [P, KD, T], F32R, ctx=inner)
                        stage_pre_norm(p, l, 1, None, (hi, lo))
                        stage_experts(p, l, hi, lo, acc, None)
                else:
                    acc = p.sb(f"acc{l}", [P, TB, D], ctx=ffn)
                    with ExitStack() as inner:
                        ht = [p.sb(f"ht_{n}{l}", [P, TB, D], F32R, ctx=inner) for n in ("hi", "lo")]
                        r = {"iota_slot": p.sb("iota_slot", [P, SL], ctx=inner),
                             "slot_of": p.sb("slot_of", [P, SLB], ctx=inner),
                             "first": p.sb("first", [P, MAX_BLOCKS], ctx=inner),
                             "table": p.sb("table", [1, MAX_BLOCKS + 4], I32, ctx=inner),
                             "row_dram": row_dram, "col_dram": col_dram}
                        with ExitStack() as norm:
                            hT = p.sb(f"hTf{l}", [P, KD, T], ctx=norm)
                            stage_pre_norm(p, l, 1, hT)
                            stage_router(p, l, hT, ht, r)
                        stage_sparse_experts(p, l, ht, acc, r)
                stage_ffn_out(p, l, acc, token_major=(l % 2 == 1))
        stage_store(p)


def rope_tables():
    import numpy as np
    rows = LAT // 64
    row = np.repeat(np.arange(rows, dtype=np.float32), 64)
    col = np.tile(np.arange(64, dtype=np.float32), rows)
    half = ROPE // 2
    inv = (np.float32(10000.0) ** (-np.arange(0, half, 2, dtype=np.float32) / half)).astype(np.float32)
    ar, ac = row[:, None] * inv[None, :], col[:, None] * inv[None, :]
    ang = np.concatenate([ar, ar, ac, ac], axis=-1).astype(np.float32)
    sign = np.repeat(np.array([-1, 1, -1, 1], np.float32), half // 2)
    return np.cos(ang).astype(np.float32), (np.sin(ang) * sign).astype(np.float32)


_OUTS = {"y_prompt": (1, CTX, D), "y_sample": (1, LAT, D), "new_ckv": (1, 2, CTX, KVR),
         "new_krope": (1, 2, CTX, ROPE), "new_ssm": (1, 2, 2, NH, HD, NS)}


def kernel(**inputs):
    import numpy as np
    import concourse.bacc as _bacc
    from concourse.bass_utils import run_bass_kernel_spmd as _run

    nc = _bacc.Bacc("TRN2", target_bir_lowering=False, num_devices=1)
    arrays = {k: np.ascontiguousarray(v) for k, v in inputs.items()}
    arrays["rope_cos"], arrays["rope_sin"] = rope_tables()
    io = {}
    for name, a in arrays.items():
        io[name] = nc.dram_tensor(name, a.shape, mybir.dt.from_np(a.dtype), kind="ExternalInput").ap()
    for name, shape in _OUTS.items():
        io[name] = nc.dram_tensor(f"out_{name}", shape, F32, kind="ExternalOutput").ap()
    build(nc, io)
    r = _run(nc, [arrays], core_ids=[0])
    return tuple(r.results[0][f"out_{name}"] for name in _OUTS)
```

```python
from contextlib import ExitStack

import concourse.bass as bass
from concourse import mybir

F32 = mybir.dt.float32
F32R = mybir.dt.float32r
U32 = mybir.dt.uint32
ALU = mybir.AluOpType
ACT = mybir.ActivationFunctionType
AX_X = mybir.AxisListType.X

P = 128
D = 1024
KD = D // P
LAT = 512
CTX = 128
T = LAT + CTX
TB = T // P
LB = LAT // P
HT = T // 2
SEQ_OF = [0] * LB + [1]
SSDW, NH, HD, NG, NS = 512, 8, 64, 2, 64
XBC = SSDW + 2 * NG * NS
XF = XBC // P
TAPS = 5
PADW = 2 + LAT + 2 + 2 + CTX + 2
QR, KVR, ROPE, NOPE, VD = 384, 256, 32, 64, 64
QD = NOPE + ROPE
PAST = 128
KEYS = PAST + T
KB = KEYS // P
C_DT = SSDW + XBC
C_CQ = C_DT + 2 * NH
C_KV = C_CQ + QR
C_KR = C_KV + KVR
IN_COLS = C_KR + ROPE
NMOD = 6
FE = 1408
FT = FE // P
NE = 8
EPS = 1e-6
SCALE = float(QD) ** -0.5
FAR = -1e30


class Signal:

    def __init__(self, nc, ctx, name):
        self.sem = ctx.enter_context(nc.semaphore(name))
        self.base = 0
        self.sent = 0

    def up(self, n=1):
        self.sent += n
        return self.sem, n

    def at(self, n):
        return self.sem, self.base + n

    def close(self):
        self.base, self.sent = self.base + self.sent, 0


def insert_dim(ap, at, n):
    dims = [list(d) for d in ap.ap]
    dims.insert(at, [0, n])
    return bass.AP(tensor=ap.tensor, offset=ap.offset, ap=dims)


class Program:
    def __init__(self, nc, io, ctx):
        self.nc, self.io, self.ctx = nc, io, ctx
        self.signals = {}
        self.stream_signals = [Signal(nc, ctx, n) for n in ("win_landed_even", "win_landed_odd", "win_hi_done",
                                                            "win_lo_done")]
        self.stage_no = 0
        sb = self.sb
        self.psum = ctx.enter_context(nc.psum_tensor("psum", [P, 8, 512], F32))
        self.x = sb("x", [P, TB, D])
        self.ident = sb("ident", [P, P])
        self.ones = sb("ones", [P, P])
        self.tri = sb("tri", [P, 2, P])
        self.far = sb("far", [P, 2, P])
        self.silu_c = sb("silu_c", [P, KD, 2])
        self.pair_sum = sb("pair_sum", [4, 2])
        self.mod = sb("mod", [P, 2, NMOD * KD, 2])
        self.b_mod = sb("b_mod_t", [P, 2, NMOD * KD])
        self.gains = sb("gains", [P, 2, 4, KD])
        self.scale_in = sb("scale_in", [P, 2, 2, KD, 2])
        self.gate_out = sb("gate_out", [P, 2, 2, KD, 2])
        self.stat = sb("stat", [P, TB])
        self.rstd = sb("rstd", [P, TB])

    def sb(self, name, shape, dt=F32, ctx=None):
        return (ctx or self.ctx).enter_context(self.nc.sbuf_tensor(name, shape, dt))

    def sig(self, name):
        if name not in self.signals:
            self.signals[name] = Signal(self.nc, self.ctx, name)
        return self.signals[name]

    def close_stage(self):
        for s in self.signals.values():
            s.close()


def chained(signal):
    count = [0]

    def link(eng, ins):
        count[0] += 1
        ins.then_inc(*signal.up())
        eng.wait_ge(*signal.at(count[0]))
    return link


def stage_setup(p):
    nc, io = p.nc, p.io
    c_in = p.sig("c_in")
    consts, pool_chain, silu_done = p.sig("consts"), p.sig("pool_chain"), p.sig("silu_done")
    with nc.Block() as block:
        @block.sync
        def _(sp):
            with nc.allow_non_contiguous_dma(reason="2048 conditioning values, one per partition row"):
                sp.dma_start(p.silu_c[:, :, 0], io["c"].rearrange("o (k p) -> p (o k)", p=P)).then_inc(*c_in.up(16))
                sp.dma_start(p.silu_c[:, :, 1], io["c_ctx"].rearrange("(k p) -> p k", p=P)).then_inc(*c_in.up(16))

        @block.gpsimd
        def _(pool):
            link = chained(pool_chain)
            pool.memset(p.ident[:], 0.0)
            pool.memset(p.ones[:], 1.0)
            pool.memset(p.tri[:], 1.0)
            link(pool, pool.memset(p.far[:], 0.0))
            pool.affine_select(out=p.ident[:], in_=p.ident[:], compare_op=ALU.not_equal, fill=1.0, base=0,
                               pattern=[[-1, P]], channel_multiplier=1)
            for tile, fill in ((p.tri, 0.0), (p.far, FAR)):
                pool.affine_select(out=tile[:, 0], in_=tile[:, 0], compare_op=ALU.is_ge, fill=fill, base=0,
                                   pattern=[[1, P]], channel_multiplier=-1)
                last = pool.affine_select(out=tile[:, 1], in_=tile[:, 1], compare_op=ALU.is_ge, fill=fill, base=0,
                                          pattern=[[-1, P]], channel_multiplier=1)
            last.then_inc(*consts.up())

        @block.scalar
        def _(act):
            act.wait_ge(*c_in.at(32))
            act.activation(p.silu_c[:], p.silu_c[:], ACT.Silu).then_inc(*silu_done.up())
            act.wait_ge(*silu_done.at(1))
    p.close_stage()


UNIT = 512
UNITS = NMOD * D // UNIT
QUARTERS = 4
QK = KD // QUARTERS
UNIT_STEPS = QUARTERS + 1


class Modulation:

    def __init__(self, p, units, bank, own, tag, ring, split):
        self.p, self.units, self.bank, self.ring, self.split = p, units, bank, ring, split
        if units:
            slots = [P, ring, QK * UNIT]
            self.w = p.sb(f"wmod_{tag}", slots, ctx=own)
            self.hi = p.sb(f"wmod_hi_{tag}", slots, F32R, ctx=own) if split else None
            self.lo = p.sb(f"wmod_lo_{tag}", slots, F32R, ctx=own) if split else None
            self.rows = 4 if split else 2
            self.row = p.sb(f"modrow_{tag}", [self.rows, UNIT], ctx=own)
        self.landed = [p.sig(f"weights_landed{r}") for r in range(4)]
        self.used, self.row_out, self.turned, self.taken, self.hi_done, self.lo_done = (p.sig(n) for n in (
            "wmod_used", "mod_row_out", "mod_turned", "mod_taken", "weights_hi", "weights_lo"))
        self.steps = [(kind, n) for n in range(len(units)) for kind in [*range(QUARTERS), "t"]]
        self.quarters = range(QUARTERS * len(units))

    def load(self, sp):
        for i in self.quarters:
            (l, u), q = self.units[i // QUARTERS], i % QUARTERS
            if i >= self.ring:
                sp.wait_ge(*(self.lo_done if self.split else self.used).at(i - self.ring + 1))
            sp.dma_start(self.w[:, i % self.ring].rearrange("p (k f) -> p k f", k=QK),
                         self.p.io["w_mod"][l, q * QK * P:(q + 1) * QK * P, u * UNIT:(u + 1) * UNIT].rearrange(
                             "(k p) f -> p k f", p=P)).then_inc(*self.landed[i % self.ring].up(16))

    def on_scalar(self, act, i):
        slot = i % self.ring
        act.wait_ge(*self.landed[slot].at(16 * (i // self.ring + 1)))
        if i >= self.ring:
            act.wait_ge(*self.used.at(i - self.ring + 1))
        act.activation(self.hi[:, slot], self.w[:, slot], ACT.Copy).then_inc(*self.hi_done.up())

    def on_gpsimd(self, pool):
        for i in self.quarters:
            slot = i % self.ring
            pool.wait_ge(*self.hi_done.at(i + 1))
            pool.tensor_tensor(self.lo[:, slot], self.w[:, slot], self.hi[:, slot].bitcast(F32),
                               ALU.subtract).then_inc(*self.lo_done.up())

    def on_tensor(self, pe, step):
        p, (kind, n) = self.p, self.steps[step]
        if kind == "t":
            pe.wait_ge(*self.row_out.at(n + 1))
            for j in range(UNIT // P):
                last = pe.matmul(p.psum[:, self.bank, 2 * j:2 * j + 2], self.row[:, j * P:(j + 1) * P],
                                 p.pair_sum[:] if self.split else p.ident[0:2, 0:2], start=True, stop=True)
            last.then_inc(*self.turned.up())
            return
        i = QUARTERS * n + kind
        if self.split:
            pe.wait_ge(*self.lo_done.at(i + 1))
        else:
            pe.wait_ge(*self.landed[i % self.ring].at(16 * (i // self.ring + 1)))
        if kind == 0 and n >= 1:
            pe.wait_ge(*self.taken.at(n))
        tiles = (self.hi, self.lo) if self.split else (self.w,)
        for k in range(QK):
            for j, tile in enumerate(tiles):
                c = p.silu_parts[:, kind * QK + k, :] if self.split else p.silu_c[:, kind * QK + k, :]
                out = p.psum[:, self.bank, :] if self.split else p.psum[0:2, self.bank, :]
                last = pe.matmul(out, c, tile[:, i % self.ring, k * UNIT:(k + 1) * UNIT],
                                 start=(kind == 0 and k == 0 and j == 0),
                                 stop=(kind == QUARTERS - 1 and k == QK - 1 and j == len(tiles) - 1))
        last.then_inc(*self.used.up())

    def on_vector(self, dve, step):
        p, (kind, n) = self.p, self.steps[step]
        l, u = self.units[n]
        if kind == QUARTERS - 1:
            dve.wait_ge(*self.used.at(QUARTERS * (n + 1)))
            dve.tensor_copy(self.row[:], p.psum[0:self.rows, self.bank, :]).then_inc(*self.row_out.up())
        elif kind == "t":
            dve.wait_ge(*self.turned.at(n + 1))
            per = UNIT // P
            dve.tensor_tensor(p.mod[:, l, u * per:(u + 1) * per, :],
                              p.psum[:, self.bank, 0:2 * per].rearrange("p (m s) -> p m s", s=2),
                              p.b_mod[:, l, u * per:(u + 1) * per].to_broadcast([P, per, 2]),
                              ALU.add).then_inc(*self.taken.up())

    def vectors(self, dve, link, l, which, kinds):
        p = self.p
        if self.units:
            dve.wait_ge(*self.taken.at(len(self.units)))
        if "scale" in kinds:
            scale = p.mod[:, l, (3 * which + 1) * KD:(3 * which + 2) * KD, :]
            link(dve, dve.scalar_tensor_tensor(
                out=p.scale_in[:, l, which], in0=scale, scalar=1.0,
                in1=p.gains[:, l, 2 * which].to_broadcast([P, KD, 2]), op0=ALU.add, op1=ALU.mult))
        if "gate" in kinds:
            gate = p.mod[:, l, (3 * which + 2) * KD:(3 * which + 3) * KD, :]
            link(dve, dve.tensor_tensor(p.gate_out[:, l, which], gate,
                                        p.gains[:, l, 2 * which + 1].to_broadcast([P, KD, 2]), ALU.mult))


def modulation_units(l):
    first = 2 * D // UNIT
    units = [(l, u) for u in range(first, UNITS)] + ([(1, u) for u in range(first)] if l == 0 else [])
    return units[0:2 + TB], units[2 + TB:]


def stage_first_modulation(p):
    nc, io = p.nc, p.io
    x_in, small, dve_c = p.sig("x_in"), p.sig("mod_small"), p.sig("dve_chain")
    with ExitStack() as own:
        mod = Modulation(p, [(0, u) for u in range(2 * D // UNIT)], 0, own, "first", 4, False)
        with nc.Block() as block:
            @block.sync
            def _(sp):
                mod.load(sp)

            @block.scalar
            def _(act):
                with nc.allow_non_contiguous_dma(reason="bias and gains, feature-major"):
                    for l in range(2):
                        act.dma_start(p.b_mod[:, l], io["b_mod"][l].rearrange("(k p) -> p k", p=P)).then_inc(*small.up(16))
                        for j, name in enumerate(("norm_pre_mix", "norm_post_mix", "norm_pre_ffn", "norm_post_ffn")):
                            act.dma_start(p.gains[:, l, j], io[name][l].rearrange("(k p) -> p k", p=P)
                                          ).then_inc(*small.up(16))
                act.dma_start(p.x[:, 0:LB], io["x_sample"].rearrange("o (b p) d -> p (o b) d", p=P)).then_inc(*x_in.up(16))
                act.dma_start(p.x[:, LB], io["x_prompt"].rearrange("o p d -> p (o d)")).then_inc(*x_in.up(16))
                act.wait_ge(*x_in.at(32))

            @block.tensor
            def _(pe):
                for step in range(len(mod.steps)):
                    mod.on_tensor(pe, step)

            @block.vector
            def _(dve):
                link = chained(dve_c)
                dve.tensor_tensor(p.pair_sum[:], p.ident[0:4, 0:2], p.ident[0:4, 2:4], ALU.add)
                dve.wait_ge(*small.at(160))
                for step in range(len(mod.steps)):
                    mod.on_vector(dve, step)
                mod.vectors(dve, link, 0, 0, ("scale",))
    p.close_stage()


def stage_pre_norm(p, l, which, hT, split=None, weights=None, clear=None):
    nc = p.nc
    sq, mean, root, xn, tr, ev, far_ev, far_hi, far_lo = (p.sig(n) for n in (
        "pn_squares", "pn_mean", "pn_root", "pn_scaled", "pn_turned", "pn_evicted", "pn_far_out", "weights_hi",
        "weights_lo"))
    dve_c = p.sig("dve_chain")
    with ExitStack() as own:
        junk = p.sb(f"pn_junk{l}{which}", [P, D], ctx=own)
        xs = p.sb(f"pn_x{l}{which}", [P, 2, D], ctx=own)
        hf = p.sb(f"pn_h{l}{which}", [P, 2, KD, P], ctx=own) if split else None
        with nc.Block() as block:
            if weights:
                @block.sync
                def _(sp):
                    for i in range(2):
                        weights.load(sp, i)

            def of_block(tile, b, part):
                return tile[:, part, b * P:(b + 1) * P]

            near, far_ = slice(0, KD // 2), slice(KD // 2, KD)

            @block.scalar
            def _(act):
                for b in range(TB):
                    ins = act.activation(junk[:], p.x[:, b], ACT.Square, accum_out=p.stat[:, b:b + 1])
                    ins.then_inc(*sq.up())
                    act.wait_ge(*sq.at(b + 1))
                act.wait_ge(*mean.at(1))
                act.activation(p.rstd[:], p.stat[:], ACT.Sqrt).then_inc(*root.up())
                for b in range(TB):
                    s = SEQ_OF[b]
                    act.wait_ge(*tr.at(b + 1))
                    if split and b >= 2:
                        act.wait_ge(*far_lo.at(b - 1))
                    for k in range(KD // 2, KD):
                        out = hf[:, b % 2, k] if split else hT[:, k, b * P:(b + 1) * P]
                        last = act.activation(
                            out, p.psum[:, 2 * (b % 4) + k // 4, (k % 4) * P:(k % 4 + 1) * P], ACT.Identity,
                            scale=p.scale_in[:, l, which, k, s:s + 1], bias=p.mod[:, l, 3 * which * KD + k, s:s + 1])
                    last.then_inc(*far_ev.up())
                    if split:
                        act.wait_ge(*far_ev.at(b + 1))
                        act.activation(of_block(split[0], b, far_), hf[:, b % 2, far_], ACT.Copy).then_inc(*far_hi.up())

            @block.tensor
            def _(pe):
                for b in range(TB):
                    pe.wait_ge(*xn.at(b + 1))
                    if b >= 4:
                        pe.wait_ge(*ev.at(b - 3))
                        pe.wait_ge(*far_ev.at(b - 3))
                    for k in range(KD):
                        last = pe.transpose(p.psum[:, 2 * (b % 4) + k // 4, (k % 4) * P:(k % 4 + 1) * P],
                                            xs[:, b % 2, k * P:(k + 1) * P], p.ident[:])
                    last.then_inc(*tr.up())

            @block.gpsimd
            def _(pool):
                if clear is not None:
                    pool.memset(clear, 0.0)
                if weights:
                    weights.first_split(pool)
                if split:
                    for b in range(TB):
                        pool.wait_ge(*far_hi.at(b + 1))
                        pool.tensor_tensor(of_block(split[1], b, far_), hf[:, b % 2, far_],
                                           of_block(split[0], b, far_).bitcast(F32), ALU.subtract).then_inc(*far_lo.up())

            @block.vector
            def _(dve):
                link = chained(dve_c)

                def scaled(b):
                    dve.tensor_scalar(xs[:, b % 2], p.x[:, b], p.rstd[:, b:b + 1], None, ALU.mult).then_inc(*xn.up())
                dve.wait_ge(*sq.at(TB))
                dve.tensor_scalar(p.stat[:], p.stat[:], 1.0 / D, EPS, ALU.mult, ALU.add).then_inc(*mean.up())
                dve.wait_ge(*root.at(1))
                link(dve, dve.reciprocal(p.rstd[:], p.rstd[:]))
                scaled(0)
                scaled(1)
                for b in range(TB):
                    s = SEQ_OF[b]
                    dve.wait_ge(*tr.at(b + 1))
                    for k in range(KD // 2):
                        out = hf[:, b % 2, k] if split else hT[:, k, b * P:(b + 1) * P]
                        last = dve.tensor_scalar(
                            out, p.psum[:, 2 * (b % 4) + k // 4, (k % 4) * P:(k % 4 + 1) * P],
                            p.scale_in[:, l, which, k, s:s + 1], p.mod[:, l, 3 * which * KD + k, s:s + 1],
                            ALU.mult, ALU.add)
                    last.then_inc(*ev.up())
                    if b + 2 < TB:
                        scaled(b + 2)
                    if split:
                        dve.wait_ge(*ev.at(b + 1))
                        link(dve, dve.tensor_copy(of_block(split[0], b, near), hf[:, b % 2, near]))
                        dve.tensor_tensor(of_block(split[1], b, near), hf[:, b % 2, near],
                                          of_block(split[0], b, near).bitcast(F32), ALU.subtract)
    p.close_stage()


class InWeights:
    PIECES = [(SSDW + f * P, SSDW + (f + 2) * P) for f in range(0, XF, 2)] + \
             [(C_DT, (C_DT + IN_COLS) // 2), ((C_DT + IN_COLS) // 2, IN_COLS), (0, SSDW // 2), (SSDW // 2, SSDW)]
    WIDEST = max(hi - lo for lo, hi in PIECES)

    def __init__(self, p, l, raw_room, ctx):
        self.p, self.l = p, l
        self.raw = raw_room[:, 0:2 * KD * self.WIDEST].rearrange("p (r c) -> p r c", r=2)
        self.hi = p.sb(f"win_hi{l}", [P, 2, KD * self.WIDEST], F32R, ctx=ctx)
        self.lo = p.sb(f"win_lo{l}", [P, 2, KD * self.WIDEST], F32R, ctx=ctx)
        own = p.stream_signals
        self.landed, (self.hi_done, self.lo_done) = own[0:2], own[2:4]

    def view(self, tile, i):
        lo, hi = self.PIECES[i]
        return tile[:, i % 2, 0:KD * (hi - lo)]

    def by_block(self, tile, i):
        return self.view(tile, i).rearrange("p (k c) -> p k c", k=KD)

    def load(self, sp, i):
        lo, hi = self.PIECES[i]
        if i >= 2:
            sp.wait_ge(*self.lo_done.at(i - 1))
        sp.dma_start(self.by_block(self.raw, i), self.p.io["w_in"][self.l, :, lo:hi].rearrange(
            "(k p) f -> p k f", p=P)).then_inc(*self.landed[i % 2].up(16))

    def first_split(self, pool):
        pool.wait_ge(*self.landed[0].at(16))
        pool.tensor_copy(self.view(self.hi, 0), self.view(self.raw, 0)).then_inc(*self.hi_done.up())
        self.split_lo(pool, 0)

    def split_hi(self, act, i):
        act.wait_ge(*self.landed[i % 2].at(16 * (i // 2 + 1)))
        act.activation(self.view(self.hi, i), self.view(self.raw, i), ACT.Copy).then_inc(*self.hi_done.up())

    def split_lo(self, pool, i):
        pool.wait_ge(*self.hi_done.at(i + 1))
        pool.tensor_tensor(self.view(self.lo, i), self.view(self.raw, i), self.view(self.hi, i).bitcast(F32),
                           ALU.subtract).then_inc(*self.lo_done.up())


def stage_in_proj(p, l, w, h_hi, h_lo, t):
    nc, io = p.nc, p.io
    mm, ev, pads, padded = p.sig("win_ps"), p.sig("win_evicted"), p.sig("win_pads"), p.sig("conv_padded")
    small, conv_done, silu_done = p.sig("ssd_small"), p.sig("conv_done"), p.sig("conv_silu_done")
    dve_c = p.sig("dve_chain")
    homes = [(0, SSDW, t["z"]), (C_DT, C_KV, t["dtcq"]), (C_KV, IN_COLS, t["ckr"])]
    feature_pieces = XF // 2
    pieces = range(len(w.PIECES))
    groups = [(i, 2 * i + f, half) for i in range(feature_pieces) for f in range(2) for half in range(2)] + \
             [(i, b, None) for i in pieces[feature_pieces:] for b in range(TB)]
    with ExitStack() as own:
        cw, cb = p.sb(f"conv_taps{l}", [P, XF, TAPS], ctx=own), p.sb(f"conv_bias{l}", [P, XF], ctx=own)
        pad = p.sb(f"conv_pad{l}", [P, 2, PADW], ctx=own)
        acc = p.sb(f"conv_acc{l}", [P, 2, PADW - 4], ctx=own)
        xbc = t["xbc"]
        with nc.Block() as block:
            @block.sync
            def _(sp):
                with nc.allow_non_contiguous_dma(reason="small per-channel vectors"):
                    for k in range(TAPS):
                        sp.dma_start(cw[:, :, k], io["conv_w"][l, k].rearrange("(f p) -> p f", p=P)).then_inc(*small.up(16))
                    sp.dma_start(cb[:], io["conv_b"][l].rearrange("(f p) -> p f", p=P)).then_inc(*small.up(16))
                for i in pieces[2:]:
                    w.load(sp, i)

            @block.gpsimd
            def _(pool):
                pool.memset(pad[:, :, 0:2], 0.0)
                pool.memset(pad[:, :, 2 + LAT:6 + LAT], 0.0)
                pool.memset(pad[:, :, PADW - 2:PADW], 0.0).then_inc(*pads.up())
                for i in pieces[1:]:
                    w.split_lo(pool, i)

            @block.scalar
            def _(act):
                def silu(f):
                    act.wait_ge(*conv_done.at(f + 1))
                    act.activation(xbc[:, f, 0:LAT], acc[:, f % 2, 0:LAT], ACT.Silu, bias=cb[:, f:f + 1])
                    act.activation(xbc[:, f, LAT:T], acc[:, f % 2, 4 + LAT:4 + LAT + CTX], ACT.Silu,
                                   bias=cb[:, f:f + 1]).then_inc(*silu_done.up())
                act.wait_ge(*small.at(16 * (TAPS + 1)))
                for i in pieces[1:]:
                    if i >= 2:
                        act.wait_ge(*mm.at(sum(g[0] <= i - 2 for g in groups)))
                    w.split_hi(act, i)
                    for f in range(max(2 * i - 3, 0), min(2 * i - 1, XF)):
                        silu(f)

            @block.tensor
            def _(pe):
                for g, (i, j, half) in enumerate(groups):
                    pe.wait_ge(*w.lo_done.at(i + 1))
                    if g >= 8:
                        pe.wait_ge(*ev.at(g - 7))
                    hi, lo = w.by_block(w.hi, i), w.by_block(w.lo, i)
                    for k in range(KD):
                        for n, (mw, mh) in enumerate(((hi, h_hi), (hi, h_lo), (lo, h_hi))):
                            first, final = k == 0 and n == 0, k == KD - 1 and n == 2
                            if half is None:
                                width = w.PIECES[i][1] - w.PIECES[i][0]
                                last = pe.matmul(p.psum[:, g % 8, 0:width], mh[:, k, j * P:(j + 1) * P],
                                                 mw[:, k, :], start=first, stop=final)
                            else:
                                last = pe.matmul(p.psum[:, g % 8, 0:HT], mw[:, k, (j % 2) * P:(j % 2 + 1) * P],
                                                 mh[:, k, half * HT:(half + 1) * HT], start=first, stop=final)
                    last.then_inc(*mm.up())

            @block.vector
            def _(dve):
                link = chained(dve_c)
                dve.wait_ge(*pads.at(1))
                dve.wait_ge(*small.at(16 * (TAPS + 1)))
                for g, (i, j, half) in enumerate(groups):
                    dve.wait_ge(*mm.at(g + 1))
                    if half is None:
                        lo, hi = w.PIECES[i]
                        for c0, c1, tile in homes:
                            a, b = max(lo, c0), min(hi, c1)
                            if a < b:
                                last = dve.tensor_copy(tile[:, j, a - c0:b - c0], p.psum[:, g % 8, a - lo:b - lo])
                        last.then_inc(*ev.up())
                        continue
                    if half == 0:
                        dve.tensor_copy(pad[:, j % 2, 2:2 + HT], p.psum[:, g % 8, 0:HT]).then_inc(*ev.up())
                        continue
                    dve.tensor_copy(pad[:, j % 2, 2 + HT:2 + LAT], p.psum[:, g % 8, 0:LAT - HT])
                    dve.tensor_copy(pad[:, j % 2, 6 + LAT:6 + LAT + CTX],
                                    p.psum[:, g % 8, LAT - HT:HT]).then_inc(*ev.up())
                    dve.wait_ge(*ev.at(g + 1))
                    width = PADW - 4
                    if j >= 2:
                        dve.wait_ge(*silu_done.at(j - 1))
                    link(dve, dve.tensor_scalar(acc[:, j % 2], pad[:, j % 2, 0:width], cw[:, j, 0:1], None, ALU.mult))
                    for k in range(1, TAPS):
                        ins = dve.scalar_tensor_tensor(out=acc[:, j % 2], in0=pad[:, j % 2, k:k + width],
                                                       scalar=cw[:, j, k:k + 1], in1=acc[:, j % 2],
                                                       op0=ALU.mult, op1=ALU.add)
                        if k < TAPS - 1:
                            link(dve, ins)
                    ins.then_inc(*conv_done.up())
    for signal in p.stream_signals:
        signal.close()
    p.close_stage()


def stage_ssd(p, l, t):
    nc, io = p.nc, p.io
    small = p.sig("ssd_small")
    dve_c = p.sig("dve_chain")
    dt_pre, e_neg, ln_u, a_exp, z_silu = (p.sig(n) for n in ("dt_pre", "dt_exp", "dt_log", "a_exp", "z_silu"))
    da_ready, la_ps, la_sb, la_exps = p.sig("da_ready"), p.sig("la_ps"), p.sig("la_sb"), p.sig("la_exps")
    turned, turned_out = p.sig("xs_turned"), p.sig("xs_turned_out")
    wx_ready, cs_ps, cs_used = p.sig("wx_ready"), p.sig("cs_ps"), p.sig("cs_used")
    st_in, st_turned, st_ready = p.sig("st_in"), p.sig("st_turned"), p.sig("st_ready")
    lab_ps, seg_ready, dec_ready, cb_ps, s_ready, y_ps, y_used = (p.sig(n) for n in (
        "lab_ps", "seg_ready", "decay_ready", "cb_ps", "scores_ready", "y_ps", "y_used"))
    squares = p.sig("pn_squares")
    cb_kept, parts_ready = p.sig("cb_kept"), p.sig("silu_parts_ready")
    fin_turned, fin_out, fin_stored = p.sig("fin_turned"), p.sig("fin_out"), p.sig("fin_stored")
    with ExitStack() as own:
        def sb(name, shape):
            return p.sb(f"ssd_{name}{l}", shape, ctx=own)
        dtb, alog, dsk = sb("dtb", [P, 2 * NH]), sb("alog", [P, 2 * NH]), sb("dsk", [P, NH])
        btok = sb("btok", [P, TB, P])
        s5 = [P, TB, 2 * NH]
        v, neg, e, u, ln, dt, da, la, el, te, cd = (sb(n, s5) for n in (
            "v", "neg", "e", "u", "ln", "dt", "da", "la", "el", "te", "cd"))
        cdg = sb("cdg", [P, TB, 2, NH // 2])
        wx = sb("wx", [P, 2, 2, SSDW])
        hs = sb("hs", [P, 2, TB, 256])
        stl = sb("stl", [P, 2, 2, P])
        hfin = sb("hfin", [P, 2, 256])
        junk, junk2 = sb("junk", [P, QR]), sb("junk2", [P, KVR])
        seg = sb("seg", [P, 2, NH, P])
        cbs = sb("cbs", [P, NG, P])
        t1, t2 = sb("t1", [P, SSDW]), sb("t2", [P, SSDW])
        xbc, z, xst, y = t["xbc"], t["z"], t["xst"], t["y_ssd"]
        dtr = t["dtcq"][:, :, 0:2 * NH]
        mod = Modulation(p, modulation_units(l)[0], 7, own, f"ssd{l}", 4, True)

        def unit_steps(n):
            return range(UNIT_STEPS * n, UNIT_STEPS * (n + 1)) if n < len(mod.units) else ()

        def split_unit(act, n):
            for i in range(QUARTERS * n, QUARTERS * (n + 1)) if n < len(mod.units) else ():
                mod.on_scalar(act, i)
        with nc.Block() as block:
            @block.sync
            def _(sp):
                for tile, name in ((dtb, "dt_bias"), (alog, "a_log"), (dsk, "d_skip")):
                    row = io[name][l].rearrange("a b -> (a b)") if name != "d_skip" else io[name][l]
                    sp.dma_start(tile[:], row.partition_broadcast(P)).then_inc(*small.up(16))
                for d in range(2):
                    for g in range(2):
                        sp.dma_start(stl[:, d, :, g * NS:(g + 1) * NS], io["state_ssm"][0, l, d, 4 * g:4 * g + 4].rearrange(
                            "(j h) q n -> (h q) j n", h=2)).then_inc(*st_in.up(16))
                mod.load(sp)
                sp.wait_ge(*fin_out.at(2))
                for d in range(2):
                    for g in range(2):
                        sp.dma_start(io["new_ssm"][0, l, d, 4 * g:4 * g + 4].rearrange("(j h) q n -> (h q) j n", h=2),
                                     stl[:, d, :, g * NS:(g + 1) * NS]).then_inc(*fin_stored.up(16))
                sp.wait_ge(*fin_stored.at(64))

            @block.scalar
            def _(act):
                act.wait_ge(*small.at(48))
                act.wait_ge(*dt_pre.at(1))
                act.activation(e[:], neg[:], ACT.Exp).then_inc(*e_neg.up())
                act.activation(alog[:], alog[:], ACT.Exp).then_inc(*a_exp.up())
                act.wait_ge(*dt_pre.at(2))
                act.activation(ln[:], u[:], ACT.Ln).then_inc(*ln_u.up())
                split_unit(act, 0)
                act.wait_ge(*la_sb.at(1))
                act.activation(el[:], la[:], ACT.Exp)
                act.activation(cd[:], cd[:], ACT.Exp)
                act.activation(te[:], te[:], ACT.Exp).then_inc(*la_exps.up())
                split_unit(act, 1)
                act.activation(z[:], z[:], ACT.Silu).then_inc(*z_silu.up())
                split_unit(act, 2)
                for b in range(TB):
                    for d in range(2):
                        act.wait_ge(*seg_ready.at(2 * b + d + 1))
                        act.activation(seg[:, d], seg[:, d], ACT.Exp).then_inc(*dec_ready.up())
                    split_unit(act, 3 + b)
                    if b >= 1:
                        act.wait_ge(*squares.at(2 * b))
                    act.activation(junk[:], t["dtcq"][:, b, 2 * NH:], ACT.Square,
                                   accum_out=t["stat"][:, 0, b:b + 1]).then_inc(*squares.up())
                    act.activation(junk2[:], t["ckr"][:, b, 0:KVR], ACT.Square,
                                   accum_out=t["stat"][:, 1, b:b + 1]).then_inc(*squares.up())

            @block.gpsimd
            def _(pool):
                mod.on_gpsimd(pool)

            @block.tensor
            def _(pe):
                def turn_state(bank, src):
                    for d in range(2):
                        for j in range(2):
                            last = pe.transpose(p.psum[:, bank, (2 * d + j) * P:(2 * d + j + 1) * P],
                                                src(d, j), p.ident[:])
                    return last
                pe.wait_ge(*st_in.at(64))
                turn_state(4, lambda d, j: stl[:, d, j, :]).then_inc(*st_turned.up())
                pe.wait_ge(*da_ready.at(1))
                lap = p.psum[:, 6, 0:4 * NH * TB].rearrange("p (b c) -> p b c", b=TB)
                for b in range(TB):
                    pe.matmul(lap[:, b, 0:NH], p.tri[:, 0], da[:, b, 0:NH], start=True, stop=True)
                    pe.matmul(lap[:, b, NH:2 * NH], p.tri[:, 1], da[:, b, NH:2 * NH], start=True, stop=True)
                    last = pe.matmul(lap[:, b, 2 * NH:4 * NH], p.ones[:], da[:, b, :], start=True, stop=True)
                last.then_inc(*la_ps.up())
                pe.wait_ge(*parts_ready.at(1))
                for step in unit_steps(0):
                    mod.on_tensor(pe, step)
                for b in range(TB):
                    if b >= 2:
                        pe.wait_ge(*turned_out.at(b - 1))
                    for f in range(4):
                        pe.transpose(p.psum[:, b % 2, f * P:(f + 1) * P], xbc[:, f, b * P:(b + 1) * P], p.ident[:])
                    pe.transpose(p.psum[:, 2 + b % 2, 0:P], xbc[:, 4, b * P:(b + 1) * P],
                                 p.ident[:]).then_inc(*turned.up())
                for b in range(TB):
                    pe.wait_ge(*wx_ready.at(b + 1))
                    if b >= 2:
                        pe.wait_ge(*cs_used.at(b - 1))
                    for d in range(2):
                        for g in range(NG):
                            last = pe.matmul(p.psum[g * NS:(g + 1) * NS, 4 + b % 2, d * 256:(d + 1) * 256],
                                             btok[:, b, g * NS:(g + 1) * NS], wx[:, b % 2, d, g * 256:(g + 1) * 256],
                                             start=(d == 0), stop=True, skip_group_check=True)
                    last.then_inc(*cs_ps.up())
                for step in unit_steps(1):
                    mod.on_tensor(pe, step)

                def every_la(b):
                    for d in range(2):
                        if b >= 1:
                            pe.wait_ge(*seg_ready.at(2 * (b - 1) + d + 1))
                        for h in range(NH):
                            last = pe.matmul(p.psum[:, 2 * d + h // 4, (h % 4) * P:(h % 4 + 1) * P],
                                             da[:, b, d * NH + h:d * NH + h + 1].to_broadcast([P, P]),
                                             p.tri[:, d], start=True, stop=True)
                        last.then_inc(*lab_ps.up())
                every_la(0)
                pe.wait_ge(*st_ready.at(1))
                for b in range(TB):
                    if b >= 1:
                        pe.wait_ge(*y_used.at(b))
                    for g in range(NG):
                        part = slice(g * NS, (g + 1) * NS)
                        last = pe.matmul(p.psum[:, 5 - g, 0:P], xbc[part, 4, b * P:(b + 1) * P],
                                         xbc[part, 5, b * P:(b + 1) * P], start=True, stop=True)
                    last.then_inc(*cb_ps.up())
                    pe.wait_ge(*cb_kept.at(b + 1))
                    for d in range(2):
                        for g in range(NG):
                            part = slice(g * NS, (g + 1) * NS)
                            pe.matmul(p.psum[:, 5 + g, d * 256:(d + 1) * 256], xbc[part, 5, b * P:(b + 1) * P],
                                      hs[part, d, b, :], start=True, stop=True)
                    for step in unit_steps(2 + b)[0:QUARTERS]:
                        mod.on_tensor(pe, step)
                    pe.wait_ge(*s_ready.at(b + 1))
                    for h in range(NH):
                        last = pe.matmul(p.psum[:, 4, h * HD:(h + 1) * HD], seg[:, 0, h],
                                         xst[:, b, h * HD:(h + 1) * HD], start=True, stop=True)
                    last.then_inc(*y_ps.up())
                    if b + 1 < TB:
                        every_la(b + 1)
                    for step in unit_steps(2 + b)[QUARTERS:]:
                        mod.on_tensor(pe, step)
                pe.wait_ge(*y_used.at(TB))
                turn_state(4, lambda d, j: hfin[:, d, j * P:(j + 1) * P]).then_inc(*fin_turned.up())

            @block.vector
            def _(dve):
                link = chained(dve_c)
                link(dve, dve.tensor_scalar(p.silu_parts[:], p.ident[:, 0:1].to_broadcast([P, KD * P]).rearrange(
                    "p (k c) -> p k c", k=KD), 0.0, None, ALU.mult))
                link(dve, dve.tensor_copy(p.silu_parts[:, :, 0:2], p.silu_c[:]))
                dve.tensor_tensor(p.silu_parts[:, :, 2:4], p.silu_c[:], p.silu_parts[:, :, 0:2].bitcast(F32),
                                  ALU.subtract).then_inc(*parts_ready.up())
                dve.wait_ge(*small.at(48))
                link(dve, dve.tensor_tensor(v[:], dtr, insert_dim(dtb[:], 1, TB), ALU.add))
                dve.scalar_tensor_tensor(out=neg[:], in0=v[:], scalar=-1.0, in1=v[:], op0=ALU.mult,
                                         op1=ALU.min).then_inc(*dt_pre.up())
                dve.wait_ge(*e_neg.at(1))
                link(dve, dve.tensor_scalar(u[:], e[:], 1.0, None, ALU.add))
                link(dve, dve.tensor_scalar(dt[:], u[:], -1.0, None, ALU.add))
                link(dve, dve.tensor_tensor(dt[:], e[:], dt[:], ALU.subtract))
                dve.scalar_tensor_tensor(out=v[:], in0=v[:], scalar=0.0, in1=dt[:], op0=ALU.max,
                                         op1=ALU.add).then_inc(*dt_pre.up())
                dve.wait_ge(*dt_pre.at(2))
                dve.wait_ge(*ln_u.at(1))
                link(dve, dve.tensor_tensor(dt[:], v[:], ln[:], ALU.add))
                dve.wait_ge(*a_exp.at(1))
                dve.scalar_tensor_tensor(out=da[:], in0=dt[:], scalar=-1.0, in1=insert_dim(alog[:], 1, TB),
                                         op0=ALU.mult, op1=ALU.mult).then_inc(*da_ready.up())
                dve.wait_ge(*st_turned.at(1))
                link(dve, dve.tensor_copy(hs[:, 0, 0, :], p.psum[:, 4, 0:256]))
                link(dve, dve.tensor_copy(hs[:, 1, LB - 1, :], p.psum[:, 4, 256:512]))
                link(dve, dve.memset(hs[:, :, LB, :], 0.0))
                dve.wait_ge(*la_ps.at(1))
                lap = p.psum[:, 6, 0:4 * NH * TB].rearrange("p (b c) -> p b c", b=TB)
                link(dve, dve.tensor_copy(la[:], lap[:, :, 0:2 * NH]))
                link(dve, dve.tensor_copy(cd[:], lap[:, :, 2 * NH:4 * NH]))
                dve.tensor_tensor(te[:], cd[:], la[:], ALU.subtract).then_inc(*la_sb.up())
                for step in unit_steps(0):
                    mod.on_vector(dve, step)
                dve.wait_ge(*la_exps.at(1))
                link(dve, dve.tensor_tensor(te[:], te[:], dt[:], ALU.mult))
                for g in range(NG):
                    for d in range(2):
                        link(dve, dve.tensor_copy(cdg[g * NS:(g + 1) * NS, :, d],
                                                  cd[g * NS:(g + 1) * NS, :, d * NH + 4 * g:d * NH + 4 * g + 4]))
                for b in range(TB):
                    dve.wait_ge(*turned.at(b + 1))
                    link(dve, dve.tensor_copy(xst[:, b], p.psum[:, b % 2]))
                    dve.tensor_copy(btok[:, b], p.psum[:, 2 + b % 2, 0:P]).then_inc(*turned_out.up())

                def advance(b, d, out):
                    link(dve, dve.tensor_tensor(out.rearrange("p (h q) -> p h q", h=4),
                                                hs[:, d, b].rearrange("p (h q) -> p h q", h=4),
                                                cdg[:, b, d].to_broadcast([P, 4, HD]), ALU.mult))
                    link(dve, dve.tensor_tensor(out, out, hadd(b, d), ALU.add))

                def hadd(b, d):
                    return adds[:, b, d, :]
                adds = t["qkv_room"][:, 0:TB * 512].rearrange("p (b d c) -> p b d c", b=TB, d=2)

                def weighted(b):
                    for d in range(2):
                        last = dve.tensor_tensor(wx[:, b % 2, d].rearrange("p (h q) -> p h q", h=NH),
                                                 xst[:, b].rearrange("p (h q) -> p h q", h=NH),
                                                 te[:, b, d * NH:(d + 1) * NH].to_broadcast([P, NH, HD]), ALU.mult)
                    last.then_inc(*wx_ready.up())
                weighted(0)
                for b in range(TB):
                    if b + 1 < TB:
                        weighted(b + 1)
                    dve.wait_ge(*cs_ps.at(b + 1))
                    dve.tensor_copy(adds[:, b], p.psum[:, 4 + b % 2].rearrange(
                        "p (d c) -> p d c", d=2)).then_inc(*cs_used.up())
                dve.wait_ge(*cs_used.at(TB))
                for b in range(LB - 1):
                    advance(b, 0, hs[:, 0, b + 1])
                for b in range(LB - 1, 0, -1):
                    advance(b, 1, hs[:, 1, b - 1])
                for step in unit_steps(1):
                    mod.on_vector(dve, step)
                dve.tensor_copy(hfin[:], adds[:, LB]).then_inc(*st_ready.up())
                for b in range(TB):
                    for d in range(2):
                        dve.wait_ge(*lab_ps.at(2 * b + d + 1))
                        if b >= 1:
                            dve.wait_ge(*y_ps.at(b))
                        for h in range(NH):
                            last = dve.scalar_tensor_tensor(
                                out=seg[:, d, h], in0=p.psum[:, 2 * d + h // 4, (h % 4) * P:(h % 4 + 1) * P],
                                scalar=la[:, b, d * NH + h:d * NH + h + 1], in1=p.far[:, d],
                                op0=ALU.subtract, op1=ALU.add)
                        last.then_inc(*seg_ready.up())
                    dve.wait_ge(*cb_ps.at(b + 1))
                    dve.tensor_copy(cbs[:, 0], p.psum[:, 5, 0:P])
                    dve.tensor_copy(cbs[:, 1], p.psum[:, 4, 0:P]).then_inc(*cb_kept.up())
                    dve.wait_ge(*dec_ready.at(2 * b + 1))
                    for h in range(NH):
                        last = dve.tensor_scalar(seg[:, 0, h], seg[:, 0, h], dt[:, b, h:h + 1], None, ALU.mult)
                    link(dve, last)
                    dve.wait_ge(*dec_ready.at(2 * b + 2))
                    for h in range(NH):
                        last = dve.scalar_tensor_tensor(
                            out=seg[:, 0, h], in0=seg[:, 1, h], scalar=dt[:, b, NH + h:NH + h + 1],
                            in1=seg[:, 0, h], op0=ALU.mult, op1=ALU.add)
                    link(dve, last)
                    dve.wait_ge(*cb_kept.at(b + 1))
                    for g in range(NG):
                        last = dve.tensor_tensor(seg[:, 0, 4 * g:4 * g + 4], seg[:, 0, 4 * g:4 * g + 4],
                                                 insert_dim(cbs[:, g], 1, 4), ALU.mult)
                    last.then_inc(*s_ready.up())
                    for step in unit_steps(2 + b)[0:QUARTERS]:
                        mod.on_vector(dve, step)

                    def heads(ap):
                        return ap.rearrange("p (h q) -> p h q", h=NH)

                    def by_group(ap):
                        return ap.rearrange("p (g h q) -> p g h q", g=NG, q=HD)

                    def inter(d):
                        return p.psum[:, 5:7, d * 256:(d + 1) * 256].rearrange("p g (h q) -> p g h q", q=HD)

                    def heads_la(d):
                        la_exp = el[:, b, d * NH:(d + 1) * NH].rearrange("p (g h) -> p g h", g=NG)
                        return la_exp.to_broadcast([P, NG, NH // NG, HD])
                    dve.wait_ge(*y_ps.at(b + 1))
                    link(dve, dve.tensor_tensor(by_group(t1[:]), inter(0), heads_la(0), ALU.mult))
                    link(dve, dve.tensor_tensor(by_group(t2[:]), inter(1), heads_la(1), ALU.mult))
                    link(dve, dve.tensor_tensor(t1[:], t1[:], t2[:], ALU.add))
                    link(dve, dve.tensor_tensor(heads(t2[:]), heads(xst[:, b]), dsk[:].to_broadcast([P, NH, HD]),
                                                ALU.mult))
                    link(dve, dve.tensor_tensor(t2[:], p.psum[:, 4], t2[:], ALU.add))
                    link(dve, dve.tensor_tensor(t1[:], t1[:], t2[:], ALU.add))
                    if b == 0:
                        dve.wait_ge(*z_silu.at(1))
                    dve.tensor_tensor(y[:, b], t1[:], z[:, b], ALU.mult).then_inc(*y_used.up())
                    for step in unit_steps(2 + b)[QUARTERS:]:
                        mod.on_vector(dve, step)
                dve.wait_ge(*fin_turned.at(1))
                dve.tensor_copy(stl[:, 0], p.psum[:, 4, 0:256].rearrange("p (j c) -> p j c", j=2)).then_inc(*fin_out.up())
                dve.tensor_copy(stl[:, 1], p.psum[:, 4, 256:512].rearrange("p (j c) -> p j c", j=2)).then_inc(*fin_out.up())
    p.close_stage()


def stage_attention(p, l, t):
    nc, io = p.nc, p.io
    w_in, gains_in, cache_in = p.sig("at_w_in"), p.sig("at_gains_in"), p.sig("at_cache_in")
    mean, root, rs = p.sig("at_mean"), p.sig("at_root"), p.sig("at_rstd")
    kvn, krt_ready, lat_tr, lat_ev = p.sig("at_kvn"), p.sig("at_krt"), p.sig("at_lat_turned"), p.sig("at_lat_out")
    new_out = p.sig("at_new_stored")
    gm_ps, gm_ev, qt_ready = p.sig("at_gemm_ps"), p.sig("at_gemm_out"), p.sig("at_q_ready")
    tr_ps, tr_ev = p.sig("at_turned"), p.sig("at_turned_out")
    sc_ps, mx_ready, e_ready, pt_ps, pt_ev, o_ps, o_ev = (p.sig(n) for n in (
        "at_scores_ps", "at_max", "at_exp", "at_probs_turned", "at_probs_out", "at_o_ps", "at_o_out"))
    zeroed = p.sig("at_zeroed")
    dve_c = p.sig("dve_chain")
    QF, VF = QR // P, KVR // P
    with ExitStack() as own:
        def sb(name, shape):
            return p.sb(f"at_{name}{l}", shape, ctx=own)
        wq = sb("wq", [P, QF, NH * QD])
        wkv = sb("wkv", [P, VF, NH * (NOPE + VD)])
        gq, kvrow = sb("gq", [P, QF]), sb("kvrow", [P, KVR])
        cos, sin = sb("cos", [P, LB, ROPE]), sb("sin", [P, LB, ROPE])
        past = sb("past", [P, KVR])
        krt = sb("krt", [P, KB, QD])
        stat, rstd = t["stat"], sb("rstd", [P, 2, TB])
        cqT = sb("cqT", [P, QF, T])
        ckvT = sb("ckvT", [P, VF, KEYS])
        qtok = sb("qtok", [P, 2, NH * QD])
        ra, rb = sb("ra", [P, NH, ROPE]), sb("rb", [P, NH, ROPE])
        qT = sb("qT", [P, NH, T])
        kT = t["qkv_room"].rearrange("p (h k) -> p h k", h=NH)
        vt = sb("vt", [P, KB, NH * VD])
        prob = sb("prob", [P, 2, LAT + PAST])
        probT = sb("probT", [P, 2, LAT + PAST])
        mx = sb("mx", [P, 2 * NH, 2])
        total = sb("total", [P, 2, NH])
        cq, ckr, o = t["dtcq"][:, :, 2 * NH:], t["ckr"], t["o"]
        ck, kr = ckr[:, :, 0:KVR], ckr[:, :, KVR:KVR + ROPE]
        mod = Modulation(p, modulation_units(l)[1], 7, own, f"at{l}", 2, True)
        turns = [("past", 0)] + [("tok", b) for b in range(TB)]
        items = [(b, h) for b in range(TB) for h in range(NH)]
        step_at = {s * 3 // 2: s for s in range(len(mod.steps))}
        item_of = {mod.steps[s]: n for n, s in step_at.items()}
        split_at = {item_of[(i - 2) % QUARTERS, (i - 2) // QUARTERS] + 1: i for i in mod.quarters if i >= 2}

        def keys_of(b):
            return (0, PAST + LAT) if b < LB else (PAST + LAT, KEYS)
        with nc.Block() as block:
            @block.sync
            def _(sp):
                with nc.allow_non_contiguous_dma(reason="one gain per partition"):
                    sp.dma_start(gq[:], io["q_norm"][l].rearrange("(k p) -> p k", p=P)).then_inc(*gains_in.up(16))
                sp.dma_start(kvrow[:], io["kv_norm"][l].partition_broadcast(P)).then_inc(*gains_in.up(16))
                sp.dma_start(cos[:], io["rope_cos"].rearrange("(b p) r -> p b r", p=P)).then_inc(*gains_in.up(16))
                sp.dma_start(sin[:], io["rope_sin"].rearrange("(b p) r -> p b r", p=P)).then_inc(*gains_in.up(16))
                sp.dma_start(past[:], io["cache_ckv"][0, l]).then_inc(*cache_in.up(16))
                sp.wait_ge(*zeroed.at(1))
                sp.dma_start(krt[:, 0, NOPE:QD], io["cache_krope"][0, l]).then_inc(*cache_in.up(16))
                sp.dma_start(wq[:], io["w_uq"][l].rearrange("(k p) f -> p k f", p=P)).then_inc(*w_in.up(16))
                sp.dma_start(wkv[:], io["w_ukv"][l].rearrange("(k p) f -> p k f", p=P)).then_inc(*w_in.up(16))
                sp.dma_start(io["new_krope"][0, l], kr[:, LB]).then_inc(*new_out.up(16))
                sp.wait_ge(*kvn.at(TB))
                sp.dma_start(io["new_ckv"][0, l], ck[:, LB]).then_inc(*new_out.up(16))
                mod.load(sp)
                sp.wait_ge(*new_out.at(32))

            @block.gpsimd
            def _(pool):
                pool.memset(krt[:], 0.0).then_inc(*zeroed.up())
                mod.on_gpsimd(pool)

            @block.scalar
            def _(act):
                act.wait_ge(*mean.at(1))
                act.activation(rstd[:], stat[:], ACT.Sqrt).then_inc(*root.up())
                for i in mod.quarters[0:2]:
                    mod.on_scalar(act, i)
                for n, (b, h) in enumerate(items):
                    lo, hi = keys_of(b)
                    act.wait_ge(*mx_ready.at(n + 1))
                    if n >= 2:
                        act.wait_ge(*pt_ps.at(n - 1))
                    if b >= 2 and h == 0:
                        act.wait_ge(*o_ev.at(b - 1))
                    w = (hi - lo) // 2
                    act.activation(prob[:, n % 2, 0:hi - lo].rearrange("p (a k) -> p a k", a=2),
                                   p.psum[:, 2 * (n % 2):2 * (n % 2) + 2, 0:w], ACT.Exp,
                                   bias=mx[:, n % (2 * NH), 1:2], scale=SCALE,
                                   accum_out=total[:, b % 2, h:h + 1]).then_inc(*e_ready.up())
                    if n in split_at:
                        mod.on_scalar(act, split_at[n])

            @block.tensor
            def _(pe):
                def turn_queries(pe, b):
                    pe.wait_ge(*qt_ready.at(b + 1))
                    if b >= 2:
                        pe.wait_ge(*tr_ev.at(b - 1))
                    for h in range(NH):
                        last = pe.transpose(p.psum[0:QD, 4 + 2 * (b % 2) + h // 4, (h % 4) * P:(h % 4 + 1) * P],
                                            qtok[:, b % 2, h * QD:(h + 1) * QD], p.ident[:])
                    last.then_inc(*tr_ps.up())

                pe.wait_ge(*cache_in.at(32))
                for n, (kind, b) in enumerate(turns):
                    if kind == "tok":
                        pe.wait_ge(*kvn.at(b + 1))
                    if n >= 4:
                        pe.wait_ge(*lat_ev.at(n - 3))
                    for k in range(VF):
                        src = past[:, k * P:(k + 1) * P] if kind == "past" else ck[:, b, k * P:(k + 1) * P]
                        last = pe.transpose(p.psum[:, 2 * (n % 4), k * P:(k + 1) * P], src, p.ident[:])
                    if kind == "tok":
                        for k in range(QF):
                            last = pe.transpose(p.psum[:, 2 * (n % 4) + 1, k * P:(k + 1) * P],
                                                cq[:, b, k * P:(k + 1) * P], p.ident[:])
                    last.then_inc(*lat_tr.up())
                pe.wait_ge(*w_in.at(32))
                pe.wait_ge(*lat_ev.at(len(turns)))
                g = 0
                for b in range(TB):
                    if b >= 2:
                        pe.wait_ge(*gm_ev.at(b - 1))
                    for part, (lo, hi) in enumerate(((0, 512), (512, NH * QD))):
                        for k in range(QF):
                            last = pe.matmul(p.psum[:, 2 * (b % 2) + part, 0:hi - lo], cqT[:, k, b * P:(b + 1) * P],
                                             wq[:, k, lo:hi], start=(k == 0), stop=(k == QF - 1))
                    last.then_inc(*gm_ps.up())
                    if b >= 1:
                        turn_queries(pe, b - 1)
                turn_queries(pe, TB - 1)
                for h in range(NH):
                    if h < 2:
                        pe.wait_ge(*gm_ev.at(TB - 1 + h))
                    else:
                        pe.wait_ge(*gm_ev.at(TB + h - 1))
                    for part in range(2):
                        for k in range(VF):
                            last = pe.matmul(p.psum[0:NOPE, 2 * (h % 2) + part, 0:KEYS // 2],
                                             wkv[:, k, h * (NOPE + VD):h * (NOPE + VD) + NOPE],
                                             ckvT[:, k, part * KEYS // 2:(part + 1) * KEYS // 2],
                                             start=(k == 0), stop=(k == VF - 1))
                    last.then_inc(*gm_ps.up())
                for n in range(KB):
                    pe.wait_ge(*gm_ev.at(TB + NH + n - 1))
                    for k in range(VF):
                        last = pe.matmul(p.psum[:, 2 * (n % 2), 0:NH * VD], ckvT[:, k, n * P:(n + 1) * P],
                                         wkv[:, k].rearrange("p (h c) -> p h c", h=NH)[:, :, NOPE:NOPE + VD],
                                         start=(k == 0), stop=(k == VF - 1))
                    last.then_inc(*gm_ps.up())
                pe.wait_ge(*krt_ready.at(1))
                pe.wait_ge(*tr_ev.at(TB))
                for n in range(KB):
                    last = pe.transpose(p.psum[0:QD, 4 + n // 3, (n % 3) * P:(n % 3 + 1) * P], krt[:, n, :], p.ident[:])
                last.then_inc(*tr_ps.up())
                pe.wait_ge(*gm_ev.at(TB + NH + KB))
                pe.wait_ge(*tr_ev.at(TB + 1))

                def scores(n):
                    b, h = items[n]
                    lo, hi = keys_of(b)
                    w = (hi - lo) // 2
                    if n >= 2:
                        pe.wait_ge(*e_ready.at(n - 1))
                    for part in range(2):
                        last = pe.matmul(p.psum[:, 2 * (n % 2) + part, 0:w], qT[0:QD, h, b * P:(b + 1) * P],
                                         kT[0:QD, h, lo + part * w:lo + (part + 1) * w], start=True, stop=True)
                    last.then_inc(*sc_ps.up())

                def turn_probs(n):
                    b, h = items[n]
                    lo, hi = keys_of(b)
                    pe.wait_ge(*e_ready.at(n + 1))
                    if n >= 1:
                        pe.wait_ge(*pt_ev.at(n))
                    for k in range((hi - lo) // P):
                        last = pe.transpose(p.psum[:, 4 + k // 4, (k % 4) * P:(k % 4 + 1) * P],
                                            prob[:, n % 2, k * P:(k + 1) * P], p.ident[:])
                    last.then_inc(*pt_ps.up())

                def outputs(n):
                    b, h = items[n]
                    lo, hi = keys_of(b)
                    pe.wait_ge(*pt_ev.at(n + 1))
                    if h == 0 and b >= 1:
                        pe.wait_ge(*o_ev.at(b))
                    nk = (hi - lo) // P
                    for k in range(nk):
                        last = pe.matmul(p.psum[:, 6, h * VD:(h + 1) * VD], probT[:, n % 2, k * P:(k + 1) * P],
                                         vt[:, lo // P + k, h * VD:(h + 1) * VD], start=(k == 0), stop=(k == nk - 1))
                    last.then_inc(*o_ps.up())
                scores(0)
                scores(1)
                for n in range(len(items)):
                    turn_probs(n)
                    if n + 2 < len(items):
                        scores(n + 2)
                    if n >= 1:
                        outputs(n - 1)
                    if n in step_at:
                        mod.on_tensor(pe, step_at[n])
                outputs(len(items) - 1)

            @block.vector
            def _(dve):
                link = chained(dve_c)

                def rotate(u, b, n):
                    def quarters(ap):
                        return ap.rearrange("p n (a s r) -> p (n a) s r", a=2, s=2) if n == 1 else \
                            ap.rearrange("p n (a s r) -> p n a s r", a=2, s=2)
                    c, s = insert_dim(cos[:, b], 1, n), insert_dim(sin[:, b], 1, n)
                    link(dve, dve.tensor_tensor(ra[:, 0:n], u, c, ALU.mult))
                    for side in range(2):
                        for a in range(2):
                            dst = slice(16 * a + 8 * side, 16 * a + 8 * side + 8)
                            src = slice(16 * a + 8 * (1 - side), 16 * a + 8 * (1 - side) + 8)
                            last = dve.tensor_tensor(rb[:, 0:n, dst], u[:, :, src], s[:, :, dst], ALU.mult)
                    link(dve, last)
                    return dve.tensor_tensor(u, ra[:, 0:n], rb[:, 0:n], ALU.add)
                dve.tensor_scalar(stat[:, 0], stat[:, 0], 1.0 / QR, EPS, ALU.mult, ALU.add)
                dve.tensor_scalar(stat[:, 1], stat[:, 1], 1.0 / KVR, EPS, ALU.mult, ALU.add).then_inc(*mean.up())
                dve.wait_ge(*root.at(1))
                dve.reciprocal(rstd[:], rstd[:]).then_inc(*rs.up())
                dve.wait_ge(*rs.at(1))
                dve.wait_ge(*gains_in.at(64))
                for b in range(TB):
                    dve.scalar_tensor_tensor(out=ck[:, b], in0=ck[:, b], scalar=rstd[:, 1, b:b + 1], in1=kvrow[:],
                                             op0=ALU.mult, op1=ALU.mult)
                    dve.tensor_scalar(cq[:, b], cq[:, b], rstd[:, 0, b:b + 1], None, ALU.mult).then_inc(*kvn.up())
                dve.wait_ge(*zeroed.at(1))
                for b in range(LB):
                    link(dve, dve.tensor_copy(krt[:, 1 + b, NOPE:QD], kr[:, b]))
                    link(dve, rotate(krt[:, 1 + b:2 + b, NOPE:QD], b, 1))
                dve.tensor_copy(krt[:, 1 + LB, NOPE:QD], kr[:, LB]).then_inc(*krt_ready.up())
                for n, (kind, b) in enumerate(turns):
                    dve.wait_ge(*lat_tr.at(n + 1))
                    last = dve.tensor_copy(ckvT[:, :, n * P:(n + 1) * P],
                                           p.psum[:, 2 * (n % 4), 0:KVR].rearrange("p (k c) -> p k c", k=VF))
                    if kind == "tok":
                        for k in range(QF):
                            last = dve.tensor_scalar(cqT[:, k, b * P:(b + 1) * P],
                                                     p.psum[:, 2 * (n % 4) + 1, k * P:(k + 1) * P],
                                                     gq[:, k:k + 1], None, ALU.mult)
                    last.then_inc(*lat_ev.up())

                def take_turned(b):
                    dve.wait_ge(*tr_ps.at(b + 1))
                    dve.tensor_copy(qT[0:QD, :, b * P:(b + 1) * P].rearrange("p (a h) c -> p a h c", a=2),
                                    p.psum[0:QD, 4 + 2 * (b % 2):6 + 2 * (b % 2)].rearrange(
                                        "p a (h c) -> p a h c", h=4)).then_inc(*tr_ev.up())
                for b in range(TB):
                    dve.wait_ge(*gm_ps.at(b + 1))
                    if b >= 2:
                        dve.wait_ge(*tr_ps.at(b - 1))
                    dve.tensor_copy(qtok[:, b % 2, 0:512], p.psum[:, 2 * (b % 2)])
                    dve.tensor_copy(qtok[:, b % 2, 512:NH * QD],
                                    p.psum[:, 2 * (b % 2) + 1, 0:NH * QD - 512]).then_inc(*gm_ev.up())
                    dve.wait_ge(*gm_ev.at(b + 1))
                    if b < LB:
                        rotate(qtok[:, b % 2].rearrange("p (h c) -> p h c", h=NH)[:, :, NOPE:QD], b,
                               NH).then_inc(*qt_ready.up())
                    else:
                        dve.engine_nop().then_inc(*qt_ready.up())
                    if b >= 1:
                        take_turned(b - 1)
                take_turned(TB - 1)
                for h in range(NH):
                    dve.wait_ge(*gm_ps.at(TB + h + 1))
                    dve.tensor_copy(kT[0:NOPE, h].rearrange("p (a k) -> p a k", a=2),
                                    p.psum[0:NOPE, 2 * (h % 2):2 * (h % 2) + 2, 0:KEYS // 2]).then_inc(*gm_ev.up())
                for n in range(KB):
                    dve.wait_ge(*gm_ps.at(TB + NH + n + 1))
                    dve.tensor_copy(vt[:, n], p.psum[:, 2 * (n % 2)]).then_inc(*gm_ev.up())
                dve.wait_ge(*tr_ps.at(TB + 1))
                for part in range(2):
                    last = dve.tensor_copy(kT[NOPE:QD, :, part * 3 * P:(part + 1) * 3 * P],
                                           insert_dim(p.psum[NOPE:QD, 4 + part, 0:3 * P], 1, NH))
                last.then_inc(*tr_ev.up())

                def largest(n):
                    b, h = items[n]
                    lo, hi = keys_of(b)
                    w = (hi - lo) // 2
                    dve.wait_ge(*sc_ps.at(n + 1))
                    m = mx[:, n % (2 * NH)]
                    link(dve, dve.tensor_reduce(m[:, 0:1], p.psum[:, 2 * (n % 2):2 * (n % 2) + 2, 0:w],
                                                mybir.AxisListType.XY, ALU.max))
                    dve.tensor_scalar(m[:, 1:2], m[:, 0:1], -SCALE, None, ALU.mult).then_inc(*mx_ready.up())

                def take_block(b):
                    dve.wait_ge(*o_ps.at(NH * (b + 1)))
                    link(dve, dve.reciprocal(total[:, b % 2], total[:, b % 2]))
                    dve.tensor_tensor(o[:, b].rearrange("p (h c) -> p h c", h=NH),
                                      p.psum[:, 6].rearrange("p (h c) -> p h c", h=NH),
                                      total[:, b % 2].to_broadcast([P, NH, VD]), ALU.mult).then_inc(*o_ev.up())
                largest(0)
                largest(1)
                for n, (b, h) in enumerate(items):
                    if n - 1 in step_at:
                        mod.on_vector(dve, step_at[n - 1])
                    lo, hi = keys_of(b)
                    dve.wait_ge(*pt_ps.at(n + 1))
                    if n >= 2:
                        dve.wait_ge(*o_ps.at(n - 1))
                    nk = (hi - lo) // P
                    first = min(nk, 4) * P
                    last = dve.tensor_copy(probT[:, n % 2, 0:first], p.psum[:, 4, 0:first])
                    if nk > 4:
                        last = dve.tensor_copy(probT[:, n % 2, first:nk * P], p.psum[:, 5, 0:nk * P - first])
                    last.then_inc(*pt_ev.up())
                    if n + 2 < len(items):
                        largest(n + 2)
                    if h == 0 and b >= 1:
                        take_block(b - 1)
                take_block(TB - 1)
                mod.vectors(dve, link, l, 0, ("gate",))
                mod.vectors(dve, link, l, 1, ("scale", "gate"))
                if l == 0:
                    mod.vectors(dve, link, 1, 0, ("scale",))
    p.close_stage()


def gate_rows(p, pe, l, which, gr_ps, gr_ev, first_bank=0):
    for s in range(2):
        for k in range(KD):
            last = pe.matmul(p.psum[:, first_bank + 2 * s + k // 4, (k % 4) * P:(k % 4 + 1) * P],
                             p.gate_out[:, l, which, k, s:s + 1].to_broadcast([P, P]), p.ident[:], start=True, stop=True)
    last.then_inc(*gr_ps.up())


def stage_out_proj(p, l, t):
    nc, io = p.nc, p.io
    landed, small = [p.sig(f"weights_landed{i}") for i in range(2)], p.sig("wo_small")
    hi_done, lo_done, y_out = p.sig("weights_hi"), p.sig("weights_lo"), p.sig("yt_out")
    sq, mean, root, rs, yn, tr, ev = (p.sig(n) for n in (
        "pn_squares", "pn_mean", "pn_root", "pn_rstd", "pn_scaled", "pn_turned", "pn_evicted"))
    gr_ps, gr_ev, mm, sq2, m2, r2, res = (p.sig(n) for n in (
        "gate_ps", "gate_out", "out_ps", "out_squares", "out_mean", "out_root", "residual"))
    dve_c = p.sig("dve_chain")
    with ExitStack() as own:
        def sb(name, shape):
            return p.sb(f"op_{name}{l}", shape, ctx=own)
        quarter = D // 4
        raw = t["qkv_room"][:, 0:2 * KD * quarter].rearrange("p (r k c) -> p r k c", r=2, k=KD)
        w_hi, w_lo = (p.sb(f"op_w_{n}{l}", [P, 4, KD, quarter], F32R, ctx=own) for n in ("hi", "lo"))
        gain = sb("gain", [P, KD])
        junk = sb("junk", [P, 512])
        stat, rstd = sb("stat", [P, TB, 2]), sb("rstd", [P, TB, 2])
        stat2, rstd2 = sb("stat2", [P, TB, 2]), sb("rstd2", [P, TB])
        yf = sb("yf", [P, 2, KD, P])
        y_hi, y_lo = (p.sb(f"op_y_{n}{l}", [P, 2, KD, P], F32R, ctx=own) for n in ("hi", "lo"))
        rows = sb("rows", [P, 2, D])
        upd = t["qkv_room"][:, 2 * KD * quarter:2 * KD * quarter + 2 * D].rearrange("p (r c) -> p r c", r=2)
        parts = (t["y_ssd"], t["o"])
        with nc.Block() as block:
            @block.sync
            def _(sp):
                with nc.allow_non_contiguous_dma(reason="one gain per partition"):
                    sp.dma_start(gain[:, 0:4], io["ssd_norm"][l].rearrange("(k p) -> p k", p=P)).then_inc(*small.up(16))
                    sp.dma_start(gain[:, 4:8], io["mla_norm"][l].rearrange("(k p) -> p k", p=P)).then_inc(*small.up(16))
                for i in range(4):
                    if i >= 2:
                        sp.wait_ge(*lo_done.at(i - 1))
                    sp.dma_start(raw[:, i % 2], io["w_out"][l, :, i * quarter:(i + 1) * quarter].rearrange(
                        "(k p) f -> p k f", p=P)).then_inc(*landed[i % 2].up(16))

            @block.gpsimd
            def _(pool):
                pool.wait_ge(*landed[0].at(16))
                pool.tensor_copy(w_hi[:, 0], raw[:, 0]).then_inc(*hi_done.up())
                for i in range(4):
                    pool.wait_ge(*hi_done.at(i + 1))
                    pool.tensor_tensor(w_lo[:, i], raw[:, i % 2], w_hi[:, i].bitcast(F32),
                                       ALU.subtract).then_inc(*lo_done.up())

            @block.scalar
            def _(act):
                n = 0
                for b in range(TB):
                    for j, part in enumerate(parts):
                        act.activation(junk[:, 0:512], part[:, b], ACT.Square, accum_out=stat[:, b, j:j + 1]).then_inc(*sq.up())
                        n += 1
                        act.wait_ge(*sq.at(n))
                act.wait_ge(*mean.at(1))
                act.activation(rstd[:], stat[:], ACT.Sqrt).then_inc(*root.up())
                for b in range(TB):
                    act.wait_ge(*rs.at(1))
                    for j, part in enumerate(parts):
                        last = act.activation(part[:, b], part[:, b], ACT.Copy, scale=rstd[:, b, j:j + 1])
                    last.then_inc(*yn.up())
                    if 1 <= b < 4:
                        act.wait_ge(*landed[b % 2].at(16 * (b // 2 + 1)))
                        act.wait_ge(*hi_done.at(b))
                        act.activation(w_hi[:, b], raw[:, b % 2], ACT.Copy).then_inc(*hi_done.up())
                for b in range(TB):
                    act.wait_ge(*mm.at(b + 1))
                    for half in range(2):
                        act.activation(junk[:, 0:512], p.psum[:, 4 + 2 * (b % 2) + half], ACT.Square,
                                       accum_out=stat2[:, b, half:half + 1]).then_inc(*sq2.up())
                        act.wait_ge(*sq2.at(2 * b + half + 1))
                    act.wait_ge(*m2.at(b + 1))
                    act.activation(rstd2[:, b:b + 1], stat2[:, b, 0:1], ACT.Sqrt).then_inc(*r2.up())

            @block.tensor
            def _(pe):
                gate_rows(p, pe, l, 0, gr_ps, gr_ev)
                pe.wait_ge(*gr_ev.at(1))

                def turn(b):
                    pe.wait_ge(*yn.at(b + 1))
                    if b >= 2:
                        pe.wait_ge(*ev.at(b - 1))
                    for k in range(KD):
                        part = parts[k // 4]
                        last = pe.transpose(p.psum[:, 2 * (b % 2) + k // 4, (k % 4) * P:(k % 4 + 1) * P],
                                            part[:, b, (k % 4) * P:(k % 4 + 1) * P], p.ident[:])
                    last.then_inc(*tr.up())
                turn(0)
                for b in range(TB):
                    if b + 1 < TB:
                        turn(b + 1)
                    pe.wait_ge(*y_out.at(b + 1))
                    if b >= 2:
                        pe.wait_ge(*res.at(b - 1))
                    for i in range(4):
                        pe.wait_ge(*lo_done.at(i + 1))
                        out = p.psum[:, 4 + 2 * (b % 2) + i // 2, (i % 2) * quarter:(i % 2 + 1) * quarter]
                        for k in range(KD):
                            for n, (y, w) in enumerate(((y_hi, w_hi), (y_hi, w_lo), (y_lo, w_hi))):
                                last = pe.matmul(out, y[:, b % 2, k, :], w[:, i, k, :],
                                                 start=(k == 0 and n == 0), stop=(k == KD - 1 and n == 2))
                    last.then_inc(*mm.up())

            @block.vector
            def _(dve):
                link = chained(dve_c)
                dve.wait_ge(*gr_ps.at(1))
                dve.tensor_copy(rows[:].rearrange("p s (a c) -> p (s a) c", a=2), p.psum[:, 0:4]).then_inc(*gr_ev.up())
                dve.wait_ge(*sq.at(2 * TB))
                dve.tensor_scalar(stat[:], stat[:], 1.0 / 512, EPS, ALU.mult, ALU.add).then_inc(*mean.up())
                dve.wait_ge(*root.at(1))
                dve.reciprocal(rstd[:], rstd[:]).then_inc(*rs.up())
                dve.wait_ge(*small.at(32))

                def take_turned(b):
                    dve.wait_ge(*tr.at(b + 1))
                    for k in range(KD):
                        last = dve.tensor_scalar(yf[:, b % 2, k],
                                                 p.psum[:, 2 * (b % 2) + k // 4, (k % 4) * P:(k % 4 + 1) * P],
                                                 gain[:, k:k + 1], None, ALU.mult)
                    last.then_inc(*ev.up())
                    dve.wait_ge(*ev.at(b + 1))
                    if b >= 2:
                        dve.wait_ge(*mm.at(b - 1))
                    link(dve, dve.tensor_copy(y_hi[:, b % 2], yf[:, b % 2]))
                    dve.tensor_tensor(y_lo[:, b % 2], yf[:, b % 2], y_hi[:, b % 2].bitcast(F32),
                                      ALU.subtract).then_inc(*y_out.up())
                take_turned(0)
                for b in range(TB):
                    if b + 1 < TB:
                        take_turned(b + 1)
                    take_residual(p, dve, link, b, p.psum[:, 4 + 2 * (b % 2):6 + 2 * (b % 2)], rows, upd,
                                  stat2, rstd2, sq2, m2, r2, res)
    p.close_stage()


def take_residual(p, dve, link, b, src, rows, upd, stat2, rstd2, sq2, m2, r2, res):
    s = SEQ_OF[b]
    dve.wait_ge(*sq2.at(2 * b + 2))
    link(dve, dve.tensor_tensor(stat2[:, b, 0:1], stat2[:, b, 0:1], stat2[:, b, 1:2], ALU.add))
    dve.tensor_scalar(stat2[:, b, 0:1], stat2[:, b, 0:1], 1.0 / D, EPS, ALU.mult, ALU.add).then_inc(*m2.up())
    dve.wait_ge(*r2.at(b + 1))
    link(dve, dve.reciprocal(rstd2[:, b:b + 1], rstd2[:, b:b + 1]))
    link(dve, dve.scalar_tensor_tensor(
        out=upd[:, b % 2].rearrange("p (a c) -> p a c", a=2), in0=src, scalar=rstd2[:, b:b + 1],
        in1=rows[:, s].rearrange("p (a c) -> p a c", a=2), op0=ALU.mult, op1=ALU.mult))
    dve.tensor_tensor(p.x[:, b], p.x[:, b], upd[:, b % 2], ALU.add).then_inc(*res.up())


I32 = mybir.dt.int32
SL = 256
SLB = SL // P
MAX_BLOCKS = (2 * T - NE) // SL + NE


def stage_router(p, l, hT, ht, r):
    nc, io = p.nc, p.io
    r_in, lg_ps, best, e2_done, made, turned, rows_out, stored, iota_done, pos_ps, ht_ps, ht_hi, ht_out = (
        p.sig(n) for n in ("router_in", "router_ps", "router_best", "router_exp", "router_made", "router_turned",
                           "router_rows", "router_stored", "router_iota", "router_pos", "router_ht_ps",
                           "router_ht_hi", "router_ht_out"))
    mask_ready, cols_out, strict_ready = p.sig("router_mask"), p.sig("router_cols"), p.sig("router_strict")
    dve_c = p.sig("dve_chain")
    hi, lo = ht
    with ExitStack() as own:
        def sb(name, shape, dt=F32):
            return p.sb(f"rt_{name}{l}", shape, dt, ctx=own)
        wr = sb("wr", [P, KD, NE])
        lg, top = sb("lg", [P, TB, NE]), sb("top", [P, TB, 8])
        idx, idf = sb("idx", [P, TB, 8], U32), sb("idf", [P, TB, 8])
        iota, iota_b = sb("iota", [P, NE]), sb("iota_b", [P, MAX_BLOCKS])
        strict = sb("strict", [P, P])
        diff, e2, w1, w2 = (sb(n, [P, TB]) for n in ("diff", "e2", "w1", "w2"))
        hit = sb("hit", [P, 2, TB, NE])
        mask = sb("mask", [P, TB, NE])
        cols = sb("cols", [P, NE, 2, TB])
        number = sb("number", [P, TB, NE])
        rows = sb("rows", [NE, T])
        cnt, nb, end, part = (sb(n, [P, NE]) for n in ("cnt", "nb", "end", "part"))
        before, before_nb = sb("before", [P, MAX_BLOCKS, NE]), sb("before_nb", [P, MAX_BLOCKS, NE])
        eb, sb_ = sb("eb", [P, MAX_BLOCKS]), sb("sb", [P, MAX_BLOCKS])
        with nc.Block() as block:
            @block.sync
            def _(sp):
                sp.dma_start(wr[:], io["moe_router"][0].rearrange("(k p) e -> p k e", p=P)).then_inc(*r_in.up(16))
                sp.wait_ge(*rows_out.at(1))
                sp.dma_start(r["row_dram"], rows[:]).then_inc(*stored.up(16))
                sp.wait_ge(*cols_out.at(1))
                sp.dma_start(r["col_dram"].rearrange("e p c -> p e c"),
                             cols[:].rearrange("p e c b -> p e (c b)")).then_inc(*stored.up(16))
                sp.wait_ge(*stored.at(32))

            @block.gpsimd
            def _(pool):
                for tile, n in ((iota, NE), (iota_b, MAX_BLOCKS), (r["iota_slot"], SL)):
                    pool.iota(tile[:], pattern=[[1, n]], base=0, channel_multiplier=0,
                              allow_small_or_imprecise_dtypes=True).then_inc(*iota_done.up())
                pool.iota(r["slot_of"][:], pattern=[[P, SLB]], base=0, channel_multiplier=1,
                          allow_small_or_imprecise_dtypes=True).then_inc(*iota_done.up())
                pool.tensor_tensor(strict[:], p.tri[:, 0], p.ident[:], ALU.subtract).then_inc(*strict_ready.up())

            @block.tensor
            def _(pe):
                pe.wait_ge(*r_in.at(16))
                for b in range(TB):
                    for k in range(KD):
                        last = pe.matmul(p.psum[:, 0, b * NE:(b + 1) * NE], hT[:, k, b * P:(b + 1) * P], wr[:, k, :],
                                         start=(k == 0), stop=(k == KD - 1))
                last.then_inc(*lg_ps.up())
                for b in range(TB):
                    if b >= 2:
                        pe.wait_ge(*ht_out.at(b - 1))
                    for k in range(KD):
                        last = pe.transpose(p.psum[:, 4 + 2 * (b % 2) + k // 4, (k % 4) * P:(k % 4 + 1) * P],
                                            hT[:, k, b * P:(b + 1) * P], p.ident[:])
                    last.then_inc(*ht_ps.up())
                pe.wait_ge(*mask_ready.at(1))
                pe.wait_ge(*strict_ready.at(1))
                for b in range(TB + 1):
                    for j in range(min(b + 1, TB)):
                        last = pe.matmul(p.psum[:, 1, b * NE:(b + 1) * NE], strict[:] if j == b else p.ones[:],
                                         mask[:, j, :], start=(j == 0), stop=(j == min(b, TB - 1)))
                last.then_inc(*pos_ps.up())
                pe.wait_ge(*made.at(1))
                for b in range(TB):
                    last = pe.transpose(p.psum[0:NE, 2 + b // 4, (b % 4) * P:(b % 4 + 1) * P], number[:, b, :], p.ident[:])
                last.then_inc(*turned.up())

            @block.scalar
            def _(act):
                for b in range(TB):
                    act.wait_ge(*ht_ps.at(b + 1))
                    act.activation(hi[:, b].rearrange("p (a c) -> p a c", a=2),
                                   p.psum[:, 4 + 2 * (b % 2):6 + 2 * (b % 2)], ACT.Copy).then_inc(*ht_hi.up())
                act.wait_ge(*best.at(1))
                act.activation(e2[:], diff[:], ACT.Exp).then_inc(*e2_done.up())

            @block.vector
            def _(dve):
                link = chained(dve_c)
                dve.wait_ge(*lg_ps.at(1))
                link(dve, dve.tensor_copy(lg[:], p.psum[:, 0, 0:TB * NE].rearrange("p (b e) -> p b e", b=TB)))
                for b in range(TB):
                    link(dve, dve.max(top[:, b], lg[:, b]))
                    link(dve, dve.max_index(idx[:, b], top[:, b], lg[:, b]))
                link(dve, dve.tensor_copy(idf[:], idx[:]))
                dve.tensor_tensor(diff[:], top[:, :, 1], top[:, :, 0], ALU.subtract).then_inc(*best.up())
                dve.wait_ge(*iota_done.at(4))
                for n in range(2):
                    link(dve, dve.tensor_tensor(hit[:, n], insert_dim(iota[:], 1, TB),
                                                idf[:, :, n].to_broadcast([P, TB, NE]), ALU.is_equal))
                dve.tensor_tensor(mask[:], hit[:, 0], hit[:, 1], ALU.add).then_inc(*mask_ready.up())
                for b in range(TB):
                    dve.wait_ge(*ht_hi.at(b + 1))
                    dve.tensor_tensor(lo[:, b].rearrange("p (a c) -> p a c", a=2),
                                      p.psum[:, 4 + 2 * (b % 2):6 + 2 * (b % 2)],
                                      hi[:, b].bitcast(F32).rearrange("p (a c) -> p a c", a=2),
                                      ALU.subtract).then_inc(*ht_out.up())
                dve.wait_ge(*e2_done.at(1))
                link(dve, dve.tensor_scalar(w1[:], e2[:], 1.0, None, ALU.add))
                link(dve, dve.reciprocal(w1[:], w1[:]))
                link(dve, dve.tensor_tensor(w2[:], e2[:], w1[:], ALU.mult))
                for n, w in enumerate((w1, w2)):
                    link(dve, dve.tensor_tensor(hit[:, n], hit[:, n], w[:].to_broadcast([P, TB, NE]), ALU.mult))
                link(dve, dve.tensor_tensor(cols[:, :, 1].rearrange("p e b -> p b e"), hit[:, 0], hit[:, 1], ALU.add))
                dve.wait_ge(*pos_ps.at(1))
                link(dve, dve.scalar_tensor_tensor(
                    out=number[:], in0=p.psum[:, 1, 0:TB * NE].rearrange("p (b e) -> p b e", b=TB), scalar=1.0,
                    in1=mask[:], op0=ALU.add, op1=ALU.mult))
                dve.tensor_scalar(number[:], number[:], -1.0, None, ALU.add).then_inc(*made.up())
                dve.wait_ge(*made.at(1))
                dve.tensor_copy(cols[:, :, 0].rearrange("p e b -> p b e"), number[:]).then_inc(*cols_out.up())
                link(dve, dve.tensor_copy(cnt[:], p.psum[:, 1, TB * NE:(TB + 1) * NE]))
                link(dve, dve.tensor_scalar(nb[:], cnt[:], 0.5, None, ALU.is_gt))
                for j in range(1, (T + SL - 1) // SL):
                    link(dve, dve.tensor_scalar(part[:], cnt[:], j * SL + 0.5, None, ALU.is_gt))
                    link(dve, dve.tensor_tensor(nb[:], nb[:], part[:], ALU.add))
                link(dve, dve.tensor_tensor_scan(end[:], p.ones[:, 0:NE], nb[:], 0.0, ALU.mult, ALU.add))
                link(dve, dve.tensor_tensor(before[:], insert_dim(end[:], 1, MAX_BLOCKS),
                                            iota_b[:].to_broadcast([P, MAX_BLOCKS, NE]), ALU.is_le))
                link(dve, dve.tensor_tensor(before_nb[:], before[:], insert_dim(nb[:], 1, MAX_BLOCKS), ALU.mult))
                link(dve, dve.tensor_reduce(eb[:], before[:], AX_X, ALU.add))
                link(dve, dve.tensor_reduce(sb_[:], before_nb[:], AX_X, ALU.add))
                link(dve, dve.tensor_scalar(eb[:], eb[:], float(NE - 1), None, ALU.min))
                link(dve, dve.tensor_tensor(sb_[:], iota_b[:], sb_[:], ALU.subtract))
                link(dve, dve.tensor_scalar(r["first"][:], sb_[:], float(SL), None, ALU.mult))
                link(dve, dve.tensor_copy(r["table"][:, 0:MAX_BLOCKS], eb[0:1, :]))
                link(dve, dve.tensor_copy(r["table"][:, MAX_BLOCKS:MAX_BLOCKS + 1], end[0:1, NE - 1:NE]))
                dve.wait_ge(*turned.at(1))
                link(dve, dve.tensor_copy(rows[:, 0:512], p.psum[0:NE, 2]))
                dve.tensor_copy(rows[:, 512:T], p.psum[0:NE, 3, 0:T - 512]).then_inc(*rows_out.up())
    p.close_stage()


G_PIECES = 2 * FT
PIECES = G_PIECES + KD
SLOT = [i % 4 for i in range(G_PIECES)] + [2, 3, 0, 1, 2, 3, 2, 3]
PAIR = [i % 4 for i in range(G_PIECES)] + [2, 3, 0, 1, 2, 3, 2, 3]


def last_user(table, i):
    for j in range(i - 1, i - 1 - PIECES, -1):
        if table[j % PIECES] == table[i]:
            return j


def stage_sparse_experts(p, l, ht, acc, r):
    nc, io = p.nc, p.io
    sem = lambda name: p.ctx.enter_context(nc.semaphore(f"{name}{l}"))
    RAWS = 3
    raw_in = [sem(f"ex_raw_in{j}") for j in range(RAWS)]
    hi_done, lo_done, piece_done, taken = sem("ex_hi_done"), sem("ex_lo_done"), sem("ex_piece_done"), sem("ex_taken")
    gate_act, hid_ready, chain, zeroed = sem("ex_gate_act"), sem("ex_hid"), sem("ex_dve"), sem("ex_zero")
    routes_in, gather_ready, scatter_ready, comb_kept = sem("ex_routes"), sem("ex_gather_m"), sem("ex_scatter_m"), sem("ex_comb")
    gathered, he_hi_done, he_lo_done = sem("ex_gathered"), sem("ex_he_hi"), sem("ex_he_lo")
    y_turned, y_hi_done, y_lo_done = sem("ex_y_turned"), sem("ex_y_hi"), sem("ex_y_lo")
    scattered, added = sem("ex_scattered"), sem("ex_added")
    SLOTS = 3
    slot_of = [i % SLOTS for i in range(PIECES)]
    GB = KD // 2
    credit = {lo_done: PIECES, piece_done: PIECES, taken: PIECES, gather_ready: 1, scatter_ready: 1, comb_kept: 1,
              gathered: GB, y_lo_done: 4, scattered: TB, added: TB}
    n_link = 2 * FT + 1
    with ExitStack() as own:
        def sb(name, shape, dt=F32):
            return p.sb(f"ex_{name}{l}", shape, dt, ctx=own)
        raw = sb("raw", [P, RAWS, FE])
        wh, wl = sb("wh", [P, SLOTS, FE], F32R), sb("wl", [P, SLOTS, FE], F32R)
        he_hi, he_lo = sb("he_hi", [P, KD, SL], F32R), sb("he_lo", [P, KD, SL], F32R)
        hh, hl = sb("hh", [P, FT, SL], F32R), sb("hl", [P, FT, SL], F32R)
        sg, hf = sb("sg", [P, SL]), sb("hf", [P, SL])
        yT = sb("yT", [P, KD, SL])
        y_hi, y_lo = sb("y_hi", [P, SLB, D], F32R), sb("y_lo", [P, SLB, D], F32R)
        matrix = sb("matrix", [P, TB * SL], F32R)
        take_m = matrix[:].rearrange("p (b s) -> p b s", b=TB)
        give_m = matrix[:].rearrange("p (s t) -> p s t", s=SLB)
        row, col = sb("row", [P, T]), sb("col", [P, 2, TB])
        number, comb = sb("number", [P, TB]), sb("comb", [P, TB])
        spare = sb("spare", [P, 16])
        bank_of = [4 + i % 4 for i in range(PIECES)]

        def size(i):
            return D if i < G_PIECES else FE

        def source(e, i):
            if i < G_PIECES:
                name, f = ("gate", "up")[i % 2], i // 2
                return io[f"moe_w_{name}"][0, bass.ds(e, 1), :, f * P:(f + 1) * P].rearrange("o (k p) c -> p (o k) c", p=P)
            m = i - G_PIECES
            return io["moe_w_down"][0, bass.ds(e, 1), :, m * P:(m + 1) * P].rearrange("o (k p) c -> p (o k) c", p=P)

        def n_blocks(eng):
            return eng.value_load(r["table"][0:1, MAX_BLOCKS:MAX_BLOCKS + 1], min_val=1, max_val=MAX_BLOCKS)

        with nc.Block() as block:
            @block.sync
            def _(sp):
                n = n_blocks(sp)
                with sp.Fori(0, MAX_BLOCKS) as b:
                    with sp.If(b < n):
                        e = sp.value_load(r["table"][0:1, bass.ds(b, 1)], min_val=0, max_val=NE - 1)
                        sp.wait_ge(scatter_ready, b + 1)
                        sp.wait_ge(gather_ready, b + 1)
                        sp.wait_ge(comb_kept, b + 1)
                        sp.dma_start(row[:], r["row_dram"][bass.ds(e, 1)].rearrange("o t -> (o t)").partition_broadcast(P)
                                     ).then_inc(routes_in, 16)
                        sp.dma_start(col[:].rearrange("p c b -> p (c b)"),
                                     r["col_dram"][bass.ds(e, 1)].rearrange("o p c -> p (o c)")).then_inc(routes_in, 16)
                        for i in range(PIECES):
                            sp.wait_ge(lo_done, (b + 1) * PIECES + i - RAWS + 1)
                            sp.dma_start(raw[:, i % RAWS, 0:size(i)].rearrange("p (k c) -> p k c", c=P),
                                         source(e, i)).then_inc(raw_in[i % RAWS], 16)

            @block.scalar
            def _(act):
                n = n_blocks(act)
                with act.Fori(0, MAX_BLOCKS) as b:
                    with act.If(b < n):
                        for i in range(PIECES):
                            act.wait_ge(raw_in[i % RAWS], b * (16 * PIECES // RAWS) + 16 * (i // RAWS + 1))
                            act.wait_ge(piece_done, (b + 1) * PIECES + last_user(slot_of, i) + 1)
                            act.activation(wh[:, slot_of[i], 0:size(i)], raw[:, i % RAWS, 0:size(i)], ACT.Copy).then_inc(hi_done, 1)
                            if i == SLOTS - 1:
                                for j in range(GB):
                                    act.wait_ge(gathered, (b + 1) * GB + j + 1)
                                    act.activation(he_hi[:, 2 * j:2 * j + 2].rearrange("p k s -> p (k s)"),
                                                   p.psum[:, j], ACT.Copy).then_inc(he_hi_done, 1)
                            f = (i - 3) // 2
                            if i % 2 == 1 and 0 <= f < FT:
                                act.wait_ge(piece_done, (b + 1) * PIECES + 2 * f + 1)
                                act.wait_ge(taken, (b + 1) * PIECES + 2 * f)
                                act.activation(sg[:], p.psum[:, bank_of[2 * f], 0:SL], ACT.Silu).then_inc(gate_act, 1)
                        for j in range(4):
                            act.wait_ge(y_turned, 2 * b + j // 2 + 1)
                            half, s = j // 2, j % 2
                            act.activation(y_hi[:, s, half * 512:(half + 1) * 512], p.psum[:, 2 * s + half],
                                           ACT.Copy).then_inc(y_hi_done, 1)

            @block.gpsimd
            def _(pool):
                n = n_blocks(pool)
                with pool.Fori(0, MAX_BLOCKS) as b:
                    with pool.If(b < n):
                        for i in range(PIECES):
                            pool.wait_ge(hi_done, b * PIECES + i + 1)
                            pool.tensor_tensor(wl[:, slot_of[i], 0:size(i)], raw[:, i % RAWS, 0:size(i)],
                                               wh[:, slot_of[i], 0:size(i)].bitcast(F32), ALU.subtract).then_inc(lo_done, 1)

            @block.tensor
            def _(pe):
                n = n_blocks(pe)
                pe.wait_ge(zeroed, len(credit))

                def turn_back(m):
                    for s in range(SLB):
                        last = pe.transpose(p.psum[:, 2 * s + m // 4, (m % 4) * P:(m % 4 + 1) * P],
                                            yT[:, m, s * P:(s + 1) * P], p.ident[:])
                    return last
                with pe.Fori(0, MAX_BLOCKS) as b:
                    with pe.If(b < n):
                        pe.wait_ge(gather_ready, b + 2)
                        pe.wait_ge(y_lo_done, (b + 1) * 4)
                        for k in range(KD):
                            for j in range(TB):
                                for m, part in enumerate(ht):
                                    last = pe.matmul(p.psum[:, k // 2, (k % 2) * SL:(k % 2 + 1) * SL],
                                                     part[:, j, k * P:(k + 1) * P], take_m[:, j],
                                                     start=(j == 0 and m == 0), stop=(j == TB - 1 and m == 1))
                            if k % 2:
                                last.then_inc(gathered, 1)
                        for i in range(PIECES):
                            pe.wait_ge(lo_done, (b + 1) * PIECES + i + 1)
                            if i < 4:
                                pe.wait_ge(added, (b + 1) * TB)
                            pe.wait_ge(taken, (b + 1) * PIECES + last_user(bank_of, i) + 1)
                            if i == 0:
                                pe.wait_ge(he_lo_done, (b + 1) * GB)
                            if i == G_PIECES:
                                pe.wait_ge(hid_ready, (b + 1) * FT)
                            steps = KD if i < G_PIECES else FT
                            mh, ml = (he_hi, he_lo) if i < G_PIECES else (hh, hl)
                            for k in range(steps):
                                cols = slice(k * P, (k + 1) * P)
                                for j, (w, m) in enumerate(((wh, mh), (wh, ml), (wl, mh))):
                                    last = pe.matmul(p.psum[:, bank_of[i], 0:SL], w[:, slot_of[i], cols], m[:, k],
                                                     start=(k == 0 and j == 0), stop=(k == steps - 1 and j == 2))
                            last.then_inc(piece_done, 1)
                            m = i - G_PIECES
                            if m >= 1:
                                pe.wait_ge(taken, (b + 1) * PIECES + G_PIECES + m)
                                last = turn_back(m - 1)
                                if m - 1 == 3:
                                    last.then_inc(y_turned, 1)
                        pe.wait_ge(taken, (b + 1) * PIECES + PIECES)
                        turn_back(KD - 1).then_inc(y_turned, 1)
                        pe.wait_ge(scatter_ready, b + 2)
                        pe.wait_ge(y_lo_done, (b + 1) * 4 + 4)
                        for j in range(TB):
                            pe.wait_ge(added, (b + 1) * TB + j - 1)
                            for half in range(2):
                                for s in range(SLB):
                                    for m, part in enumerate((y_hi, y_lo)):
                                        last = pe.matmul(p.psum[:, 4 + 2 * (j % 2) + half], give_m[:, s, j * P:(j + 1) * P],
                                                         part[:, s, half * 512:(half + 1) * 512],
                                                         start=(s == 0 and m == 0), stop=(s == SLB - 1 and m == 1))
                            last.then_inc(scattered, 1)

            @block.vector
            def _(dve):
                for j, (signal, count) in enumerate(credit.items()):
                    dve.memset(spare[:, j:j + 1], 0.0).then_inc(signal, count)
                dve.engine_nop().then_inc(zeroed, len(credit))
                n = n_blocks(dve)
                with dve.Fori(0, MAX_BLOCKS) as b:
                    with dve.If(b < n):
                        links = 0

                        def link(ins):
                            nonlocal links
                            ins.then_inc(chain, 1)
                            links += 1
                            dve.wait_ge(chain, b * n_link + links)
                        dve.wait_ge(routes_in, 32 * b + 32)
                        dve.wait_ge(scattered, (b + 1) * TB)
                        link(dve.tensor_scalar(number[:], col[:, 0], r["first"][:, bass.ds(b, 1)], None, ALU.subtract))
                        for j in range(TB):
                            last = dve.tensor_scalar(take_m[:, j], r["iota_slot"][:], number[:, j:j + 1], None, ALU.is_equal)
                        last.then_inc(gather_ready, 1)
                        dve.tensor_copy(comb[:], col[:, 1]).then_inc(comb_kept, 1)
                        for j in range(GB):
                            dve.wait_ge(he_hi_done, b * GB + j + 1)
                            part = slice(2 * j, 2 * j + 2)
                            dve.tensor_tensor(he_lo[:, part].rearrange("p k s -> p (k s)"), p.psum[:, j],
                                              he_hi[:, part].bitcast(F32).rearrange("p k s -> p (k s)"),
                                              ALU.subtract).then_inc(he_lo_done, 1)
                        for i in range(PIECES):
                            if i < G_PIECES and i % 2 == 0:
                                continue
                            dve.wait_ge(piece_done, (b + 1) * PIECES + i + 1)
                            res = p.psum[:, bank_of[i], 0:SL]
                            if i < G_PIECES:
                                f = i // 2
                                dve.wait_ge(gate_act, b * FT + f + 1)
                                ins = dve.tensor_tensor(hf[:], res, sg[:], ALU.mult)
                                link(ins)
                                link(dve.tensor_copy(hh[:, f], hf[:]))
                                dve.tensor_tensor(hl[:, f], hf[:], hh[:, f].bitcast(F32), ALU.subtract).then_inc(hid_ready, 1)
                                dve.wait_ge(hid_ready, b * FT + f + 1)
                                dve.engine_nop().then_inc(taken, 2)
                            else:
                                dve.tensor_copy(yT[:, i - G_PIECES], res).then_inc(taken, 1)
                            if i == 5:
                                for s in range(SLB):
                                    last = dve.tensor_scalar(give_m[:, s], row[:], r["first"][:, bass.ds(b, 1)],
                                                             r["slot_of"][:, s:s + 1], ALU.subtract, ALU.is_equal)
                                last.then_inc(scatter_ready, 1)
                        for j in range(4):
                            half, s = j // 2, j % 2
                            dve.wait_ge(y_hi_done, 4 * b + j + 1)
                            cols = slice(half * 512, (half + 1) * 512)
                            dve.tensor_tensor(y_lo[:, s, cols], p.psum[:, 2 * s + half], y_hi[:, s, cols].bitcast(F32),
                                              ALU.subtract).then_inc(y_lo_done, 1)
                        dve.wait_ge(comb_kept, b + 2)
                        for j in range(TB):
                            dve.wait_ge(scattered, (b + 1) * TB + j + 1)
                            a = acc[:, j].rearrange("p (a c) -> p a c", a=2)
                            dve.scalar_tensor_tensor(out=a, in0=p.psum[:, 4 + 2 * (j % 2):6 + 2 * (j % 2)],
                                                     scalar=comb[:, j:j + 1], in1=a, op0=ALU.mult,
                                                     op1=ALU.add).then_inc(added, 1)
    p.close_stage()


def stage_dense(p, l, hi, lo, acc):
    nc, io = p.nc, p.io
    halves_ff = 2
    sem = lambda name: p.ctx.enter_context(nc.semaphore(f"{name}{l}"))
    raw_in = [sem(f"ex_raw_in{r}") for r in range(2)]
    hi_done, lo_done, piece_done, taken = sem("ex_hi_done"), sem("ex_lo_done"), sem("ex_piece_done"), sem("ex_taken")
    gate_act, hid_ready, chain, zeroed = sem("ex_gate_act"), sem("ex_hid"), sem("ex_dve"), sem("ex_zero")
    n_link = FT * 2
    with ExitStack() as own:
        def sb(name, shape, dt=F32):
            return p.sb(f"ex_{name}{l}", shape, dt, ctx=own)
        raw = sb("raw", [P, 2, FE])
        wh, wl = sb("wh", [P, 4, FE], F32R), sb("wl", [P, 4, FE], F32R)
        hh, hl = sb("hh", [P, FT, T], F32R), sb("hl", [P, FT, T], F32R)
        sg, hf = sb("sg", [P, T]), sb("hf", [P, T])

        def size(i):
            return D if i < G_PIECES else FE

        def source(e, i):
            if i < G_PIECES:
                name, f = ("gate", "up")[i % 2], i // 2
                return io[f"ffn_w_{name}"][0, :, bass.ds(e * FE + f * P, P)].rearrange("(k p) c -> p k c", p=P)
            m = i - G_PIECES
            return io["ffn_w_down"][0, bass.ds(e * FE, FE), m * P:(m + 1) * P].rearrange("(k p) c -> p k c", p=P)

        with nc.Block() as block:
            @block.sync
            def _(sp):
                with sp.Fori(0, halves_ff) as e:
                    for i in range(PIECES):
                        sp.wait_ge(lo_done, (e + 1) * PIECES + i - 1)
                        sp.dma_start(raw[:, i % 2, 0:size(i)].rearrange("p (k c) -> p k c", c=P),
                                     source(e, i)).then_inc(raw_in[i % 2], 16)

            @block.scalar
            def _(act):
                with act.Fori(0, halves_ff) as e:
                    for i in range(PIECES):
                        act.wait_ge(raw_in[i % 2], e * (8 * PIECES) + 16 * (i // 2 + 1))
                        act.wait_ge(piece_done, (e + 1) * PIECES + last_user(SLOT, i) + 1)
                        act.activation(wh[:, SLOT[i], 0:size(i)], raw[:, i % 2, 0:size(i)], ACT.Copy).then_inc(hi_done, 1)
                        f = (i - 3) // 2
                        if i % 2 == 1 and 0 <= f < FT:
                            act.wait_ge(piece_done, (e + 1) * PIECES + 2 * f + 1)
                            act.wait_ge(taken, (e + 1) * PIECES + 2 * f)
                            act.activation(sg[:].rearrange("p (a c) -> p a c", a=2),
                                           p.psum[:, 2 * PAIR[2 * f]:2 * PAIR[2 * f] + 2, 0:HT],
                                           ACT.Silu).then_inc(gate_act, 1)

            @block.gpsimd
            def _(pool):
                with pool.Fori(0, halves_ff) as e:
                    for i in range(PIECES):
                        pool.wait_ge(hi_done, e * PIECES + i + 1)
                        ins = pool.tensor_tensor(wl[:, SLOT[i], 0:size(i)], raw[:, i % 2, 0:size(i)],
                                                 wh[:, SLOT[i], 0:size(i)].bitcast(F32), ALU.subtract)
                        ins.then_inc(lo_done, 1)

            @block.tensor
            def _(pe):
                pe.wait_ge(zeroed, 1)
                with pe.Fori(0, halves_ff) as e:
                    for i in range(PIECES):
                        pe.wait_ge(lo_done, (e + 1) * PIECES + i + 1)
                        pe.wait_ge(taken, (e + 1) * PIECES + last_user(PAIR, i) + 1)
                        if i == G_PIECES:
                            pe.wait_ge(hid_ready, (e + 1) * FT)
                        steps = KD if i < G_PIECES else FT
                        mh, ml = (hi, lo) if i < G_PIECES else (hh, hl)
                        for k in range(steps):
                            cols = slice(k * P, (k + 1) * P)
                            for n, (w, m) in enumerate(((wh, mh), (wh, ml), (wl, mh))):
                                for half in range(2):
                                    last = pe.matmul(p.psum[:, 2 * PAIR[i] + half, 0:HT], w[:, SLOT[i], cols],
                                                     m[:, k, half * HT:(half + 1) * HT],
                                                     start=(k == 0 and n == 0), stop=(k == steps - 1 and n == 2))
                        last.then_inc(piece_done, 1)

            @block.vector
            def _(dve):
                dve.memset(sg[:, 0:1], 0.0).then_inc(lo_done, PIECES)
                dve.memset(sg[:, 1:2], 0.0).then_inc(piece_done, PIECES)
                dve.memset(sg[:, 2:3], 0.0).then_inc(taken, PIECES)
                dve.engine_nop().then_inc(zeroed, 1)
                with dve.Fori(0, halves_ff) as e:
                    links = 0

                    def link(ins):
                        nonlocal links
                        links += 1
                        ins.then_inc(chain, 1)
                        dve.wait_ge(chain, e * n_link + links)
                    for i in range(PIECES):
                        if i < G_PIECES and i % 2 == 0:
                            continue
                        dve.wait_ge(piece_done, (e + 1) * PIECES + i + 1)
                        halves = p.psum[:, 2 * PAIR[i]:2 * PAIR[i] + 2, 0:HT]
                        if i < G_PIECES:
                            f = i // 2
                            dve.wait_ge(gate_act, e * FT + f + 1)
                            ins = dve.tensor_tensor(hf[:].rearrange("p (a c) -> p a c", a=2), halves,
                                                    sg[:].rearrange("p (a c) -> p a c", a=2), ALU.mult)
                            link(ins)
                            link(dve.tensor_copy(hh[:, f], hf[:]))
                            dve.tensor_tensor(hl[:, f], hf[:], hh[:, f].bitcast(F32), ALU.subtract).then_inc(hid_ready, 1)
                            dve.wait_ge(hid_ready, e * FT + f + 1)
                            dve.engine_nop().then_inc(taken, 2)
                        else:
                            m = acc[:, i - G_PIECES].rearrange("p (a c) -> p a c", a=2)
                            dve.tensor_tensor(m, m, halves, ALU.add).then_inc(taken, 1)
    p.close_stage()


def stage_ffn_out(p, l, acc, token_major):
    nc, io = p.nc, p.io
    gr_ps, gr_ev, mm, sq2, m2, r2, res = (p.sig(n) for n in (
        "gate_ps", "gate_out", "out_ps", "out_squares", "out_mean", "out_root", "residual"))
    dve_c = p.sig("dve_chain")
    with ExitStack() as own:
        def sb(name, shape):
            return p.sb(f"fo_{name}{l}", shape, ctx=own)
        junk, rows, upd = sb("junk", [P, 512]), sb("rows", [P, 2, D]), sb("upd", [P, 2, D])
        stat2, rstd2 = sb("stat2", [P, TB, 2]), sb("rstd2", [P, TB])

        def source(b):
            if token_major:
                return acc[:, b].rearrange("p (a c) -> p a c", a=2)
            return p.psum[:, 4 + 2 * (b % 2):6 + 2 * (b % 2)]
        with nc.Block() as block:
            @block.scalar
            def _(act):
                for b in range(TB):
                    if not token_major:
                        act.wait_ge(*mm.at(b + 1))
                    for half in range(2):
                        act.activation(junk[:], source(b)[:, half], ACT.Square,
                                       accum_out=stat2[:, b, half:half + 1]).then_inc(*sq2.up())
                        act.wait_ge(*sq2.at(2 * b + half + 1))
                    act.wait_ge(*m2.at(b + 1))
                    act.activation(rstd2[:, b:b + 1], stat2[:, b, 0:1], ACT.Sqrt).then_inc(*r2.up())

            @block.tensor
            def _(pe):
                gate_rows(p, pe, l, 1, gr_ps, gr_ev)
                for b in range(0 if token_major else TB):
                    if b >= 2:
                        pe.wait_ge(*res.at(b - 1))
                    for k in range(KD):
                        last = pe.transpose(p.psum[:, 4 + 2 * (b % 2) + k // 4, (k % 4) * P:(k % 4 + 1) * P],
                                            acc[:, k, b * P:(b + 1) * P], p.ident[:])
                    last.then_inc(*mm.up())

            @block.vector
            def _(dve):
                link = chained(dve_c)
                dve.wait_ge(*gr_ps.at(1))
                link(dve, dve.tensor_copy(rows[:].rearrange("p s (a c) -> p (s a) c", a=2), p.psum[:, 0:4]))
                for b in range(TB):
                    take_residual(p, dve, link, b, source(b), rows, upd,
                                  stat2, rstd2, sq2, m2, r2, res)
    p.close_stage()


def stage_store(p):
    nc, io = p.nc, p.io
    out = p.sig("y_stored")
    with nc.Block() as block:
        @block.sync
        def _(sp):
            sp.dma_start(io["y_sample"].rearrange("o (b p) d -> p (o b) d", p=P), p.x[:, 0:LB]).then_inc(*out.up(16))
            sp.dma_start(io["y_prompt"].rearrange("o p d -> p (o d)"), p.x[:, LB]).then_inc(*out.up(16))
            sp.wait_ge(*out.at(32))
    p.close_stage()




def build(nc, io):
    with ExitStack() as ctx:
        p = Program(nc, io, ctx)
        row_dram = nc.dram_tensor("token_numbers", (NE, T), F32, kind="Internal").ap()
        col_dram = nc.dram_tensor("token_columns", (NE, P, 2 * TB), F32, kind="Internal").ap()
        stage_setup(p)
        stage_first_modulation(p)
        for l in range(2):
            with ExitStack() as mixer:
                def sb(name, shape, where=mixer):
                    return p.sb(f"mx_{name}{l}", shape, ctx=where)
                t = {"z": sb("z", [P, TB, SSDW]), "dtcq": sb("dtcq", [P, TB, 2 * NH + QR]),
                     "ckr": sb("ckr", [P, TB, KVR + ROPE]), 
                     "xst": sb("xst", [P, TB, SSDW]), "stat": sb("stat", [P, 2, TB]), "qkv_room": sb("qkv_room", [P, NH * KEYS])}
                t["y_ssd"] = t["z"]
                t["o"] = t["xst"]
                p.silu_parts = p.sb(f"silu_parts{l}", [P, KD, P], F32R, ctx=mixer)
                scan = mixer.enter_context(ExitStack())
                t["xbc"] = sb("xbc", [P, XF, T], scan)
                with ExitStack() as inner:
                    hi = p.sb(f"hm_hi{l}", [P, KD, T], F32R, ctx=inner)
                    lo = p.sb(f"hm_lo{l}", [P, KD, T], F32R, ctx=inner)
                    weights = InWeights(p, l, t["qkv_room"], inner)
                    stage_pre_norm(p, l, 0, None, (hi, lo), weights)
                    stage_in_proj(p, l, weights, hi, lo, t)
                stage_ssd(p, l, t)
                scan.close()
                stage_attention(p, l, t)
                stage_out_proj(p, l, t)
            with ExitStack() as ffn:
                if l % 2 == 0:
                    acc = p.sb(f"acc{l}", [P, KD, T], ctx=ffn)
                    with ExitStack() as inner:
                        hi = p.sb(f"h_hi{l}", [P, KD, T], F32R, ctx=inner)
                        lo = p.sb(f"h_lo{l}", [P, KD, T], F32R, ctx=inner)
                        stage_pre_norm(p, l, 1, None, (hi, lo), clear=acc[:])
                        stage_dense(p, l, hi, lo, acc)
                else:
                    acc = p.sb(f"acc{l}", [P, TB, D], ctx=ffn)
                    with ExitStack() as inner:
                        ht = [p.sb(f"ht_{n}{l}", [P, TB, D], F32R, ctx=inner) for n in ("hi", "lo")]
                        r = {"iota_slot": p.sb("iota_slot", [P, SL], ctx=inner),
                             "slot_of": p.sb("slot_of", [P, SLB], ctx=inner),
                             "first": p.sb("first", [P, MAX_BLOCKS], ctx=inner),
                             "table": p.sb("table", [1, MAX_BLOCKS + 4], I32, ctx=inner),
                             "row_dram": row_dram, "col_dram": col_dram}
                        with ExitStack() as norm:
                            hT = p.sb(f"hTf{l}", [P, KD, T], ctx=norm)
                            stage_pre_norm(p, l, 1, hT, clear=acc[:])
                            stage_router(p, l, hT, ht, r)
                        stage_sparse_experts(p, l, ht, acc, r)
                stage_ffn_out(p, l, acc, token_major=(l % 2 == 1))
        stage_store(p)


def rope_tables():
    import numpy as np
    rows = LAT // 64
    row = np.repeat(np.arange(rows, dtype=np.float32), 64)
    col = np.tile(np.arange(64, dtype=np.float32), rows)
    half = ROPE // 2
    inv = (np.float32(10000.0) ** (-np.arange(0, half, 2, dtype=np.float32) / half)).astype(np.float32)
    ar, ac = row[:, None] * inv[None, :], col[:, None] * inv[None, :]
    ang = np.concatenate([ar, ar, ac, ac], axis=-1).astype(np.float32)
    sign = np.repeat(np.array([-1, 1, -1, 1], np.float32), half // 2)
    return np.cos(ang).astype(np.float32), (np.sin(ang) * sign).astype(np.float32)


_OUTS = {"y_prompt": (1, CTX, D), "y_sample": (1, LAT, D), "new_ckv": (1, 2, CTX, KVR),
         "new_krope": (1, 2, CTX, ROPE), "new_ssm": (1, 2, 2, NH, HD, NS)}


def kernel(**inputs):
    import numpy as np
    import concourse.bacc as _bacc
    from concourse.bass_utils import run_bass_kernel_spmd as _run

    nc = _bacc.Bacc("TRN2", target_bir_lowering=False, num_devices=1)
    arrays = {k: np.ascontiguousarray(v) for k, v in inputs.items()}
    arrays["rope_cos"], arrays["rope_sin"] = rope_tables()
    io = {}
    for name, a in arrays.items():
        io[name] = nc.dram_tensor(name, a.shape, mybir.dt.from_np(a.dtype), kind="ExternalInput").ap()
    for name, shape in _OUTS.items():
        io[name] = nc.dram_tensor(f"out_{name}", shape, F32, kind="ExternalOutput").ap()
    build(nc, io)
    r = _run(nc, [arrays], core_ids=[0])
    return tuple(r.results[0][f"out_{name}"] for name in _OUTS)
```
